# Optimizing a Trainium2 kernel written in Bass

```python
import math
import jax, jax.numpy as jnp
from jax import lax
import numpy as np

D_MODEL = 1024
BATCH = 1
SEQ = 1024
DEPTH = 1
DEC_BATCH = 8
DEC_SEQ = 1
PAST_LEN = 8192
PAGE_SIZE = 128

CONV_WIDTH = 3
CONV_A_WIDTH = D_MODEL // 2
SSM_WIDTH = D_MODEL // 2
SSM_GROUP = 16
SSM_GROUPS = SSM_WIDTH // SSM_GROUP
SSM_STATE = 64
D_FF = 2816
PLE_DIM = 256
NORM_EPS = 1e-6
DT_MIN = 1e-3
DT_MAX = 1e-1
IN_PROJ_WIDTH = 3 * CONV_A_WIDTH + SSM_WIDTH + 2 * D_MODEL
SPLITS = (CONV_A_WIDTH, 2 * CONV_A_WIDTH, 3 * CONV_A_WIDTH,
          3 * CONV_A_WIDTH + SSM_WIDTH, 3 * CONV_A_WIDTH + SSM_WIDTH + D_MODEL)

kernel_name = "hybrid_shortconv_s5_convffn_step"

def rms_norm(x, g):
    xf = x.astype(jnp.float32)
    y = xf * lax.rsqrt(jnp.mean(xf * xf, axis=-1, keepdims=True) + NORM_EPS)
    return (y * g.astype(jnp.float32)).astype(x.dtype)

def causal_dwconv(u, buf, w, b):
    t = u.shape[1]
    ext = jnp.concatenate([buf.astype(u.dtype), u], axis=1)
    y = b + sum(ext[:, k:k + t] * w[k] for k in range(CONV_WIDTH))
    return y, ext[:, -(CONV_WIDTH - 1):]

def _complex_linear_combine(left, right):
    a1r, a1i, b1r, b1i = left
    a2r, a2i, b2r, b2i = right
    return (a2r * a1r - a2i * a1i,
            a2r * a1i + a2i * a1r,
            a2r * b1r - a2i * b1i + b2r,
            a2r * b1i + a2i * b1r + b2i)

def s5_mimo(u, s0_re, s0_im, log_dt, lam_re, lam_im, b_re, b_im, c_re, c_im, d_skip):
    bt, t, _ = u.shape
    ug = u.reshape(bt, t, SSM_GROUPS, SSM_GROUP)
    dt = jnp.exp(log_dt)[:, None]
    mag = jnp.exp(lam_re * dt)
    ang = lam_im * dt
    abar_re = mag * jnp.cos(ang)
    abar_im = mag * jnp.sin(ang)
    den = lam_re * lam_re + lam_im * lam_im
    nr = abar_re - 1
    coef_re = (nr * lam_re + abar_im * lam_im) / den
    coef_im = (abar_im * lam_re - nr * lam_im) / den
    bbar_re = coef_re[..., None] * b_re - coef_im[..., None] * b_im
    bbar_im = coef_re[..., None] * b_im + coef_im[..., None] * b_re
    bu_re = jnp.einsum('btgh,gph->btgp', ug, bbar_re)
    bu_im = jnp.einsum('btgh,gph->btgp', ug, bbar_im)
    a_re = jnp.broadcast_to(abar_re, (1, t) + abar_re.shape)
    a_im = jnp.broadcast_to(abar_im, (1, t) + abar_im.shape)
    cum_re, cum_im, h_re, h_im = lax.associative_scan(
        _complex_linear_combine, (a_re, a_im, bu_re, bu_im), axis=1)
    s0r = s0_re[:, None].astype(u.dtype)
    s0i = s0_im[:, None].astype(u.dtype)
    s_re = h_re + cum_re * s0r - cum_im * s0i
    s_im = h_im + cum_re * s0i + cum_im * s0r
    y = (jnp.einsum('btgp,ghp->btgh', s_re, c_re)
         - jnp.einsum('btgp,ghp->btgh', s_im, c_im)
         + d_skip.reshape(SSM_GROUPS, SSM_GROUP) * ug)
    return y.reshape(bt, t, SSM_WIDTH), s_re[:, -1], s_im[:, -1]

def hybrid_layer(x, p, conv_buf, s_re, s_im, ffn_buf,
                 norm_mix, w_in, conv_a_w, conv_a_b, w_out_a,
                 log_dt, lam_re, lam_im, b_re, b_im, c_re, c_im, d_skip,
                 w_glu_a, w_glu_b, w_o,
                 norm_ffn, w_up, ffn_conv_w, ffn_conv_b, w_down,
                 norm_ple, w_ple_gate, w_ple):
    xn = rms_norm(x, norm_mix)
    h, gate_b_in, gate_c_in, u, gate_a, gate_s = jnp.split(xn @ w_in, SPLITS, axis=-1)
    conv_y, new_conv_buf = causal_dwconv(gate_c_in * h, conv_buf, conv_a_w, conv_a_b)
    z_a = (gate_b_in * conv_y) @ w_out_a
    ssm_y, new_re, new_im = s5_mimo(u, s_re, s_im, log_dt, lam_re, lam_im,
                                    b_re, b_im, c_re, c_im, d_skip)
    ssm_y = jax.nn.gelu(ssm_y)
    z_b = (ssm_y @ w_glu_a) * jax.nn.sigmoid(ssm_y @ w_glu_b)
    x = x + (jax.nn.sigmoid(gate_a) * z_a + jax.nn.sigmoid(gate_s) * z_b) @ w_o
    up_a, up_b = jnp.split(rms_norm(x, norm_ffn) @ w_up, 2, axis=-1)
    up_a, new_ffn_buf = causal_dwconv(up_a, ffn_buf, ffn_conv_w, ffn_conv_b)
    x = x + (jax.nn.gelu(up_a) * up_b) @ w_down
    x = x + jax.nn.sigmoid(rms_norm(x, norm_ple) @ w_ple_gate) * (p @ w_ple)
    return x, new_conv_buf, new_re, new_im, new_ffn_buf

def run_trunk(x, p, conv_bufs, ssm_re, ssm_im, ffn_bufs,
              norm_mix, w_in, conv_a_w, conv_a_b, w_out_a,
              log_dt, lam_re, lam_im, b_re, b_im, c_re, c_im, d_skip,
              w_glu_a, w_glu_b, w_o,
              norm_ffn, w_up, ffn_conv_w, ffn_conv_b, w_down,
              norm_ple, w_ple_gate, w_ple, norm_final):
    new_conv, new_re, new_im, new_ffn = [], [], [], []
    for i in range(DEPTH):
        x, cb, sr, si, fb = hybrid_layer(
            x, p[i], conv_bufs[i], ssm_re[i], ssm_im[i], ffn_bufs[i],
            norm_mix[i], w_in[i], conv_a_w[i], conv_a_b[i], w_out_a[i],
            log_dt[i], lam_re[i], lam_im[i], b_re[i], b_im[i], c_re[i], c_im[i], d_skip[i],
            w_glu_a[i], w_glu_b[i], w_o[i],
            norm_ffn[i], w_up[i], ffn_conv_w[i], ffn_conv_b[i], w_down[i],
            norm_ple[i], w_ple_gate[i], w_ple[i])
        new_conv.append(cb)
        new_re.append(sr)
        new_im.append(si)
        new_ffn.append(fb)
    y = rms_norm(x, norm_final)
    return y, jnp.stack(new_conv), jnp.stack(new_re), jnp.stack(new_im), jnp.stack(new_ffn)

def setup_inputs(seed: int = 0) -> dict:
    key = jax.random.key(seed)
    ks = jax.random.split(key, 40)
    f32 = jnp.float32
    nrm = lambda k, shape, scale: scale * jax.random.normal(k, shape, f32)
    gain = lambda k, shape: 1.0 + 0.05 * jax.random.normal(k, shape, f32)
    n_idx = jnp.arange(SSM_STATE, dtype=f32)
    lam_re = -0.5 + 0.01 * jax.random.normal(ks[12], (DEPTH, SSM_GROUPS, SSM_STATE), f32)
    lam_im = math.pi * n_idx + 0.01 * jax.random.normal(ks[13], (DEPTH, SSM_GROUPS, SSM_STATE), f32)
    log_dt = jax.random.uniform(ks[11], (DEPTH, SSM_GROUPS), f32,
                                math.log(DT_MIN), math.log(DT_MAX))
    return {
        "x_prompt": nrm(ks[0], (BATCH, SEQ, D_MODEL), 1.0),
        "x_sample": nrm(ks[1], (DEC_BATCH, DEC_SEQ, D_MODEL), 1.0),
        "p_prompt": nrm(ks[2], (DEPTH, BATCH, SEQ, PLE_DIM), 1.0),
        "p_sample": nrm(ks[3], (DEPTH, DEC_BATCH, DEC_SEQ, PLE_DIM), 1.0),
        "state_conv_a": nrm(ks[4], (DEPTH, DEC_BATCH, CONV_WIDTH - 1, CONV_A_WIDTH), 1.0),
        "state_ssm_re": nrm(ks[5], (DEPTH, DEC_BATCH, SSM_GROUPS, SSM_STATE), 0.5),
        "state_ssm_im": nrm(ks[6], (DEPTH, DEC_BATCH, SSM_GROUPS, SSM_STATE), 0.5),
        "state_ffn_conv": nrm(ks[7], (DEPTH, DEC_BATCH, CONV_WIDTH - 1, D_FF), 1.0),
        "norm_mix": gain(ks[8], (DEPTH, D_MODEL)),
        "w_in": nrm(ks[9], (DEPTH, D_MODEL, IN_PROJ_WIDTH), D_MODEL ** -0.5),
        "conv_a_w": nrm(ks[10], (DEPTH, CONV_WIDTH, CONV_A_WIDTH), CONV_WIDTH ** -0.5),
        "conv_a_b": nrm(ks[14], (DEPTH, CONV_A_WIDTH), 0.01),
        "w_out_a": nrm(ks[15], (DEPTH, CONV_A_WIDTH, D_MODEL), CONV_A_WIDTH ** -0.5),
        "log_dt": log_dt,
        "lam_re": lam_re,
        "lam_im": lam_im,
        "b_re": nrm(ks[16], (DEPTH, SSM_GROUPS, SSM_STATE, SSM_GROUP), (2 * SSM_GROUP) ** -0.5),
        "b_im": nrm(ks[17], (DEPTH, SSM_GROUPS, SSM_STATE, SSM_GROUP), (2 * SSM_GROUP) ** -0.5),
        "c_re": nrm(ks[18], (DEPTH, SSM_GROUPS, SSM_GROUP, SSM_STATE), (2 * SSM_STATE) ** -0.5),
        "c_im": nrm(ks[19], (DEPTH, SSM_GROUPS, SSM_GROUP, SSM_STATE), (2 * SSM_STATE) ** -0.5),
        "d_skip": nrm(ks[20], (DEPTH, SSM_WIDTH), 0.5),
        "w_glu_a": nrm(ks[21], (DEPTH, SSM_WIDTH, D_MODEL), SSM_WIDTH ** -0.5),
        "w_glu_b": nrm(ks[22], (DEPTH, SSM_WIDTH, D_MODEL), SSM_WIDTH ** -0.5),
        "w_o": nrm(ks[23], (DEPTH, D_MODEL, D_MODEL), D_MODEL ** -0.5),
        "norm_ffn": gain(ks[24], (DEPTH, D_MODEL)),
        "w_up": nrm(ks[25], (DEPTH, D_MODEL, 2 * D_FF), D_MODEL ** -0.5),
        "ffn_conv_w": nrm(ks[26], (DEPTH, CONV_WIDTH, D_FF), CONV_WIDTH ** -0.5),
        "ffn_conv_b": nrm(ks[27], (DEPTH, D_FF), 0.01),
        "w_down": nrm(ks[28], (DEPTH, D_FF, D_MODEL), D_FF ** -0.5),
        "norm_ple": gain(ks[29], (DEPTH, D_MODEL)),
        "w_ple_gate": nrm(ks[30], (DEPTH, D_MODEL, D_MODEL), D_MODEL ** -0.5),
        "w_ple": nrm(ks[31], (DEPTH, PLE_DIM, D_MODEL), PLE_DIM ** -0.5),
        "norm_final": gain(ks[32], (D_MODEL,)),
    }

def reference(x_prompt, x_sample, p_prompt, p_sample,
              state_conv_a, state_ssm_re, state_ssm_im, state_ffn_conv,
              norm_mix, w_in, conv_a_w, conv_a_b, w_out_a,
              log_dt, lam_re, lam_im, b_re, b_im, c_re, c_im, d_skip,
              w_glu_a, w_glu_b, w_o,
              norm_ffn, w_up, ffn_conv_w, ffn_conv_b, w_down,
              norm_ple, w_ple_gate, w_ple, norm_final):
    weights = (norm_mix, w_in, conv_a_w, conv_a_b, w_out_a,
               log_dt, lam_re, lam_im, b_re, b_im, c_re, c_im, d_skip,
               w_glu_a, w_glu_b, w_o,
               norm_ffn, w_up, ffn_conv_w, ffn_conv_b, w_down,
               norm_ple, w_ple_gate, w_ple, norm_final)
    bp = x_prompt.shape[0]
    dt_ = x_prompt.dtype
    zero_conv = jnp.zeros((DEPTH, bp, CONV_WIDTH - 1, CONV_A_WIDTH), dt_)
    zero_re = jnp.zeros((DEPTH, bp, SSM_GROUPS, SSM_STATE), dt_)
    zero_im = jnp.zeros((DEPTH, bp, SSM_GROUPS, SSM_STATE), dt_)
    zero_ffn = jnp.zeros((DEPTH, bp, CONV_WIDTH - 1, D_FF), dt_)
    y_prompt, conv_a_p, ssm_re_p, ssm_im_p, ffn_p = run_trunk(
        x_prompt, p_prompt, zero_conv, zero_re, zero_im, zero_ffn, *weights)
    y_sample, conv_a_s, ssm_re_s, ssm_im_s, ffn_s = run_trunk(
        x_sample, p_sample, state_conv_a, state_ssm_re, state_ssm_im, state_ffn_conv, *weights)
    return (y_prompt, y_sample, conv_a_p, ssm_re_p, ssm_im_p, ffn_p,
            conv_a_s, ssm_re_s, ssm_im_s, ffn_s)


_drawn_inputs = setup_inputs


def setup_inputs(seed=0):
    import zlib

    import numpy as np

    out = dict(_drawn_inputs(seed))
    spreads = {}
    factors = {'conv_a_b': 8.0, 'lam_re': 4.048, 'w_glu_b': 2.674, 'ffn_conv_b': 8.0, 'norm_ple': 7.61}
    for name, (base, spread) in spreads.items():
        noise = np.random.default_rng([zlib.crc32(name.encode()), seed]).standard_normal(out[name].shape)
        drawn = base * np.exp(spread * noise) if base else spread * noise
        out[name] = __import__('jax').numpy.asarray(drawn.astype(out[name].dtype))
    for name, factor in factors.items():
        out[name] = (out[name] * factor).astype(out[name].dtype)
    return out
```

```python
import math
from contextlib import ExitStack

import concourse.bass as bass
from concourse import mybir

F32 = mybir.dt.float32
F32R = mybir.dt.float32r
I32 = mybir.dt.int32
ALU = mybir.AluOpType
ACT = mybir.ActivationFunctionType

P = 128
D = 1024
SEQ = 1024
NB = 8
T = SEQ + NB
NCH = 3
TN = T // NCH
DT = D // P
CA = D // 2
CT = CA // P
FF = 2816
FT = FF // P
FP = FT // 2
PLE = 256
PT = PLE // P
G = 32
NJ = G // 2
HG = 16
NS = 64
CH = 8
NC = SEQ // CH
NBLK = NC // CH
UC = NC + NB
UW = NC + 2 * NB
SW = NB + 1 + NC + NB
EPS = 1e-6

def A_POW(k, c):
    return 2 * k + c
def A_CHUNK(i, c):
    return 2 * (CH + 1) + 2 * (i - 1) + c
def A_BLOCK(r, c):
    return A_CHUNK(CH, c) if r == 0 else 34 + 2 * (r - 1) + c
COEF = 40
NPOW = 42

K_MIX, K_FFN, K_PLE, K_CAW, K_CAB, K_DSK, K_FW, K_FB = 0, 8, 16, 24, 36, 40, 44, 110
NK1, NK2 = 44, 88

IN_H, IN_B, IN_C, IN_U, IN_GA, IN_GS = 0, 4, 8, 12, 16, 24

N_U0, N_NORM1 = 0, 1
def n_u(q): return 0 if q == 0 else 1 + q
N_P2, G_P2 = 5, 4
N_P3, G_P3 = 17, 16
N_P4, G_P4 = 33, 32
N_P5, G_P5 = 57, 48
N_A0, G_A0, N_NORM2 = 65, 56, 66
N_P6, G_P6 = 67, 57
N_END, G_END = N_P6 + 12 * (FP - 1), G_P6 + 4 * (FP - 1)
N_DOWN_END = N_END + 3
N_P7, G_P7 = N_DOWN_END + DT, G_END + 3
N_NORM3, N_PW0, N_G1 = N_P7 + 1, N_P7 + 2, N_P7 + 3
N_P7L, G_P7L = N_P7 + 5, G_P7 + 2
N_P8 = N_P7L + 12

M_VEC, M_CB, M_S0, M_CT, M_X = 0, 1, 2, 3, 4
M_AP = M_X + 18
M_W1 = M_AP + 2
M_G = M_W1 + 8
M_V = M_G + 8
M_PT = M_V + 32
M_OUT = M_PT + 5


def _stage_count(g, i=None, per_trip=0):
    if g % 2 == 0 or g < G_P4:
        n, each = 16 * (g // 2 + 1), 16
    elif g < G_P5:
        n, each = 16 * (G_P4 // 2) + 32 * ((g - G_P4) // 2 + 1), 32
    else:
        n, each = 16 * (G_P4 // 2) + 32 * DT + 16 * ((g - G_P5) // 2 + 1), 16
    return n if i is None else n + i * (each * per_trip // 2)


class _Steps:

    def __init__(self, eng, sem):
        self.eng, self.sem, self.n, self.i, self.per = eng, sem, 0, None, 0

    def link(self, ins):
        ins.then_inc(self.sem, 1)
        self.n += 1
        self.eng.wait_ge(self.sem, self.n if self.i is None else self.i * self.per + self.n)

    def enter(self, i, per):
        self.i, self.per, self.start = i, per, self.n

    def leave(self, trips):
        assert self.n - self.start == self.per, (self.n - self.start, self.per)
        self.n = self.start + trips * self.per
        self.i = None


def decoder_step(nc, a, out):
    ctx = ExitStack()
    with ctx:
        def sem(name):
            return ctx.enter_context(nc.semaphore(name))

        base = (nc.sbuf_base + 31) // 32 * 32
        TB4 = 4 * T
        A0 = base
        B0 = A0 + 16 * TB4
        C0 = B0 + 8 * TB4
        D0 = C0 + 8 * TB4
        E0 = D0 + 8 * TB4

        def at(name, shape, off, dt=F32):
            return nc.alloc_sbuf_tensor_at(name, shape, dt, offset=off)

        XH = at("XH", [P, DT * T], A0, F32R)
        XL = at("XL", [P, DT * T], A0 + 8 * TB4, F32R)
        XLo = A0 + 8 * TB4
        VA1 = at("VEC1", [NK1, P], XLo)
        VA2 = at("VEC2", [NK2, P], XLo + 512)
        CN = at("CN", [P, 2, 2, P], XLo + 1024)
        CBN = at("CBN", [2 * NB, CA + FF], XLo + 3072)
        S0N = at("S0N", [NB, 2, NJ * P], XLo + 3072 + 4 * (CA + FF))
        OUTT = [at(f"OUTT{i}", [P, D], A0 + 4096 * i) for i in range(3)]
        GF = at("GF", [P, D], A0 + 3 * 4096)
        XN = at("XN", [P, DT, D], B0)
        W1T = at("W1T", [P, 2, NJ, CH * HG], B0)
        MT = at("MT", [P, NJ * (CH + 1) * HG], B0 + 16384)
        BB = at("BB", [P, 2, NJ, HG], B0 + 16384 + 9216)
        VAH = at("VAH", [P, CT * T], B0, F32R)
        VAL = at("VAL", [P, CT * T], B0 + CT * TB4, F32R)
        TL = at("TL", [P, DT * T], B0, F32R)
        GH = at("GH", [P, 2 * T], B0, F32R)
        GL = at("GL", [P, 2 * T], B0 + 2 * TB4, F32R)
        PSS = at("PSS", [NB, PLE], B0)
        PH = at("PH", [P, PT * T], B0 + 4 * TB4, F32R)
        PL = at("PL", [P, PT * T], B0 + 6 * TB4, F32R)
        SST = at("SST", [NB + 1, 2 * NJ * P], B0)
        AP = at("AP", [NJ, NPOW, P], C0)
        tiny0 = C0 + NPOW * 512
        LAM = at("LAM", [NJ, 2, P], tiny0)
        LDT = at("LDT", [NJ, 2], tiny0 + 1024)
        DTM = at("DTM", [NJ, 2], tiny0 + 1056)
        E1 = at("E1", [NJ, P], tiny0 + 1088)
        E2 = at("E2", [NJ, P], tiny0 + 1600)
        E3 = at("E3", [NJ, P], tiny0 + 2112)
        EI = at("EI", [NJ, P], tiny0 + 2624, I32)
        KF = at("KF", [NJ, 2, P], tiny0 + 3136)
        CS = at("CS", [NJ, 2, P], tiny0 + 4160)
        Q1 = at("Q1", [NJ, 4, P], tiny0 + 5184)
        Q2 = at("Q2", [NJ, 4, P], tiny0 + 7232)
        W1 = at("W1", [P, 2, NJ, P], C0)
        TO = at("TO", [P, G, P], C0 + 16384)
        TF = at("TF", [P, DT * T], C0)
        TH = at("TH", [P, DT * T], C0, F32R)
        DHW = at("DHW", [P, 2 * D], C0, F32R)
        DLW = at("DLW", [P, 2 * D], C0 + 8192, F32R)
        DST = at("DST", [P, 2, D], C0 + 16384)
        PST = at("PST", [P, DT, PLE], C0 + 24576)
        OST = at("OST", [NB + 2, CA + FF], C0 + 16384)
        XT = at("XT", [P, DT * T], D0)
        W2 = at("W2", [P, 2, NJ, (CH + 1) * HG], D0)
        U = at("U", [P, CH, UW], D0 + 18432)
        S = at("S", [P, 2, 4, SW], D0 + 18432 + 4608)
        GB = at("GB", [HG, NJ, P], D0 + 18432)
        APT = at("APT", [P, NPOW, NJ], D0 + 18432 + 4608 + 4640)
        YST = at("YST", [P, 3, UC], D0 + 18432 + 4608 + 4640 + 4 * NPOW * NJ)
        YGH = at("YGH", [P, CT * T], D0, F32R)
        YGL = at("YGL", [P, CT * T], D0 + CT * TB4, F32R)
        X = XT
        RS = at("RS", [P, T], E0)
        W0 = E0 + TB4
        WST = at("WST", [P, 2, D], W0)
        WH = at("WH", [P, 2 * D], W0 + 8192, F32R)
        WL = at("WL", [P, 2 * D], W0 + 16384, F32R)
        T0 = W0 + 24576
        TA = at("TA", [P, T], T0)
        TBf = at("TB", [P, T], T0 + TB4)
        TC = at("TC", [P, T], T0 + 2 * TB4)
        XS = at("XS", [NB, D], T0)
        BN = at("BN", [P, 2, NJ, HG], T0 + 2 * TB4)
        CTT = at("CTT", [P, 2, NJ, HG], T0 + 2 * TB4 + 2048)
        ST1 = at("ST1", [P, 480], T0 + 2 * TB4)
        ST2 = at("ST2", [P, 480], T0 + 2 * TB4 + 1920)
        k0 = T0 + 3 * TB4
        IDN = at("IDN", [P, P], k0)
        ONES = at("ONES", [P, P], k0 + 512)
        KV = at("KV", [P, NK1 + NK2], k0 + 1024)
        CB = at("CB", [P, CT + FT, 2 * NB], k0 + 1024 + 544)
        LAST = at("LAST", [P, CT + FT, NB + 2], k0 + 1568 + 1664)
        FS = at("FS", [P, 2, NJ, NB + 1], k0 + 3232 + 1056)
        S0 = at("S0", [P, 2, NJ, NB], k0 + 4288 + 1152)
        US = at("US", [P, CT, NB], k0 + 5440 + 1024)
        EP = at("EP", [P, 1], k0 + 6464 + 128)
        SSC = at("SSC", [P, 4], k0 + 6592 + 32)

        PS = ctx.enter_context(nc.psum_tensor("PS", [P, 8, 512], F32))
        xscr = nc.dram_tensor("xscr", [DT, P, T], F32, kind="Internal").ap()
        uscr = nc.dram_tensor("uscr", [CA, T], F32, kind="Internal").ap()
        yscr = nc.dram_tensor("yscr", [G, P, UC], F32, kind="Internal").ap()

        s_idn = sem("s_idn")
        s_lam = sem("s_lam")
        s_nat = sem("s_nat")
        s_bn = sem("s_bn")
        s_x = [sem(f"s_x{t}") for t in range(5)]
        s_md = sem("s_md")
        s_mf = sem("s_mf")
        s_stage = [sem("s_stage0"), sem("s_stage1")]
        s_wh = sem("s_wh")
        s_wl = sem("s_wl")
        s_po = sem("s_po")
        s_ev = sem("s_ev")
        s_sq = sem("s_sq")
        s_acc = sem("s_acc")
        s_xh = sem("s_xh")
        s_xl = sem("s_xl")
        s_rt = sem("s_rt")
        s_dv = sem("s_dv")
        s_ac = sem("s_ac")
        s_pl = sem("s_pl")
        s_xsp = sem("s_xsp")
        s_xr = [sem("s_xr0"), sem("s_xr1")]
        s_ang = sem("s_ang")
        s_sin = sem("s_sin")
        s_pow = sem("s_pow")
        s_w1t = sem("s_w1t")
        s_w2 = sem("s_w2")
        s_z = sem("s_z")
        s_to = [sem("s_to0"), sem("s_to1")]
        s_us = [sem(f"s_us{q}") for q in range(CT)]
        s_ul = [sem(f"s_ul{q}") for q in range(CT)]
        s_uz = sem("s_uz")
        s_scan = sem("s_scan")
        s_ys = sem("s_ys")
        s_yl = sem("s_yl")
        s_ci = sem("s_ci")
        s_cb = sem("s_cb")
        s_va = sem("s_va")
        s_vh = sem("s_vh")
        s_vl = sem("s_vl")
        s_y = sem("s_y")
        s_yg = sem("s_yg")
        s_yl2 = sem("s_yl2")
        s_sa = sem("s_sa")
        s_sg = sem("s_sg")
        s_tf = sem("s_tf")
        s_th = sem("s_th")
        s_tl = sem("s_tl")
        s_fi = sem("s_fi")
        s_fb = sem("s_fb")
        s_fc = sem("s_fc")
        s_ge = sem("s_ge")
        s_g = sem("s_g")
        s_gh = sem("s_gh")
        s_gl = sem("s_gl")
        s_dst = sem("s_dst")
        s_dh = sem("s_dh")
        s_dl = sem("s_dl")
        s_p = sem("s_p")
        s_ph = sem("s_ph")
        s_sp = sem("s_sp")
        s_xo = sem("s_xo")
        s_gf = sem("s_gf")
        s_ss = sem("s_ss")
        s_ot = sem("s_ot")
        s_or = [sem(f"s_or{i}") for i in range(3)]
        s_so = sem("s_so")
        s_out = sem("s_out")

        block = ctx.enter_context(nc.Block())

        def set3(n):
            s = n % 2
            return PS[:, 3 * s:3 * s + 3, 0:TN]

        def bank(k):
            return PS[:, 6 + k % 2, :]

        def v3(t):
            return t.rearrange("p (c n) -> p c n", n=TN)

        def tile(t, m):
            return t[:, bass.ts(m, T)]

        @block.sync
        def _(sp):
            win = a["w_in"][0].rearrange("(k p) n -> p k n", p=P)
            wup = a["w_up"][0].rearrange("(k p) n -> p k n", p=P)
            woa = a["w_out_a"][0].rearrange("(k p) n -> p k n", p=P)
            wga = a["w_glu_a"][0].rearrange("(k p) n -> p k n", p=P)
            wgb = a["w_glu_b"][0].rearrange("(k p) n -> p k n", p=P)
            wo = a["w_o"][0].rearrange("(k p) n -> p k n", p=P)
            wgt = a["w_ple_gate"][0].rearrange("(k p) n -> p k n", p=P)
            wdn = a["w_down"][0].rearrange("(f p) n -> p f n", p=P)
            wpl = a["w_ple"][0].rearrange("(f p) n -> p f n", p=P)

            def load(slot, src, tiles=DT, off=0):
                dst = WST[:, slot, off * P:(off + tiles) * P].rearrange("p (k n) -> p k n", n=P)
                sp.dma_start(dst, src).then_inc(s_stage[slot], 16)

            def tiles_of(w, col):
                return w[:, :, bass.ts(col, P)]

            pair = "(j two) p -> j (two p)"
            sp.dma_start(LAM[:, 0, :], a["lam_re"][0].rearrange(pair, two=2)).then_inc(s_lam, 16)
            sp.dma_start(LAM[:, 1, :], a["lam_im"][0].rearrange(pair, two=2)).then_inc(s_lam, 16)
            sp.dma_start(LDT[:, :], a["log_dt"][0].rearrange("(j two) -> j two", two=2)).then_inc(s_lam, 16)
            row = "(t p) -> t p"
            for k, name in ((K_MIX, "norm_mix"), (K_FFN, "norm_ffn"), (K_PLE, "norm_ple"),
                            (K_CAB, "conv_a_b"), (K_DSK, "d_skip")):
                n = a[name].shape[1] // P
                sp.dma_start(VA1[k:k + n, :], a[name][0].rearrange(row, p=P)).then_inc(s_nat, 16)
            sp.dma_start(VA1[K_CAW:K_CAB, :], a["conv_a_w"][0].rearrange("k (t p) -> (k t) p", p=P)).then_inc(s_nat, 16)
            sp.dma_start(VA2[0:3 * FT, :], a["ffn_conv_w"][0].rearrange("k (t p) -> (k t) p", p=P)).then_inc(s_nat, 16)
            sp.dma_start(VA2[3 * FT:4 * FT, :], a["ffn_conv_b"][0].rearrange(row, p=P)).then_inc(s_nat, 16)
            sp.dma_start(CBN[:, 0:CA], a["state_conv_a"][0].rearrange("b k d -> (b k) d")).then_inc(s_nat, 16)
            sp.dma_start(CBN[:, CA:], a["state_ffn_conv"][0].rearrange("b k d -> (b k) d")).then_inc(s_nat, 16)
            sp.dma_start(S0N[:, 0, :], a["state_ssm_re"][0].rearrange("b g p -> b (g p)")).then_inc(s_nat, 16)
            sp.dma_start(S0N[:, 1, :], a["state_ssm_im"][0].rearrange("b g p -> b (g p)")).then_inc(s_nat, 16)
            for c, name in enumerate(("c_re", "c_im")):
                cj = a[name][0].rearrange("(j two) h p -> j h two p", two=2)
                for half in range(2):
                    for j in range(8):
                        sp.dma_start(CN[j * HG:(j + 1) * HG, c, half, :].rearrange("h (two p) -> h two p", two=2),
                                     cj[8 * half + j]).then_inc(s_nat, 16)
            load(0, tiles_of(win, IN_U))
            load(1, tiles_of(win, IN_U + 1))
            for c, name in enumerate(("b_re", "b_im")):
                sp.dma_start(BN[:, c, :, :], a[name][0].rearrange("(j two) p h -> (two p) j h", two=2)).then_inc(s_bn, 16)
            for q in (2, 3):
                sp.wait_ge(s_wl, q - 1)
                load(q % 2, tiles_of(win, IN_U + q))
            sp.wait_ge(s_mf, M_AP)
            sp.dma_start(xscr.rearrange("m p t -> p m t"), XT[:, :].rearrange("p (m t) -> p m t", t=T)).then_inc(s_xsp, 16)

            def conv_group(g):
                q, part = divmod(g - G_P2, 3)
                sp.wait_ge(s_wl, g - 1)
                load(g % 2, tiles_of(win, (IN_H, IN_C, IN_B)[part] + q))

            conv_group(G_P2)
            for half in range(2):
                sp.wait_ge(s_z, 1)
                sp.wait_ge(s_mf, M_G + 4 * half + 4)
                for r in range(CH):
                    i = CH - 1 - r
                    sp.dma_start(TO[r * HG:(r + 1) * HG, half * NJ:(half + 1) * NJ, i * HG:P],
                                 GB[:, :, 0:P - i * HG]).then_inc(s_to[half], 16)
            conv_group(G_P2 + 1)
            def load_u(q):
                sp.wait_ge(s_us[q], 32)
                if q == 0:
                    sp.wait_ge(s_to[1], 16 * CH)
                    sp.wait_ge(s_uz, 1)
                else:
                    sp.wait_ge(s_md, M_V + 8 * q)
                src = uscr[q * P:(q + 1) * P, :].rearrange("(g h) t -> h g t", h=HG)
                for r in range(CH):
                    i = CH - 1 - r
                    sp.dma_start(U[r * HG:(r + 1) * HG, :, NB:NB + NC], src[:, :, i * NC:(i + 1) * NC]).then_inc(s_ul[q], 16)
                sp.dma_start(U[0:HG, :, NB + NC:UW], src[:, :, SEQ:T]).then_inc(s_ul[q], 16)
                sp.dma_start(U[P - HG:P, :, 0:NB], src[:, :, SEQ:T]).then_inc(s_ul[q], 16)

            load_u(0)
            for q in range(CT):
                for part in range(3):
                    g = G_P2 + 3 * q + part + 2
                    if g < G_P3:
                        conv_group(g)
                    if part == 0 and q > 0:
                        load_u(q)
            def p3_loads(i):
                for j in range(2):
                    m = i * 2 + j
                    sp.wait_ge(s_wl, i * 4 + (G_P3 + 2 * j - 1))
                    load(0, tiles_of(win, m + IN_GA))
                    sp.wait_ge(s_wl, i * 4 + (G_P3 + 2 * j))
                    load(1, tiles_of(woa, m), CT)
            with sp.Fori(0, 4) as i:
                p3_loads(i)
                sp.wait_ge(s_ys, 16 * 16)
                sp.wait_ge(s_yl2, i + 1)
                for g in range(8):
                    sp.dma_start(TA[g * HG:(g + 1) * HG, 0:SEQ].rearrange("h (i c) -> h i c", c=NC),
                                 yscr[i * 8 + g].rearrange("(i h) c -> h i c", h=HG)[:, :, NB:UC]).then_inc(s_yl, 16)
                    sp.dma_start(TA[g * HG:(g + 1) * HG, SEQ:T], yscr[i * 8 + g, 0:HG, 0:NB]).then_inc(s_yl, 16)
                sp.dma_start(TBf[:, :], uscr[bass.ts(i, P), :]).then_inc(s_yl, 16)
            with sp.Fori(0, DT) as m:
                sp.wait_ge(s_wl, m * 2 + (G_P4 - 1))
                load(0, tiles_of(win, m + IN_GS))
                sp.wait_ge(s_wl, m * 2 + G_P4)
                load(1, tiles_of(wgb, m), CT)
                load(1, tiles_of(wga, m), CT, CT)
            with sp.Fori(0, 4) as i:
                for j in range(2):
                    sp.wait_ge(s_wl, i * 2 + (G_P5 + j - 1))
                    load(j, tiles_of(wo, i * 2 + j))
                    if j == 0:
                        sp.wait_ge(s_tl, DT + 1)
                    sp.wait_ge(s_ev, i * 2 + (N_P5 + j - 1))
                    sp.dma_start((TA, TBf)[j][:, :], xscr[i * 2 + j]).then_inc(s_xr[j], 16)
            sp.wait_ge(s_wl, G_A0 - 1)
            load(0, tiles_of(wup, 0))
            sp.wait_ge(s_po, N_P5 + DT)
            sp.dma_start(PST[:, :, :], a["p_prompt"][0, 0].rearrange("(t p) d -> p t d", p=P)).then_inc(s_p, 16)
            sp.dma_start(PSS[:, :], a["p_sample"][0, :, 0, :]).then_inc(s_p, 16)
            sp.dma_start(DST[:, :, :], wdn[:, 0:2, :]).then_inc(s_dst, 16)
            with sp.Fori(0, FP - 1) as p:
                for j, col in ((0, p * 2 + FT), (1, p * 2 + 1), (2, p * 2 + (FT + 1)), (3, p * 2 + 2)):
                    sp.wait_ge(s_wl, p * 4 + (G_P6 + j - 1))
                    load((G_P6 + j) % 2, tiles_of(wup, col))
                    if j == 3:
                        sp.wait_ge(s_dl, p + 1)
                        sp.dma_start(DST[:, :, :], wdn[:, bass.ds(p * 2 + 2, 2), :]).then_inc(s_dst, 16)
            for j, col in enumerate((2 * FT - 2, FT - 1, 2 * FT - 1)):
                sp.wait_ge(s_wl, G_END + j - 1)
                load((G_END + j) % 2, tiles_of(wup, col))
            sp.wait_ge(s_dl, FP)
            sp.dma_start(DST[:, :, :], wpl).then_inc(s_dst, 16)
            for m in range(2):
                sp.wait_ge(s_wl, G_P7 + m - 1)
                load((G_P7 + m) % 2, tiles_of(wgt, m))
            with sp.Fori(0, 3) as i:
                for j in range(2):
                    sp.wait_ge(s_wl, i * 2 + (G_P7L + j - 1))
                    load(j, tiles_of(wgt, i * 2 + (2 + j)))
            sp.wait_ge(s_mf, M_OUT + 15)
            sp.dma_start(out["conv_a_p"][0, 0], OST[0:2, 0:CA]).then_inc(s_so, 16)
            sp.dma_start(out["conv_a_s"][0, :, 1, :], OST[2:2 + NB, 0:CA]).then_inc(s_so, 16)
            sp.dma_start(out["conv_a_s"][0, :, 0, :], a["state_conv_a"][0, :, 1, :]).then_inc(s_so, 16)
            sp.dma_start(out["ffn_p"][0, 0], OST[0:2, CA:]).then_inc(s_so, 16)
            sp.dma_start(out["ffn_s"][0, :, 1, :], OST[2:2 + NB, CA:]).then_inc(s_so, 16)
            sp.dma_start(out["ffn_s"][0, :, 0, :], a["state_ffn_conv"][0, :, 1, :]).then_inc(s_so, 16)
            for c, part in enumerate(("re", "im")):
                half = SST[:, c * NJ * P:(c + 1) * NJ * P]
                sp.dma_start(out[f"ssm_{part}_p"][0].rearrange("b g p -> b (g p)"), half[0:1, :]).then_inc(s_so, 16)
                sp.dma_start(out[f"ssm_{part}_s"][0].rearrange("b g p -> b (g p)"), half[1:1 + NB, :]).then_inc(s_so, 16)
            sp.wait_ge(s_po, N_P8)
            sp.dma_start(GF[:, :], a["norm_final"].rearrange("(o n) -> o n", o=1).to_broadcast([P, D])).then_inc(s_gf, 16)
            for t in range(DT + 1):
                sp.wait_ge(s_ev, N_P8 + t + 1)
                if t < DT:
                    sp.dma_start(out["y_prompt"][0, t * P:(t + 1) * P, :], OUTT[t % 3][:, :]).then_inc(s_or[t % 3], 16)
                else:
                    sp.dma_start(out["y_sample"][:, 0, :], OUTT[t % 3][0:NB, :]).then_inc(s_or[t % 3], 16)
            for r in range(3):
                sp.wait_ge(s_or[r], 48)
            sp.wait_ge(s_so, 160)

        @block.gpsimd
        def _(pool):
            own = _Steps(pool, s_pl)
            nc.gpsimd.memset(IDN[:, :], 0.0).then_inc(s_idn, 1)
            nc.gpsimd.memset(ONES[:, :], 1.0).then_inc(s_idn, 1)
            nc.gpsimd.memset(EP[:, :], EPS).then_inc(s_idn, 1)
            pool.wait_ge(s_idn, 3)
            nc.gpsimd.affine_select(out=IDN[:, :], in_=IDN[:, :], compare_op=ALU.not_equal, fill=1.0, base=0,
                                    pattern=[[-1, P]], channel_multiplier=1).then_inc(s_idn, 1)

            def lo(g, slot, tiles=DT):
                pool.wait_ge(s_wh, g + 1)
                w = slice(slot * D, slot * D + tiles * P)
                nc.gpsimd.tensor_tensor(WL[:, w], WST[:, slot, 0:tiles * P], WH[:, w].bitcast(F32),
                                        ALU.subtract).then_inc(s_wl, 1)

            def clear_sum():
                own.link(nc.gpsimd.memset(RS[:, :], 0.0))

            def add_squares(m, sq):
                pool.wait_ge(s_sq, m + 1)
                if not isinstance(m, int) or m:
                    pool.wait_ge(s_acc, m)
                nc.gpsimd.tensor_tensor(RS[:, :], RS[:, :], sq[:, :], ALU.add).then_inc(s_acc, 1)

            clear_sum()
            lo(0, 0)
            lo(1, 1)
            for m in range(DT):
                add_squares(m, TBf)
            pool.wait_ge(s_mf, M_W1)
            nc.gpsimd.memset(TO[:, :, :], 0.0).then_inc(s_z, 1)
            lo(2, 0)
            lo(3, 1)
            lo(4, 0)
            pool.wait_ge(s_to[1], 16 * CH)
            nc.gpsimd.memset(U[:, :, 0:NB], 0.0)
            nc.gpsimd.memset(U[:, :, NB + NC:UW], 0.0)
            nc.gpsimd.memset(S[:, :, :, NB:NB + 1], 0.0).then_inc(s_uz, 1)
            for g in range(G_P2 + 1, G_P3 + 1):
                lo(g, g % 2)
            with pool.Fori(0, DT) as m:
                lo(m * 2 + (G_P3 + 1), 1, CT)
                lo(m * 2 + (G_P3 + 2), 0)
            with pool.Fori(0, DT) as m:
                lo(m * 2 + (G_P4 + 1), 1)
                lo(m * 2 + (G_P4 + 2), 0)
            pool.wait_ge(s_ev, N_P4 + 3 * (DT - 1) + 1)
            clear_sum()
            with pool.Fori(0, 4) as i:
                for j in range(2):
                    lo(i * 2 + (G_P5 + j + 1), (j + 1) % 2)
                    add_squares(i * 2 + (DT + j), TC)

            def lo_down(p):
                pool.wait_ge(s_dh, p + 1)
                nc.gpsimd.tensor_tensor(DLW[:, :], DST[:, :, :].rearrange("p f n -> p (f n)"),
                                        DHW[:, :].bitcast(F32), ALU.subtract).then_inc(s_dl, 1)

            lo(G_P6, G_P6 % 2)
            with pool.Fori(0, FP - 1) as p:
                lo(p * 4 + (G_P6 + 1), 0)
                lo_down(p)
                for j in (1, 2, 3):
                    lo(p * 4 + (G_P6 + 1 + j), (G_P6 + 1 + j) % 2)
            lo(G_END + 1, 0)
            lo_down(FP - 1)
            lo(G_END + 2, 1)
            lo(G_P7, 0)
            pool.wait_ge(s_ev, N_DOWN_END)
            clear_sum()
            lo(G_P7 + 1, 1)
            for m in range(DT):
                add_squares(2 * DT + m, TC)
            lo_down(FP)
            lo(G_P7L, 0)
            for g in range(G_P7L + 1, G_P7 + DT):
                lo(g, g % 2)

        @block.scalar
        def _(act):
            own = _Steps(act, s_ac)
            copy = lambda o, i, f=ACT.Copy, **k: nc.scalar.activation(o, i, f, **k)

            def hi(g, slot, n_first, tiles=DT, i=None, per_trip=0):
                act.wait_ge(s_stage[slot], _stage_count(g, i, per_trip))
                if n_first is not None:
                    act.wait_ge(s_po, n_first)
                copy(WH[:, slot * D:slot * D + tiles * P], WST[:, slot, 0:tiles * P]).then_inc(s_wh, 1)

            def evict_misc(k, o, i, **kw):
                act.wait_ge(s_md, k + 1)
                copy(o, i, **kw).then_inc(s_mf, 1)

            def split_hi(count, xt, m, gain, sq, sums):
                if sums is not None:
                    act.wait_ge(s_acc, sums)
                copy(sq[:, :], xt, ACT.Square).then_inc(s_sq, 1)
                copy(tile(XH, m), xt, scale=gain).then_inc(s_xh, 1)

            def rms(n):
                act.wait_ge(s_po, n + 1)
                copy(v3(RS[:, :]), set3(n), ACT.Sqrt, bias=EP[:, :], scale=1.0 / D).then_inc(s_rt, 1)

            for t in range(4):
                src = a["x_prompt"][0, 2 * t * P:2 * (t + 1) * P, :].rearrange("(t p) d -> p t d", p=P)
                act.dma_start(XN[:, 2 * t:2 * t + 2, :], src).then_inc(s_x[t], 16)
            act.dma_start(XS[:, :], a["x_sample"][:, 0, :]).then_inc(s_x[4], 16)
            evict_misc(M_VEC, KV[:, :], bank(M_VEC)[:, 0:NK1 + NK2])
            evict_misc(M_CB, CB[:, :, :], bank(M_CB)[:, 0:(CT + FT) * 16].rearrange("p (t n) -> p t n", n=16))
            evict_misc(M_S0, S0[:, :, :, :], bank(M_S0)[:, 0:256].rearrange("p (c j b) -> p c j b", c=2, b=NB))
            evict_misc(M_CT, CTT[:, :, :, :], bank(M_CT)[:, :].rearrange("p (c j h) -> p c j h", c=2, h=HG))
            act.wait_ge(s_ang, 1)
            copy(CS[:, :, :], KF[:, :, :], ACT.Sin).then_inc(s_sin, 1)
            X3 = XT[:, :].rearrange("p (m t) -> p m t", t=T)
            for t in range(DT + 1):
                w = P if t < DT else NB
                for half in range(2):
                    evict_misc(M_X + 2 * t + half, X3[:, 4 * half:4 * half + 4, t * P:t * P + w],
                               bank(M_X + half)[:, :].rearrange("p (m t) -> p m t", t=P)[:, :, 0:w])
            hi(0, 0, None)
            hi(1, 1, None)
            act.wait_ge(s_mf, M_AP)
            for m in range(DT):
                split_hi(m, tile(XT, m), m, KV[:, K_MIX + m:K_MIX + m + 1], TBf, m if m else None)
            rms(N_NORM1)
            act.wait_ge(s_xl, DT)
            act.wait_ge(s_xsp, 16)
            evict_misc(M_AP, APT[:, 0:32, :], bank(M_AP)[:, :].rearrange("p (r j) -> p r j", j=NJ))
            evict_misc(M_AP + 1, APT[:, 32:NPOW, :],
                       bank(M_AP + 1)[:, 0:(NPOW - 32) * NJ].rearrange("p (r j) -> p r j", j=NJ))

            def store_u(q):
                act.wait_ge(s_ev, n_u(q) + 1)
                ut = (TA, TBf)[q % 2][:, :].rearrange("p (i c) -> p i c", i=CH)
                act.dma_start(uscr[q * P:(q + 1) * P, 0:SEQ].rearrange("p (i c) -> p i c", i=CH),
                              ut[:, :, 0:NC]).then_inc(s_us[q], 16)
                act.dma_start(uscr[q * P:(q + 1) * P, SEQ:T], US[:, q, :]).then_inc(s_us[q], 16)

            hi(2, 0, n_u(1))
            store_u(0)
            hi(3, 1, n_u(2))
            store_u(1)
            W1f = W1[:, :, :, :].rearrange("p c j n -> p (c j) n")
            for s in range(8):
                evict_misc(M_W1 + s, W1f[:, 4 * s:4 * s + 4, :], bank(M_W1 + s)[:, :].rearrange("p (j n) -> p j n", n=P))
            hi(4, 0, n_u(3))
            store_u(2)
            G4 = GB[:, :, :].rearrange("h (j two) n -> h j two n", two=2)
            for s in range(8):
                if s == 4:
                    act.wait_ge(s_to[0], 16 * CH)
                jj = 4 * ((s // 2) % 2)
                evict_misc(M_G + s, G4[:, jj:jj + 4, s % 2, :], bank(M_G + s)[0:HG, :].rearrange("p (j n) -> p j n", n=P))
            store_u(3)
            yst = [0]

            def evict_y(q):
                for s, (g0, ng) in enumerate(((0, 3), (1, 3), (6, 1), (7, 1))):
                    k = M_V + 8 * q + 4 + s
                    if yst[0]:
                        act.wait_ge(s_ys, 16 * yst[0])
                    evict_misc(k, YST[:, 0:ng, :], bank(k)[:, 0:ng * UC].rearrange("p (g c) -> p g c", c=UC))
                    act.wait_ge(s_mf, k + 1)
                    dst = yscr[8 * q + g0:8 * q + g0 + 2 * ng - 1:2]
                    act.dma_start(dst.rearrange("g p c -> p g c"), YST[:, 0:ng, :]).then_inc(s_ys, 16)
                    yst[0] += 1

            for q in range(CT):
                n = N_P2 + 3 * q
                g = G_P2 + 3 * q
                if q:
                    evict_y(q - 1)
                hi(g + 1, (g + 1) % 2, n)
                hi(g + 2, (g + 2) % 2, n + 1)
                if q:
                    act.wait_ge(s_scan, q)
                for j in range(4):
                    k = M_V + 8 * q + j
                    evict_misc(k, S[:, :, j, NB + 1:SW], bank(k)[:, 0:2 * UC].rearrange("p (c n) -> p c n", n=UC))
                act.wait_ge(s_ci, q + 1)
                copy(TA[:, :], TBf[:, :], ACT.Identity, scale=KV[:, K_CAW + 2 * CT + q:K_CAW + 2 * CT + q + 1],
                     bias=KV[:, K_CAB + q:K_CAB + q + 1]).then_inc(s_cb, 1)
                hi(g + 3, (g + 3) % 2, n + 2)
                act.wait_ge(s_va, q + 1)
                copy(tile(VAH, q), TA[:, :]).then_inc(s_vh, 1)
            evict_y(CT - 1)
            with act.Fori(0, 4) as i:
                for j in range(2):
                    n, g = N_P3 + 2 * j, G_P3 + 2 * j
                    m = i * 2 + j
                    hi(g + 1, 1, i * 4 + n, CT, i, 4)
                    act.wait_ge(s_ev, i * 4 + (n + 1))
                    copy(tile(TF, m), tile(TF, m), ACT.Sigmoid).then_inc(s_sa, 1)
                    hi(g + 2, 0, i * 4 + (n + 1), DT, i, 4)
                act.wait_ge(s_y, i + 1)
                copy(TC[:, 0:SEQ].rearrange("p (c i) -> p i c", i=CH), TA[:, 0:SEQ].rearrange("p (i c) -> p i c", i=CH),
                     ACT.Gelu_apprx_tanh).then_inc(s_yg, 1)
                copy(TC[:, SEQ:T], TA[:, SEQ:T], ACT.Gelu_apprx_tanh).then_inc(s_yg, 1)
                act.wait_ge(s_yg, i * 3 + 2)
                copy(tile(YGH, i), TC[:, :]).then_inc(s_yg, 1)
            with act.Fori(0, 4) as i:
                for j in range(2):
                    n, g = N_P4 + 3 * j, G_P4 + 2 * j
                    hi(g + 1, 1, i * 6 + n, DT, i, 4)
                    act.wait_ge(s_ev, i * 6 + (n + 1))
                    copy(TA[:, :], TA[:, :], ACT.Sigmoid).then_inc(s_sg, 1)
                    act.wait_ge(s_po, i * 6 + (n + 2))
                    act.wait_ge(s_tf, i * 2 + (j + 1))
                    copy(v3(TBf[:, :]), set3(n + 1), ACT.Sigmoid).then_inc(s_ev, 1)
                    hi(g + 2, 0, i * 6 + (n + 1), DT, i, 4)
                    act.wait_ge(s_tf, i * 2 + (j + 2))
                    copy(tile(TH, i * 2 + j), TA[:, :]).then_inc(s_th, 1)
            with act.Fori(0, 4) as i:
                for j in range(2):
                    m = i * 2 + j
                    hi(G_P5 + j + 1, (j + 1) % 2, i * 2 + (N_P5 + j), DT, i, 2)
                    act.wait_ge(s_ev, i * 2 + (N_P5 + j + 1))
                    split_hi(None, tile(XT, m), m, KV[:, bass.ds(m + K_FFN, 1)], TC, i * 2 + (DT + j))
            hi(G_P6, G_P6 % 2, N_A0)
            rms(N_NORM2)

            def hi_down(p, n_before):
                act.wait_ge(s_dst, p * 16 + 16)
                act.wait_ge(s_po, n_before)
                copy(DHW[:, :], DST[:, :, :].rearrange("p f n -> p (f n)")).then_inc(s_dh, 1)

            def conv_tap(f):
                act.wait_ge(s_fi, f + 1)
                copy(TBf[:, :], TA[:, :], ACT.Identity, scale=KV[:, bass.ds(f + (K_FW + 2 * FT), 1)],
                     bias=KV[:, bass.ds(f + K_FB, 1)]).then_inc(s_fb, 1)
                act.wait_ge(s_fc, f + 1)
                copy(TBf[:, :], TBf[:, :], ACT.Gelu_apprx_tanh).then_inc(s_ge, 1)

            def split_g(f, j):
                act.wait_ge(s_g, f + 1)
                copy(tile(GH, j), TC[:, :]).then_inc(s_gh, 1)

            conv_tap(0)
            for k in range(5):
                act.wait_ge(s_md, M_PT + k + 1)
                if k < 4:
                    kk, h = divmod(k, 2)
                    copy(PH[:, kk * T + 512 * h:kk * T + 512 * (h + 1)], bank(M_PT + k)[:, :]).then_inc(s_ph, 1)
                else:
                    copy(PH[:, :].rearrange("p (k t) -> p k t", t=T)[:, :, SEQ:T],
                         bank(M_PT + k)[:, 0:2 * NB].rearrange("p (k t) -> p k t", t=NB)).then_inc(s_ph, 1)
            with act.Fori(0, FP - 1) as p:
                nb = p * 12 + N_P6
                hi(G_P6 + 1, 0, nb, DT, p, 4)
                split_g(p * 2, 0)
                hi_down(p, nb)
                hi(G_P6 + 2, 1, nb + 1, DT, p, 4)
                conv_tap(p * 2 + 1)
                hi(G_P6 + 3, 0, nb + 2, DT, p, 4)
                split_g(p * 2 + 1, 1)
                hi(G_P6 + 4, 1, nb + 3, DT, p, 4)
                conv_tap(p * 2 + 2)
            hi(G_END + 1, 0, N_END)
            split_g(FT - 2, 0)
            hi_down(FP - 1, N_END)
            hi(G_END + 2, 1, N_END + 1)
            conv_tap(FT - 1)
            hi(G_P7, 0, N_END + 2)
            split_g(FT - 1, 1)
            hi(G_P7 + 1, 1, N_DOWN_END)
            for m in range(DT):
                act.wait_ge(s_ev, N_DOWN_END + m + 1)
                split_hi(None, tile(XT, m), m, KV[:, K_PLE + m:K_PLE + m + 1], TC, 2 * DT + m)
            hi_down(FP, N_P7)
            rms(N_NORM3)

            def ple_gate(m, n):
                act.wait_ge(s_ev, n + 1)
                copy(TA[:, :], TA[:, :], ACT.Sigmoid).then_inc(s_sp, 1)

            hi(G_P7L, 0, N_PW0 + 1)
            ple_gate(0, N_P7)
            ple_gate(1, N_G1)
            for k in range(7):
                w = 512 if k < 6 else 256
                evict_misc(M_OUT + k, OST[:, 512 * k:512 * k + w], bank(M_OUT + k)[0:NB + 2, 0:w])
            for k in range(8):
                evict_misc(M_OUT + 7 + k, SST[:, 512 * k:512 * (k + 1)], bank(M_OUT + 7 + k)[0:NB + 1, :])
            for m in range(2, DT):
                n = N_P7L + 2 * (m - 2)
                if m + 1 < DT:
                    hi(G_P7 + m + 1, (m + 1) % 2, n)
                ple_gate(m, n)
            for t in range(DT + 1):
                n = N_P8 + t
                w = P if t < DT else NB
                o = PS[0:w, 3 * (n % 2):3 * (n % 2) + 2, :].rearrange("p a b -> p (a b)")
                act.wait_ge(s_po, n + 1)
                if t >= 2:
                    act.wait_ge(s_ev, n - 1)
                own.link(copy(TC[0:w, 0:D], o, ACT.Square, accum_out=SSC[0:w, t % 2:t % 2 + 1]))
                copy(SSC[0:w, 2 + t % 2:3 + t % 2], SSC[0:w, t % 2:t % 2 + 1], ACT.Sqrt, bias=EP[0:w, :],
                     scale=1.0 / D).then_inc(s_ss, 1)

        @block.vector
        def _(dve):
            own = _Steps(dve, s_dv)
            link = own.link
            tt, ts_, stt = nc.vector.tensor_tensor, nc.vector.tensor_scalar, nc.vector.scalar_tensor_tensor
            MAGIC = 12582912.0

            def exp_small(o, x, e1, e2, ei):
                link(ts_(x, x, -87.0, 88.0, ALU.max, ALU.min))
                link(ts_(e1, x, 1.0 / math.log(2.0), MAGIC, ALU.mult, ALU.add))
                link(ts_(e1, e1, MAGIC, None, ALU.subtract))
                link(stt(x, e1, -0.693359375, x, ALU.mult, ALU.add))
                link(stt(x, e1, 2.12194440e-4, x, ALU.mult, ALU.add))
                link(ts_(e2, x, 1.0 / 5040, None, ALU.mult))
                for d in (720, 120, 24, 6, 2, 1):
                    link(stt(e2, e2, 1.0 / d, x, ALU.add, ALU.mult))
                link(ts_(e1, e1, 127.0, 8388608.0, ALU.add, ALU.mult))
                link(nc.vector.tensor_copy(ei, e1))
                link(stt(o, e2, 1.0, ei.bitcast(F32), ALU.add, ALU.mult))

            dve.wait_ge(s_lam, 48)
            exp_small(DTM[:, :], LDT[:, :], E1[:, 0:2], E2[:, 0:2], EI[:, 0:2])
            dtb = DTM[:, :].unsqueeze(2).to_broadcast([NJ, 2, NS])
            lre, lim = LAM[:, 0, :], LAM[:, 1, :]
            half = "j (two p) -> j two p"
            two = lambda v: v.rearrange(half, two=2)
            link(tt(two(E3[:, :]), two(lim), dtb, ALU.mult))
            link(ts_(KF[:, 0, :], E3[:, :], 1.0 / (2 * math.pi), 0.25, ALU.mult, ALU.add))
            link(ts_(KF[:, 1, :], E3[:, :], 1.0 / (2 * math.pi), None, ALU.mult))
            link(ts_(KF[:, :, :], KF[:, :, :], MAGIC, MAGIC, ALU.add, ALU.subtract))
            for c in range(2):
                dst = CS[:, c, :]
                src = E3[:, :]
                for part in (6.28125, 1.93500518798828125e-3, 3.0199159819e-7):
                    link(stt(dst, KF[:, c, :], -part, src, ALU.mult, ALU.add))
                    src = dst
            link(ts_(KF[:, 0, :], CS[:, 0, :], math.pi / 2, None, ALU.add))
            link(nc.vector.tensor_copy(KF[:, 1, :], CS[:, 1, :]))
            ts_(KF[:, :, :], KF[:, :, :], -3.1415925, 3.1415925, ALU.max, ALU.min).then_inc(s_ang, 1)
            link(tt(two(E3[:, :]), two(lre), dtb, ALU.mult))
            exp_small(Q1[:, 0, :], E3[:, :], E1[:, :], E2[:, :], EI[:, :])
            dve.wait_ge(s_sin, 1)
            mag = Q1[:, 0:1, :].to_broadcast([NJ, 2, P])
            link(nc.vector.memset(AP[:, A_POW(0, 0), :], 1.0))
            link(nc.vector.memset(AP[:, A_POW(0, 1), :], 0.0))
            link(tt(AP[:, A_POW(1, 0):A_POW(1, 1) + 1, :], CS[:, :, :], mag, ALU.mult))
            are, aim = AP[:, A_POW(1, 0), :], AP[:, A_POW(1, 1), :]
            link(tt(E1[:, :], lre, lre, ALU.mult))
            link(tt(E2[:, :], lim, lim, ALU.mult))
            link(tt(E1[:, :], E1[:, :], E2[:, :], ALU.add))
            link(nc.vector.reciprocal(E3[:, :], E1[:, :]))
            link(ts_(E1[:, :], are, -1.0, None, ALU.add))
            link(tt(E2[:, :], E1[:, :], lre, ALU.mult))
            link(tt(Q1[:, 0, :], aim, lim, ALU.mult))
            link(tt(E2[:, :], E2[:, :], Q1[:, 0, :], ALU.add))
            link(tt(AP[:, COEF, :], E2[:, :], E3[:, :], ALU.mult))
            link(tt(E2[:, :], E1[:, :], lim, ALU.mult))
            link(tt(Q1[:, 0, :], aim, lre, ALU.mult))
            link(tt(E2[:, :], Q1[:, 0, :], E2[:, :], ALU.subtract))
            link(tt(AP[:, COEF + 1, :], E2[:, :], E3[:, :], ALU.mult))

            def cmul(dst, src, by, n):
                rows = lambda r, c: AP[:, r:r + 2 * n, :].rearrange("j (n c) p -> j n c p", c=2)[:, :, c, :]
                b = [AP[:, by + c:by + c + 1, :].to_broadcast([NJ, n, P]) for c in range(2)]
                q1, q2 = Q1[:, 0:n, :], Q2[:, 0:n, :]
                tt(q1, rows(src, 0), b[0], ALU.mult).then_inc(s_dv, 1)
                link2(tt(q2, rows(src, 1), b[1], ALU.mult))
                link(tt(rows(dst, 0), q1, q2, ALU.subtract))
                tt(q1, rows(src, 0), b[1], ALU.mult).then_inc(s_dv, 1)
                link2(tt(q2, rows(src, 1), b[0], ALU.mult))
                link(tt(rows(dst, 1), q1, q2, ALU.add))

            def link2(ins):
                own.n += 1
                link(ins)

            r = A_POW
            cmul(r(2, 0), r(1, 0), r(1, 0), 1)
            cmul(r(3, 0), r(1, 0), r(2, 0), 2)
            cmul(r(5, 0), r(1, 0), r(4, 0), 4)
            link(nc.vector.tensor_copy(AP[:, A_CHUNK(1, 0):A_CHUNK(1, 0) + 2, :], AP[:, r(8, 0):r(8, 0) + 2, :]))
            r = A_CHUNK
            cmul(r(2, 0), r(1, 0), r(1, 0), 1)
            cmul(r(3, 0), r(1, 0), r(2, 0), 2)
            cmul(r(5, 0), r(1, 0), r(4, 0), 4)
            for k in range(3):
                cmul(A_BLOCK(k + 1, 0), A_BLOCK(k, 0), A_BLOCK(k, 0), 1)
            nc.vector.tensor_copy(Q1[:, 0, 0:1], AP[:, NPOW - 1, 0:1]).then_inc(s_pow, 1)

            def split_lo(count, xt, m, gain):
                dve.wait_ge(s_xh, count + 1)
                stt(tile(XL, m), xt, gain, tile(XH, m).bitcast(F32), ALU.mult, ALU.subtract).then_inc(s_xl, 1)

            dve.wait_ge(s_md, M_X)
            for m in range(DT):
                split_lo(m, tile(XT, m), m, KV[:, K_MIX + m:K_MIX + m + 1])

            def recip(count):
                dve.wait_ge(s_rt, count)
                link(nc.vector.reciprocal(RS[:, :], RS[:, :]))

            def scaled(n, o, wait_n=None):
                dve.wait_ge(s_po, (n if wait_n is None else wait_n) + 1)
                tt(v3(o), set3(n), v3(RS[:, :]), ALU.mult).then_inc(s_ev, 1)

            def evict_u(q):
                n = n_u(q)
                dve.wait_ge(s_po, n + 1)
                if q >= 2:
                    dve.wait_ge(s_us[q - 2], 32)
                if q == 1:
                    dve.wait_ge(s_acc, DT)
                tt(US[:, q, :], PS[:, 3 * (n % 2) + 2, TN - NB:TN], RS[:, SEQ:T], ALU.mult)
                o = (TA, TBf)[q % 2][:, :].rearrange("p (i c d) -> p c d i", i=CH, c=NCH)
                i0 = set3(n).rearrange("p c (d i) -> p c d i", i=CH)
                i1 = v3(RS[:, :]).rearrange("p c (d i) -> p c d i", i=CH)
                last = None
                for c in range(NCH):
                    last = tt(o[:, c], i0[:, c], i1[:, c], ALU.mult)
                last.then_inc(s_ev, 2 if q == 0 else 1)

            recip(1)
            evict_u(0)
            dve.wait_ge(s_mf, M_W1)
            dve.wait_ge(s_bn, 32)
            cf = [APT[:, COEF + c, :].unsqueeze(2).to_broadcast([P, NJ, HG]) for c in range(2)]
            mt = MT[:, 0:NJ * HG].rearrange("p (j h) -> p j h", h=HG)
            link(tt(BB[:, 0], BN[:, 0], cf[0], ALU.mult))
            link(tt(mt, BN[:, 1], cf[1], ALU.mult))
            link(tt(BB[:, 0], BB[:, 0], mt, ALU.subtract))
            link(tt(BB[:, 1], BN[:, 1], cf[0], ALU.mult))
            link(tt(mt, BN[:, 0], cf[1], ALU.mult))
            link(tt(BB[:, 1], BB[:, 1], mt, ALU.add))

            def power_rows(o, v, n, sign):
                w = [APT[:, 0:2 * n, :].rearrange("p (k c) j -> p c j k", c=2)[:, c].unsqueeze(3).to_broadcast([P, NJ, n, HG])
                     for c in range(2)]
                x = [v[:, c].unsqueeze(2).to_broadcast([P, NJ, n, HG]) for c in range(2)]
                m4 = MT[:, 0:NJ * n * HG].rearrange("p (j k h) -> p j k h", j=NJ, k=n)
                o4 = [o[:, c].rearrange("p j (k h) -> p j k h", k=n) for c in range(2)]
                link(tt(o4[0], x[0], w[0], ALU.mult))
                link(tt(m4, x[1], w[1], ALU.mult))
                link(tt(o4[0], o4[0], m4, ALU.subtract))
                link(tt(o4[1], x[1], w[0], ALU.mult))
                link(tt(m4, x[0], w[1], ALU.mult))
                if sign > 0:
                    return tt(o4[1], o4[1], m4, ALU.add)
                return stt(o[:, 1].rearrange("p j n -> p (j n)"), o[:, 1].rearrange("p j n -> p (j n)"), -1.0,
                           MT[:, 0:NJ * n * HG], ALU.mult, ALU.subtract)

            power_rows(W1T, BB, CH, 1).then_inc(s_w1t, 1)
            evict_u(1)
            power_rows(W2, CTT, CH + 1, -1).then_inc(s_w2, 1)
            evict_u(2)
            evict_u(3)

            def scan(q):
                dve.wait_ge(s_mf, M_V + 8 * q + 4)
                js = slice(4 * q, 4 * q + 4)
                blk = S[:, :, :, NB + 1:NB + 1 + NC].rearrange("p c j (b i) -> p c j b i", i=CH)

                def cmac(dst, src, pw, n, shp):
                    view = (lambda x: x.rearrange("p (a b) -> p a b", a=shp[0])) if len(shp) == 2 else \
                        (lambda x: x.rearrange("p (a b c) -> p a b c", a=shp[0], b=shp[1]))
                    if 2 * n <= 480:
                        t1, t2, t3, t4 = (view(x) for x in (ST1[:, 0:n], ST1[:, n:2 * n], ST2[:, 0:n], ST2[:, n:2 * n]))
                        tt(t1, src[0], pw[0], ALU.mult)
                        tt(t2, src[1], pw[1], ALU.mult)
                        tt(t3, src[1], pw[0], ALU.mult)
                        link(tt(t4, src[0], pw[1], ALU.mult))
                        tt(dst[0], dst[0], t1, ALU.add)
                        link(tt(dst[1], dst[1], t3, ALU.add))
                        tt(dst[0], dst[0], t2, ALU.subtract)
                        link(tt(dst[1], dst[1], t4, ALU.add))
                    else:
                        t1, t2 = view(ST1[:, 0:n]), view(ST2[:, 0:n])
                        tt(t1, src[0], pw[0], ALU.mult)
                        link(tt(t2, src[1], pw[1], ALU.mult))
                        link(tt(dst[0], dst[0], t1, ALU.add))
                        link(tt(dst[0], dst[0], t2, ALU.subtract))
                        tt(t1, src[1], pw[0], ALU.mult)
                        link(tt(t2, src[0], pw[1], ALU.mult))
                        link(tt(dst[1], dst[1], t1, ALU.add))
                        link(tt(dst[1], dst[1], t2, ALU.add))

                def pws(row, w):
                    return [APT[:, row + c, js].unsqueeze(2).to_broadcast([P, 4, w]) for c in range(2)]

                for i in range(1, CH):
                    cmac([blk[:, c, :, :, i] for c in range(2)], [blk[:, c, :, :, i - 1] for c in range(2)],
                         pws(A_POW(CH, 0), NBLK), 4 * NBLK, [4, NBLK])
                for lv in range(4):
                    d = 1 << lv
                    w = NBLK - d
                    cmac([blk[:, c, :, d:, CH - 1] for c in range(2)], [blk[:, c, :, 0:w, CH - 1] for c in range(2)],
                         pws(A_BLOCK(lv, 0), w), 4 * w, [4, w])
                shp = [P, 4, NBLK - 1, CH - 1]
                pw = [APT[:, A_CHUNK(1, 0):A_CHUNK(CH, 0), js].rearrange("p (i c) j -> p c j i", c=2)[:, c]
                      .unsqueeze(2).to_broadcast(shp) for c in range(2)]
                cmac([blk[:, c, :, 1:, 0:CH - 1] for c in range(2)],
                     [blk[:, c, :, 0:NBLK - 1, CH - 1].unsqueeze(3).to_broadcast(shp) for c in range(2)],
                     pw, 4 * (NBLK - 1) * (CH - 1), shp[1:])
                s0 = [S0[:, c, js, :] for c in range(2)]
                cmac([S[:, c, :, SW - NB:SW] for c in range(2)], s0, pws(A_POW(1, 0), NB), 4 * NB, [4, NB])
                for c in range(2):
                    nc.vector.tensor_copy(FS[:, c, js, :], S[:, c, :, SW - NB - 1:SW])
                nc.vector.tensor_copy(S[:, 0, :, 0:NB], s0[0])
                nc.vector.tensor_copy(S[:, 1, :, 0:NB], s0[1]).then_inc(s_scan, 1)

            def conv(o, x, t, kw, tiles, col):
                def w(k):
                    c = col + kw + k * tiles
                    return KV[:, c:c + 1] if isinstance(c, int) else KV[:, bass.ds(c, 1)]
                st = CB[:, t, :] if isinstance(t, int) else CB[:, bass.ds(t, 1), :].rearrange("p t n -> p (t n)")
                st = st.rearrange("p (b k) -> p k b", k=2)
                stt(o[:, SEQ:T], st[:, 1], w(1), o[:, SEQ:T], ALU.mult, ALU.add)
                link(stt(o[:, 1:SEQ], x[:, 0:SEQ - 1], w(1), o[:, 1:SEQ], ALU.mult, ALU.add))
                stt(o[:, SEQ:T], st[:, 0], w(0), o[:, SEQ:T], ALU.mult, ALU.add)
                return stt(o[:, 2:SEQ], x[:, 0:SEQ - 2], w(0), o[:, 2:SEQ], ALU.mult, ALU.add)

            dve.wait_ge(s_us[2], 32)
            dve.wait_ge(s_us[3], 32)
            for q in range(CT):
                n = N_P2 + 3 * q
                if q:
                    dve.wait_ge(s_vl, q)
                scaled(n, TA[:, :])
                scan(q)
                scaled(n + 1, TBf[:, :])
                dve.wait_ge(s_ev, n + 2)
                tt(TBf[:, :], TBf[:, :], TA[:, :], ALU.mult).then_inc(s_ci, 1)
                dve.wait_ge(s_ci, q + 1)
                nc.vector.tensor_copy(LAST[:, q, :], TBf[:, SEQ - 2:T])
                dve.wait_ge(s_cb, q + 1)
                link(conv(TA, TBf, q, q, CT, K_CAW))
                scaled(n + 2, TBf[:, :])
                dve.wait_ge(s_ev, n + 3)
                tt(TA[:, :], TA[:, :], TBf[:, :], ALU.mult).then_inc(s_va, 1)
                dve.wait_ge(s_va, q + 1)
                dve.wait_ge(s_vh, q + 1)
                tt(tile(VAL, q), TA[:, :], tile(VAH, q).bitcast(F32), ALU.subtract).then_inc(s_vl, 1)
            dve.wait_ge(s_vl, CT)
            nc.vector.tensor_copy(SSC[:, 0:1], EP[:, :]).then_inc(s_yl2, 1)
            with dve.Fori(0, 4) as i:
                for j in range(2):
                    n = N_P3 + 2 * j
                    scaled(n, tile(TF, i * 2 + j), i * 4 + n)
                    if j == 0:
                        dve.wait_ge(s_yl, i * 272 + 272)
                        tt_y = stt(TA[:, :], TBf[:, :], KV[:, bass.ds(i + K_DSK, 1)], TA[:, :], ALU.mult, ALU.add)
                        tt_y.then_inc(s_y, 1)
                    dve.wait_ge(s_sa, i * 2 + (j + 1))
                    dve.wait_ge(s_po, i * 4 + (n + 2))
                    tt(v3(tile(TF, i * 2 + j)), set3(n + 1), v3(tile(TF, i * 2 + j)), ALU.mult).then_inc(s_ev, 1)
                dve.wait_ge(s_yg, i * 3 + 3)
                tt(tile(YGL, i), TC[:, :], tile(YGH, i).bitcast(F32), ALU.subtract).then_inc(s_yl2, 1)
            dve.wait_ge(s_yl2, CT + 1)
            nc.vector.tensor_copy(SSC[:, 0:1], EP[:, :]).then_inc(s_tf, 1)
            nc.vector.tensor_copy(SSC[:, 1:2], EP[:, :]).then_inc(s_tl, 1)
            with dve.Fori(0, 4) as i:
                own.enter(i, 2)
                for j in range(2):
                    n = N_P4 + 3 * j
                    m = i * 2 + j
                    dve.wait_ge(s_tl, i * 2 + (j + 1))
                    scaled(n, TA[:, :], i * 6 + n)
                    dve.wait_ge(s_ev, i * 6 + (n + 2))
                    dve.wait_ge(s_po, i * 6 + (n + 3))
                    tt(v3(TBf[:, :]), set3(n + 2), v3(TBf[:, :]), ALU.mult).then_inc(s_ev, 1)
                    dve.wait_ge(s_ev, i * 6 + (n + 3))
                    dve.wait_ge(s_sg, i * 2 + (j + 1))
                    link(tt(TA[:, :], TA[:, :], TBf[:, :], ALU.mult))
                    tt(TA[:, :], TA[:, :], tile(TF, m), ALU.add).then_inc(s_tf, 1)
                    dve.wait_ge(s_th, i * 2 + (j + 1))
                    tt(tile(TL, m), TA[:, :], tile(TH, m).bitcast(F32), ALU.subtract).then_inc(s_tl, 1)
                own.leave(4)
            with dve.Fori(0, 4) as i:
                for j in range(2):
                    n = N_P5 + j
                    m = i * 2 + j
                    dve.wait_ge(s_xr[j], i * 16 + 16)
                    dve.wait_ge(s_po, i * 2 + (n + 1))
                    tt(v3(tile(XT, m)), set3(n), v3((TA, TBf)[j][:, :]), ALU.add).then_inc(s_ev, 1)
                    split_lo(i * 2 + (DT + j), tile(XT, m), m, KV[:, bass.ds(m + K_FFN, 1)])
            recip(2)

            def up_a(f, n, wait_n, both=1):
                dve.wait_ge(s_po, wait_n + 1)
                if not isinstance(f, int) or f:
                    dve.wait_ge(s_fc, f)
                tt(v3(TA[:, :]), set3(n), v3(RS[:, :]), ALU.mult).then_inc(s_ev, both)
                dve.wait_ge(s_ev, wait_n + both)
                nc.vector.tensor_copy(LAST[:, bass.ds(f + CT, 1), :].rearrange("p t n -> p (t n)"),
                                      TA[:, SEQ - 2:T]).then_inc(s_fi, 1)
                dve.wait_ge(s_fb, f + 1)
                conv(TBf, TA, f + CT, f, FT, K_FW).then_inc(s_fc, 1)

            def up_b(f, j, n, wait_n):
                dve.wait_ge(s_gl, f + 1)
                scaled(n, TC[:, :], wait_n)
                dve.wait_ge(s_ev, wait_n + 1)
                dve.wait_ge(s_ge, f + 1)
                tt(TC[:, :], TC[:, :], TBf[:, :], ALU.mult).then_inc(s_g, 1)
                dve.wait_ge(s_gh, f + 1)
                tt(tile(GL, j), TC[:, :], tile(GH, j).bitcast(F32), ALU.subtract).then_inc(s_gl, 1)

            def down(n, wait_n):
                for m in range(DT):
                    dve.wait_ge(s_po, wait_n + (m + 1))
                    xm = v3(tile(XT, m))
                    tt(xm, set3(n + m), xm, ALU.add).then_inc(s_ev, 1)

            dve.wait_ge(s_acc, 2 * DT)
            nc.vector.tensor_copy(SSC[:, 2:3], EP[:, :]).then_inc(s_gl, 1)
            up_a(0, N_A0, N_A0, 2)
            for k in range(5):
                dve.wait_ge(s_ph, k + 1)
                if k < 4:
                    kk, h = divmod(k, 2)
                    w = slice(kk * T + 512 * h, kk * T + 512 * (h + 1))
                    tt(PL[:, w], bank(M_PT + k)[:, :], PH[:, w].bitcast(F32), ALU.subtract).then_inc(s_mf, 1)
                else:
                    w3 = lambda t: t.rearrange("p (k t) -> p k t", t=T)[:, :, SEQ:T]
                    tt(w3(PL[:, :]), bank(M_PT + k)[:, 0:2 * NB].rearrange("p (k t) -> p k t", t=NB),
                       w3(PH[:, :].bitcast(F32)), ALU.subtract).then_inc(s_mf, 1)
            with dve.Fori(0, FP - 1) as p:
                own.enter(p, 2)
                nb = p * 12 + N_P6
                up_b(p * 2, 0, N_P6, nb)
                up_a(p * 2 + 1, N_P6 + 1, nb + 1)
                up_b(p * 2 + 1, 1, N_P6 + 2, nb + 2)
                up_a(p * 2 + 2, N_P6 + 3, nb + 3)
                down(N_P6 + 4, nb + 4)
                own.leave(FP - 1)
            up_b(FT - 2, 0, N_END, N_END)
            up_a(FT - 1, N_END + 1, N_END + 1)
            up_b(FT - 1, 1, N_END + 2, N_END + 2)
            for m in range(DT):
                n = N_DOWN_END + m
                dve.wait_ge(s_po, n + 1)
                xm = v3(tile(XT, m))
                tt(xm, set3(n), xm, ALU.add).then_inc(s_ev, 1)
                split_lo(2 * DT + m, tile(XT, m), m, KV[:, K_PLE + m:K_PLE + m + 1])
            recip(3)

            def ple(m, n_g, n_p, wg, wp, both=1):
                dve.wait_ge(s_po, wg + 1)
                tt(v3(TA[:, :]), set3(n_g), v3(RS[:, :]), ALU.mult).then_inc(s_ev, both)
                dve.wait_ge(s_sp, m + 1)
                dve.wait_ge(s_po, wp + 1)
                if not isinstance(m, int) or m:
                    dve.wait_ge(s_xo, m)
                tt(v3(TBf[:, :]), set3(n_p), v3(TA[:, :]), ALU.mult).then_inc(s_ev, 1)
                dve.wait_ge(s_ev, wp + 1)
                tt(tile(XT, m), tile(XT, m), TBf[:, :], ALU.add).then_inc(s_xo, 1)

            ple(0, N_P7, N_PW0, N_P7, N_PW0, 2)
            ple(1, N_G1, N_G1 + 1, N_G1, N_G1 + 1)
            with dve.Fori(0, 3) as i:
                for j in range(2):
                    n = N_P7L + 2 * j
                    ple(i * 2 + (2 + j), n, n + 1, i * 4 + n, i * 4 + (n + 1))
            dve.wait_ge(s_gf, 16)
            for t in range(DT + 1):
                n = N_P8 + t
                w = P if t < DT else NB
                o = PS[0:w, 3 * (n % 2):3 * (n % 2) + 2, :].rearrange("p a b -> p (a b)")
                dve.wait_ge(s_ss, t + 1)
                if t >= 3:
                    dve.wait_ge(s_or[t % 3], 16 * (t // 3))
                link(nc.vector.reciprocal(SSC[0:w, 2 + t % 2:3 + t % 2], SSC[0:w, 2 + t % 2:3 + t % 2]))
                stt(OUTT[t % 3][0:w, :], o, SSC[0:w, 2 + t % 2:3 + t % 2], GF[0:w, :], ALU.mult, ALU.mult).then_inc(s_ev, 1)

        @block.tensor
        def _(pe):
            mm, tr = nc.tensor.matmul, nc.tensor.transpose

            def product(n, wait_n, slot_off, ks, xh, xl, ready=None, wh=WH, wl=WL):
                if not isinstance(wait_n, int) or wait_n >= 2:
                    pe.wait_ge(s_ev, wait_n - 1)
                last = None
                for k in range(ks):
                    if ready is not None:
                        ready(k)
                    w = slice(slot_off + k * P, slot_off + (k + 1) * P)
                    for r, (ww, xx) in enumerate(((wh, xh), (wh, xl), (wl, xh))):
                        for c in range(NCH):
                            cols = slice(k * T + c * TN, k * T + (c + 1) * TN)
                            last = mm(PS[:, 3 * (n % 2) + c, 0:TN], ww[:, w], xx[:, cols],
                                      start=(k == 0 and r == 0), stop=(k == ks - 1 and r == 2))
                last.then_inc(s_po, 1)

            def group(g):
                pe.wait_ge(s_wl, g + 1)

            def misc(k):
                if k >= 2:
                    pe.wait_ge(s_mf, k - 1)
                return bank(k)

            def sum_squares(n, wait_n, tiles):
                pe.wait_ge(s_ev, wait_n - 1) if wait_n >= 2 else None
                pe.wait_ge(s_acc, tiles)
                last = None
                for c in range(NCH):
                    last = mm(PS[:, 3 * (n % 2) + c, 0:TN], ONES[:, :], RS[:, c * TN:(c + 1) * TN], start=True, stop=True)
                last.then_inc(s_po, 1)

            pe.wait_ge(s_idn, 4)
            pe.wait_ge(s_nat, 16 * (8 + 4 + 32))
            b = misc(M_VEC)
            tr(b[:, 0:NK1], VA1[:, :], IDN[0:NK1, 0:NK1])
            tr(b[:, NK1:NK1 + NK2], VA2[:, :], IDN[0:NK2, 0:NK2]).then_inc(s_md, 1)
            b = misc(M_CB)
            for t in range(CT + FT):
                last = tr(b[:, 16 * t:16 * (t + 1)], CBN[:, t * P:(t + 1) * P], IDN[0:16, 0:16])
            last.then_inc(s_md, 1)
            b = misc(M_S0)
            for c in range(2):
                for j in range(NJ):
                    o = (c * NJ + j) * NB
                    last = tr(b[:, o:o + NB], S0N[:, c, j * P:(j + 1) * P], IDN[0:NB, 0:NB])
            last.then_inc(s_md, 1)
            b = misc(M_CT)
            for c in range(2):
                for half in range(2):
                    last = tr(b[:, (2 * c + half) * P:(2 * c + half + 1) * P], CN[:, c, half, :], IDN[:, :])
            last.then_inc(s_md, 1)
            for t in range(DT + 1):
                w = P if t < DT else NB
                if t % 2 == 0:
                    pe.wait_ge(s_x[t // 2], 16)
                for half in range(2):
                    b = misc(M_X + 2 * t + half)
                    for m in range(4):
                        f = slice((4 * half + m) * P, (4 * half + m + 1) * P)
                        src = XN[:, t, f] if t < DT else XS[:, f]
                        last = tr(b[:, m * P:m * P + w], src, IDN[0:w, 0:w])
                    last.then_inc(s_md, 1)
            group(0)
            product(n_u(0), n_u(0), 0, DT, XH, XL, lambda k: pe.wait_ge(s_xl, k + 1))
            sum_squares(N_NORM1, 0, DT)
            pe.wait_ge(s_pow, 1)
            for s, (r0, r1) in enumerate(((0, 32), (32, NPOW))):
                b = misc(M_AP + s)
                for r in range(r0, r1):
                    last = tr(b[:, (r - r0) * NJ:(r - r0 + 1) * NJ], AP[:, r, :], IDN[0:NJ, 0:NJ])
                last.then_inc(s_md, 1)
            for q in (1, 2):
                group(q)
                product(n_u(q), n_u(q), (q % 2) * D, DT, XH, XL)
            pe.wait_ge(s_w1t, 1)
            for s in range(8):
                b = misc(M_W1 + s)
                for j in range(4):
                    c, jj = divmod(4 * s + j, NJ)
                    last = tr(b[:, j * P:(j + 1) * P], W1T[:, c, jj, :], IDN[:, :])
                last.then_inc(s_md, 1)
            group(3)
            product(n_u(3), n_u(3), D, DT, XH, XL)
            pe.wait_ge(s_w2, 1)
            for s in range(8):
                b = misc(M_G + s)
                two = s % 2
                rows = slice(two * NS, two * NS + NS)
                for idx in range(4):
                    j = 4 * (s // 2) + idx
                    for c in range(2):
                        last = mm(b[0:HG, idx * P:(idx + 1) * P], BB[rows, c, j, :], W2[rows, c, j, 0:P],
                                  start=(c == 0), stop=(c == 1))
                last.then_inc(s_md, 1)

            def inputs_to_states(q):
                pe.wait_ge(s_ul[q], 160)
                for j in range(4):
                    b = misc(M_V + 8 * q + j)
                    for two in range(2):
                        for c in range(2):
                            last = mm(b[two * NS:(two + 1) * NS, c * UC:(c + 1) * UC],
                                      W1[:, c, 4 * q + j, two * NS:(two + 1) * NS], U[:, 2 * j + two, NB:UW],
                                      start=True, stop=True)
                    last.then_inc(s_md, 1)

            def outputs(q):
                pe.wait_ge(s_scan, q + 1)
                for s, gs in enumerate(((0, 2, 4), (1, 3, 5), (6,), (7,))):
                    b = misc(M_V + 8 * q + 4 + s)
                    for idx, gl in enumerate(gs):
                        rows = slice((gl % 2) * NS, (gl % 2) * NS + NS)
                        o = b[:, idx * UC:(idx + 1) * UC]
                        for c in range(2):
                            mm(o, W2[rows, c, 4 * q + gl // 2, HG:HG + P], S[rows, c, gl // 2, 0:UC],
                               start=(c == 0), stop=False)
                        last = mm(o, TO[:, 8 * q + gl, :], U[:, gl, 0:UC], start=False, stop=True)
                    last.then_inc(s_md, 1)

            for q in range(CT):
                for part in range(3):
                    g, n = G_P2 + 3 * q + part, N_P2 + 3 * q + part
                    group(g)
                    product(n, n, (g % 2) * D, DT, XH, XL)
                    if part == 0:
                        if q == 0:
                            for h in range(2):
                                pe.wait_ge(s_to[h], 16 * CH)
                        else:
                            pass
                        inputs_to_states(q)
                outputs(q)
            with pe.Fori(0, 4) as i:
                for j in range(2):
                    n, g = N_P3 + 2 * j, G_P3 + 2 * j
                    group(i * 4 + g)
                    product(n, i * 4 + n, 0, DT, XH, XL)
                    group(i * 4 + (g + 1))
                    product(n + 1, i * 4 + (n + 1), D, CT, VAH, VAL, lambda k: pe.wait_ge(s_vl, k + 1))
            with pe.Fori(0, 4) as i:
                for j in range(2):
                    n, g = N_P4 + 3 * j, G_P4 + 2 * j
                    group(i * 4 + g)
                    product(n, i * 6 + n, 0, DT, XH, XL)
                    group(i * 4 + (g + 1))
                    product(n + 1, i * 6 + (n + 1), D, CT, YGH, YGL, lambda k: pe.wait_ge(s_yl2, k + 2))
                    product(n + 2, i * 6 + (n + 2), D + CT * P, CT, YGH, YGL)
            with pe.Fori(0, 4) as i:
                for j in range(2):
                    group(i * 2 + (G_P5 + j))
                    product(N_P5 + j, i * 2 + (N_P5 + j), j * D, DT, TH, TL, lambda k: pe.wait_ge(s_tl, k + 2))
            group(G_A0)
            product(N_A0, N_A0, 0, DT, XH, XL, lambda k: pe.wait_ge(s_xl, DT + k + 1))
            sum_squares(N_NORM2, N_NORM2, 2 * DT)
            pe.wait_ge(s_p, 32)
            for kk in range(PT):
                for h in range(2):
                    b = misc(M_PT + 2 * kk + h)
                    for t in range(4):
                        last = tr(b[:, t * P:(t + 1) * P], PST[:, 4 * h + t, kk * P:(kk + 1) * P], IDN[:, :])
                    last.then_inc(s_md, 1)
            b = misc(M_PT + 4)
            for kk in range(PT):
                last = tr(b[:, kk * NB:(kk + 1) * NB], PSS[:, kk * P:(kk + 1) * P], IDN[0:NB, 0:NB])
            last.then_inc(s_md, 1)

            def down(n, wait_n, p):
                pe.wait_ge(s_dl, p + 1)
                pe.wait_ge(s_gl, p * 2 + 3)
                for m in range(DT):
                    down_out(n + m, wait_n + m, m, GH, GL)

            def down_out(n, wait_n, m, xh, xl):
                pe.wait_ge(s_ev, wait_n - 1)
                last = None
                for k in range(2):
                    w = slice(k * D + m * P, k * D + (m + 1) * P)
                    for r, (ww, xx) in enumerate(((DHW, xh), (DHW, xl), (DLW, xh))):
                        for c in range(NCH):
                            last = mm(PS[:, 3 * (n % 2) + c, 0:TN], ww[:, w], xx[:, k * T + c * TN:k * T + (c + 1) * TN],
                                      start=(k == 0 and r == 0), stop=(k == 1 and r == 2))
                last.then_inc(s_po, 1)

            with pe.Fori(0, FP - 1) as p:
                for j in range(4):
                    group(p * 4 + (G_P6 + j))
                    product(N_P6 + j, p * 12 + (N_P6 + j), ((G_P6 + j) % 2) * D, DT, XH, XL)
                down(N_P6 + 4, p * 12 + (N_P6 + 4), p)
            for j in range(3):
                group(G_END + j)
                product(N_END + j, N_END + j, ((G_END + j) % 2) * D, DT, XH, XL)
            down(N_DOWN_END, N_DOWN_END, FP - 1)
            group(G_P7)
            product(N_P7, N_P7, 0, DT, XH, XL, lambda k: pe.wait_ge(s_xl, 2 * DT + k + 1))
            sum_squares(N_NORM3, N_NORM3, 3 * DT)
            pe.wait_ge(s_dl, FP + 1)
            pe.wait_ge(s_mf, M_PT + 5)
            down_out(N_PW0, N_PW0, 0, PH, PL)
            group(G_P7 + 1)
            product(N_G1, N_G1, D, DT, XH, XL)
            down_out(N_G1 + 1, N_G1 + 1, 1, PH, PL)
            for k in range(7):
                b = misc(M_OUT + k)
                for t in range(4 * k, min(4 * k + 4, CT + FT)):
                    last = tr(b[0:NB + 2, (t - 4 * k) * P:(t - 4 * k + 1) * P], LAST[:, t, :], IDN[:, :])
                last.then_inc(s_md, 1)
            for k in range(8):
                b = misc(M_OUT + 7 + k)
                for r in range(4):
                    c, j = divmod(4 * k + r, NJ)
                    last = tr(b[0:NB + 1, r * P:(r + 1) * P], FS[:, c, j, :], IDN[:, :])
                last.then_inc(s_md, 1)
            for m in range(2, DT):
                n = N_P7L + 2 * (m - 2)
                group(G_P7 + m)
                product(n, n, (m % 2) * D, DT, XH, XL)
                down_out(n + 1, n + 1, m, PH, PL)
            pe.wait_ge(s_xo, DT)
            for t in range(DT + 1):
                n = N_P8 + t
                w = P if t < DT else NB
                pe.wait_ge(s_ev, n - 1)
                for m in range(DT):
                    last = tr(PS[0:w, 3 * (n % 2) + m // 4, (m % 4) * P:(m % 4 + 1) * P],
                              XT[:, m * T + t * P:m * T + t * P + w], IDN[:, :])
                last.then_inc(s_po, 1)


_INS = ["x_prompt", "x_sample", "p_prompt", "p_sample", "state_conv_a", "state_ssm_re", "state_ssm_im",
        "state_ffn_conv", "norm_mix", "w_in", "conv_a_w", "conv_a_b", "w_out_a", "log_dt", "lam_re", "lam_im",
        "b_re", "b_im", "c_re", "c_im", "d_skip", "w_glu_a", "w_glu_b", "w_o", "norm_ffn", "w_up",
        "ffn_conv_w", "ffn_conv_b", "w_down", "norm_ple", "w_ple_gate", "w_ple", "norm_final"]
_OUTS = [("y_prompt", (1, SEQ, D)), ("y_sample", (NB, 1, D)),
         ("conv_a_p", (1, 1, 2, CA)), ("ssm_re_p", (1, 1, G, NS)), ("ssm_im_p", (1, 1, G, NS)),
         ("ffn_p", (1, 1, 2, FF)),
         ("conv_a_s", (1, NB, 2, CA)), ("ssm_re_s", (1, NB, G, NS)), ("ssm_im_s", (1, NB, G, NS)),
         ("ffn_s", (1, NB, 2, FF))]


def kernel(**inputs):
    import numpy as np
    import concourse.bacc as bacc
    from concourse.bass_utils import run_bass_kernel_spmd

    nc = bacc.Bacc("TRN2", target_bir_lowering=False, num_devices=1)
    arrays, ins, outs = {}, {}, {}
    for name in _INS:
        arr = np.ascontiguousarray(inputs[name])
        arrays["in_" + name] = arr
        ins[name] = nc.dram_tensor("in_" + name, arr.shape, F32, kind="ExternalInput").ap()
    for name, shape in _OUTS:
        outs[name] = nc.dram_tensor("out_" + name, shape, F32, kind="ExternalOutput").ap()
    decoder_step(nc, ins, outs)
    r = run_bass_kernel_spmd(nc, [arrays], core_ids=[0])
    return tuple(r.results[0]["out_" + name] for name, _ in _OUTS)
```

```python
import math
from contextlib import ExitStack

import concourse.bass as bass
from concourse import mybir

F32 = mybir.dt.float32
F32R = mybir.dt.float32r
I32 = mybir.dt.int32
ALU = mybir.AluOpType
ACT = mybir.ActivationFunctionType

P = 128
D = 1024
SEQ = 1024
NB = 8
T = SEQ + NB
NCH = 3
TN = T // NCH
DT = D // P
CA = D // 2
CT = CA // P
FF = 2816
FT = FF // P
FP = FT // 2
PLE = 256
PT = PLE // P
G = 32
NJ = G // 2
HG = 16
NS = 64
CH = 8
NC = SEQ // CH
NBLK = NC // CH
UC = NC + NB
UW = NC + 2 * NB
SW = NB + 1 + NC + NB
EPS = 1e-6

def A_POW(k, c):
    return 2 * k + c
def A_CHUNK(i, c):
    return 2 * (CH + 1) + 2 * (i - 1) + c
def A_BLOCK(r, c):
    return A_CHUNK(CH, c) if r == 0 else 34 + 2 * (r - 1) + c
COEF = 40
NPOW = 42

K_MIX, K_FFN, K_PLE, K_CAW, K_CAB, K_DSK, K_FW, K_FB = 0, 8, 16, 24, 36, 40, 44, 110
NK1, NK2 = 44, 88

IN_H, IN_B, IN_C, IN_U, IN_GA, IN_GS = 0, 4, 8, 12, 16, 24

N_U, N_P2, G_P2 = 0, 4, 4
N_P3, G_P3 = 16, 16
N_P4, G_P4 = 32, 32
N_P5, G_P5 = 56, 48
N_A0, G_A0 = 64, 56
N_P6, G_P6 = 65, 57
N_END, G_END = N_P6 + 12 * (FP - 1), G_P6 + 4 * (FP - 1)
N_DOWN_END = N_END + 3
N_P7, G_P7 = N_DOWN_END + DT, G_END + 3
N_PW0, N_G1 = N_P7 + 1, N_P7 + 2
N_P7L, G_P7L = N_P7 + 4, G_P7 + 2
N_P8 = N_P7L + 12

M_VEC, M_CB, M_S0, M_CT, M_X = 0, 1, 2, 3, 4
M_AP = M_X + 18
M_W1 = M_AP + 2
M_G = M_W1 + 8
M_V = M_G + 8
M_PT = M_V + 32
M_OUT = M_PT + 5


def _stage_count(g, i=None, per_trip=0):
    if g % 2 == 0 or g < G_P4:
        n, each = 16 * (g // 2 + 1), 16
    elif g < G_P5:
        n, each = 16 * (G_P4 // 2) + 32 * ((g - G_P4) // 2 + 1), 32
    else:
        n, each = 16 * (G_P4 // 2) + 32 * DT + 16 * ((g - G_P5) // 2 + 1), 16
    return n if i is None else n + i * (each * per_trip // 2)


class _Steps:

    def __init__(self, eng, sem):
        self.eng, self.sem, self.n, self.i, self.per = eng, sem, 0, None, 0

    def link(self, ins):
        ins.then_inc(self.sem, 1)
        self.n += 1
        self.eng.wait_ge(self.sem, self.n if self.i is None else self.i * self.per + self.n)

    def enter(self, i, per):
        self.i, self.per, self.start = i, per, self.n

    def leave(self, trips):
        assert self.n - self.start == self.per, (self.n - self.start, self.per)
        self.n = self.start + trips * self.per
        self.i = None


def decoder_step(nc, a, out):
    ctx = ExitStack()
    with ctx:
        def sem(name):
            return ctx.enter_context(nc.semaphore(name))

        base = (nc.sbuf_base + 31) // 32 * 32
        TB4 = 4 * T
        A0 = base
        B0 = A0 + 16 * TB4
        C0 = B0 + 8 * TB4
        D0 = C0 + 8 * TB4
        E0 = D0 + 8 * TB4

        def at(name, shape, off, dt=F32):
            return nc.alloc_sbuf_tensor_at(name, shape, dt, offset=off)

        XH = at("XH", [P, DT * T], A0, F32R)
        XL = at("XL", [P, DT * T], A0 + 8 * TB4, F32R)
        XLo = A0 + 8 * TB4
        VA1 = at("VEC1", [NK1, P], XLo)
        VA2 = at("VEC2", [NK2, P], XLo + 512)
        CN = at("CN", [P, 2, 2, P], XLo + 1024)
        CBN = at("CBN", [2 * NB, CA + FF], XLo + 3072)
        S0N = at("S0N", [NB, 2, NJ * P], XLo + 3072 + 4 * (CA + FF))
        OUTT = [at(f"OUTT{i}", [P, D], A0 + 4096 * i) for i in range(3)]
        GF = at("GF", [P, D], A0 + 3 * 4096)
        XN = at("XN", [P, DT, D], B0)
        W1T = at("W1T", [P, 2, NJ, CH * HG], B0)
        MT = at("MT", [P, NJ * (CH + 1) * HG], B0 + 16384)
        BB = at("BB", [P, 2, NJ, HG], B0 + 16384 + 9216)
        VAH = at("VAH", [P, CT * T], B0, F32R)
        VAL = at("VAL", [P, CT * T], B0 + CT * TB4, F32R)
        TL = at("TL", [P, DT * T], B0, F32R)
        GH = at("GH", [P, 2 * T], B0, F32R)
        GL = at("GL", [P, 2 * T], B0 + 2 * TB4, F32R)
        PH = at("PH", [P, PT * T], B0 + 4 * TB4, F32R)
        PL = at("PL", [P, PT * T], B0 + 6 * TB4, F32R)
        SST = at("SST", [NB + 1, 2 * NJ * P], B0)
        AP = at("AP", [NJ, NPOW, P], C0)
        tiny0 = C0 + NPOW * 512
        LAM = at("LAM", [NJ, 2, P], tiny0)
        LDT = at("LDT", [NJ, 2], tiny0 + 1024)
        DTM = at("DTM", [NJ, 2], tiny0 + 1056)
        E1 = at("E1", [NJ, P], tiny0 + 1088)
        E2 = at("E2", [NJ, P], tiny0 + 1600)
        E3 = at("E3", [NJ, P], tiny0 + 2112)
        EI = at("EI", [NJ, P], tiny0 + 2624, I32)
        KF = at("KF", [NJ, 2, P], tiny0 + 3136)
        CS = at("CS", [NJ, 2, P], tiny0 + 4160)
        Q1 = at("Q1", [NJ, 4, P], tiny0 + 5184)
        Q2 = at("Q2", [NJ, 4, P], tiny0 + 7232)
        W1 = at("W1", [P, 2, NJ, P], C0)
        TO = at("TO", [P, G, P], C0 + 16384)
        TF = at("TF", [P, DT * T], C0)
        TH = at("TH", [P, DT * T], C0, F32R)
        DHW = at("DHW", [P, 2 * D], C0, F32R)
        DLW = at("DLW", [P, 2 * D], C0 + 8192, F32R)
        DST = at("DST", [P, 2, D], C0 + 16384)
        PST = at("PST", [P, DT, PLE], C0 + 24576)
        PHW = at("PHW", [P, 2 * D], C0 + 24576, F32R)
        PLW = at("PLW", [P, 2 * D], C0 + 16384, F32R)
        OST = at("OST", [NB + 2, CA + FF], C0)
        XT = at("XT", [P, DT * T], D0)
        W2 = at("W2", [P, 2, NJ, (CH + 1) * HG], D0)
        U = at("U", [P, CH, UW], D0 + 18432)
        S = at("S", [P, 2, 4, SW], D0 + 18432 + 4608)
        GB = at("GB", [HG, NJ, P], D0 + 18432)
        APT = at("APT", [P, NPOW, NJ], D0 + 18432 + 4608 + 4640)
        YST = at("YST", [P, 2, 2, UC], D0 + 18432 + 4608 + 4640 + 4 * NPOW * NJ)
        YGH = at("YGH", [P, CT * T], D0, F32R)
        YGL = at("YGL", [P, CT * T], D0 + CT * TB4, F32R)
        X = XT
        RS = at("RS", [P, T], E0)
        W0 = E0 + TB4
        WST = at("WST", [P, 2, D], W0)
        WH = at("WH", [P, 2 * D], W0 + 8192, F32R)
        WL = at("WL", [P, 2 * D], W0 + 16384, F32R)
        T0 = W0 + 24576
        TA = at("TA", [P, T], T0)
        TBf = at("TB", [P, T], T0 + TB4)
        TC = at("TC", [P, T], T0 + 2 * TB4)
        XS = at("XS", [NB, D], T0)
        BN = at("BN", [P, 2, NJ, HG], T0 + 2 * TB4)
        CTT = at("CTT", [P, 2, NJ, HG], T0 + 2 * TB4 + 2048)
        ST1 = at("ST1", [P, 480], T0 + 2 * TB4)
        ST2 = at("ST2", [P, 480], T0 + 2 * TB4 + 1920)
        k0 = T0 + 3 * TB4
        IDN = at("IDN", [P, P], k0)
        ONES = at("ONES", [P, P], k0 + 512)
        KV = at("KV", [P, NK1 + NK2], k0 + 1024)
        CB = at("CB", [P, CT + FT, 2 * NB], k0 + 1024 + 544)
        LAST = at("LAST", [P, CT + FT, NB + 2], k0 + 1568 + 1664)
        FS = at("FS", [P, 2, NJ, NB + 1], k0 + 3232 + 1056)
        S0 = at("S0", [P, 2, NJ, NB], k0 + 4288 + 1152)
        PSS = at("PSS", [NB, PLE], k0 + 5440)
        US = at("US", [P, CT, NB], k0 + 5440 + 1024)
        EP = at("EP", [P, 1], k0 + 6464 + 128)
        SSC = at("SSC", [P, 4], k0 + 6592 + 32)

        PS = ctx.enter_context(nc.psum_tensor("PS", [P, 8, 512], F32))
        xscr = nc.dram_tensor("xscr", [DT, P, T], F32, kind="Internal").ap()
        uscr = nc.dram_tensor("uscr", [CA, T], F32, kind="Internal").ap()
        yscr = nc.dram_tensor("yscr", [G, P, UC], F32, kind="Internal").ap()

        s_idn = sem("s_idn")
        s_lam = sem("s_lam")
        s_nat = sem("s_nat")
        s_bn = sem("s_bn")
        s_x = [sem(f"s_x{t}") for t in range(5)]
        s_md = sem("s_md")
        s_mf = sem("s_mf")
        s_stage = [sem("s_stage0"), sem("s_stage1")]
        s_wh = sem("s_wh")
        s_wl = sem("s_wl")
        s_po = sem("s_po")
        s_ev = sem("s_ev")
        s_sq = sem("s_sq")
        s_acc = sem("s_acc")
        s_xh = sem("s_xh")
        s_xl = sem("s_xl")
        s_nm = sem("s_nm")
        s_rt = sem("s_rt")
        s_dv = sem("s_dv")
        s_ac = sem("s_ac")
        s_pl = sem("s_pl")
        s_xsp = sem("s_xsp")
        s_xr = [sem("s_xr0"), sem("s_xr1")]
        s_ang = sem("s_ang")
        s_sin = sem("s_sin")
        s_pow = sem("s_pow")
        s_w1t = sem("s_w1t")
        s_w2 = sem("s_w2")
        s_z = sem("s_z")
        s_to = [sem("s_to0"), sem("s_to1")]
        s_us = [sem(f"s_us{q}") for q in range(CT)]
        s_ul = [sem(f"s_ul{q}") for q in range(CT)]
        s_uz = sem("s_uz")
        s_scan = sem("s_scan")
        s_ys = [sem("s_ys0"), sem("s_ys1")]
        s_yl = sem("s_yl")
        s_ci = sem("s_ci")
        s_cb = sem("s_cb")
        s_va = sem("s_va")
        s_vh = sem("s_vh")
        s_vl = sem("s_vl")
        s_y = sem("s_y")
        s_yg = sem("s_yg")
        s_yl2 = sem("s_yl2")
        s_sa = sem("s_sa")
        s_sg = sem("s_sg")
        s_tf = sem("s_tf")
        s_th = sem("s_th")
        s_tl = sem("s_tl")
        s_fi = sem("s_fi")
        s_fb = sem("s_fb")
        s_fc = sem("s_fc")
        s_ge = sem("s_ge")
        s_g = sem("s_g")
        s_gh = sem("s_gh")
        s_gl = sem("s_gl")
        s_dst = sem("s_dst")
        s_dh = sem("s_dh")
        s_dl = sem("s_dl")
        s_p = sem("s_p")
        s_ph = sem("s_ph")
        s_sp = sem("s_sp")
        s_xo = sem("s_xo")
        s_gf = sem("s_gf")
        s_ss = sem("s_ss")
        s_ot = sem("s_ot")
        s_or = [sem(f"s_or{i}") for i in range(3)]
        s_so = sem("s_so")
        s_out = sem("s_out")

        block = ctx.enter_context(nc.Block())

        def set3(n):
            s = n % 2
            return PS[:, 3 * s:3 * s + 3, 0:TN]

        def bank(k):
            return PS[:, 6 + k % 2, :]

        def v3(t):
            return t.rearrange("p (c n) -> p c n", n=TN)

        def tile(t, m):
            return t[:, bass.ts(m, T)]

        @block.sync
        def _(sp):
            win = a["w_in"][0].rearrange("(k p) n -> p k n", p=P)
            wup = a["w_up"][0].rearrange("(k p) n -> p k n", p=P)
            woa = a["w_out_a"][0].rearrange("(k p) n -> p k n", p=P)
            wga = a["w_glu_a"][0].rearrange("(k p) n -> p k n", p=P)
            wgb = a["w_glu_b"][0].rearrange("(k p) n -> p k n", p=P)
            wo = a["w_o"][0].rearrange("(k p) n -> p k n", p=P)
            wgt = a["w_ple_gate"][0].rearrange("(k p) n -> p k n", p=P)
            wdn = a["w_down"][0].rearrange("(f p) n -> p f n", p=P)
            wpl = a["w_ple"][0].rearrange("(f p) n -> p f n", p=P)

            def load(slot, src, tiles=DT, off=0):
                dst = WST[:, slot, off * P:(off + tiles) * P].rearrange("p (k n) -> p k n", n=P)
                sp.dma_start(dst, src).then_inc(s_stage[slot], 16)

            def tiles_of(w, col):
                return w[:, :, bass.ts(col, P)]

            pair = "(j two) p -> j (two p)"
            sp.dma_start(LAM[:, 0, :], a["lam_re"][0].rearrange(pair, two=2)).then_inc(s_lam, 16)
            sp.dma_start(LAM[:, 1, :], a["lam_im"][0].rearrange(pair, two=2)).then_inc(s_lam, 16)
            sp.dma_start(LDT[:, :], a["log_dt"][0].rearrange("(j two) -> j two", two=2)).then_inc(s_lam, 16)
            row = "(t p) -> t p"
            for k, name in ((K_MIX, "norm_mix"), (K_FFN, "norm_ffn"), (K_PLE, "norm_ple"),
                            (K_CAB, "conv_a_b"), (K_DSK, "d_skip")):
                n = a[name].shape[1] // P
                sp.dma_start(VA1[k:k + n, :], a[name][0].rearrange(row, p=P)).then_inc(s_nat, 16)
            sp.dma_start(VA1[K_CAW:K_CAB, :], a["conv_a_w"][0].rearrange("k (t p) -> (k t) p", p=P)).then_inc(s_nat, 16)
            sp.dma_start(VA2[0:3 * FT, :], a["ffn_conv_w"][0].rearrange("k (t p) -> (k t) p", p=P)).then_inc(s_nat, 16)
            sp.dma_start(VA2[3 * FT:4 * FT, :], a["ffn_conv_b"][0].rearrange(row, p=P)).then_inc(s_nat, 16)
            sp.dma_start(CBN[:, 0:CA], a["state_conv_a"][0].rearrange("b k d -> (b k) d")).then_inc(s_nat, 16)
            sp.dma_start(CBN[:, CA:], a["state_ffn_conv"][0].rearrange("b k d -> (b k) d")).then_inc(s_nat, 16)
            sp.dma_start(S0N[:, 0, :], a["state_ssm_re"][0].rearrange("b g p -> b (g p)")).then_inc(s_nat, 16)
            sp.dma_start(S0N[:, 1, :], a["state_ssm_im"][0].rearrange("b g p -> b (g p)")).then_inc(s_nat, 16)
            for c, name in enumerate(("c_re", "c_im")):
                cj = a[name][0].rearrange("(j two) h p -> j h two p", two=2)
                for half in range(2):
                    for j in range(8):
                        sp.dma_start(CN[j * HG:(j + 1) * HG, c, half, :].rearrange("h (two p) -> h two p", two=2),
                                     cj[8 * half + j]).then_inc(s_nat, 16)
            load(0, tiles_of(win, IN_U))
            load(1, tiles_of(win, IN_U + 1))
            for c, name in enumerate(("b_re", "b_im")):
                sp.dma_start(BN[:, c, :, :], a[name][0].rearrange("(j two) p h -> (two p) j h", two=2)).then_inc(s_bn, 16)
            for q in (2, 3):
                sp.wait_ge(s_wl, q - 1)
                load(q % 2, tiles_of(win, IN_U + q))
            sp.wait_ge(s_mf, M_AP)
            sp.dma_start(xscr.rearrange("m p t -> p m t"), XT[:, :].rearrange("p (m t) -> p m t", t=T)).then_inc(s_xsp, 16)

            def conv_group(g):
                q, part = divmod(g - G_P2, 3)
                sp.wait_ge(s_wl, g - 1)
                load(g % 2, tiles_of(win, (IN_H, IN_C, IN_B)[part] + q))

            conv_group(G_P2)
            for half in range(2):
                sp.wait_ge(s_z, 1)
                sp.wait_ge(s_mf, M_G + 4 * half + 4)
                for r in range(CH):
                    i = CH - 1 - r
                    sp.dma_start(TO[r * HG:(r + 1) * HG, half * NJ:(half + 1) * NJ, i * HG:P],
                                 GB[:, :, 0:P - i * HG]).then_inc(s_to[half], 16)
            conv_group(G_P2 + 1)
            def load_u(q):
                sp.wait_ge(s_us[q], 32)
                if q == 0:
                    sp.wait_ge(s_to[1], 16 * CH)
                    sp.wait_ge(s_uz, 1)
                else:
                    sp.wait_ge(s_md, M_V + 8 * q)
                src = uscr[q * P:(q + 1) * P, :].rearrange("(g h) t -> h g t", h=HG)
                for r in range(CH):
                    i = CH - 1 - r
                    sp.dma_start(U[r * HG:(r + 1) * HG, :, NB:NB + NC], src[:, :, i * NC:(i + 1) * NC]).then_inc(s_ul[q], 16)
                sp.dma_start(U[0:HG, :, NB + NC:UW], src[:, :, SEQ:T]).then_inc(s_ul[q], 16)
                sp.dma_start(U[P - HG:P, :, 0:NB], src[:, :, SEQ:T]).then_inc(s_ul[q], 16)

            load_u(0)
            for q in range(CT):
                for part in range(3):
                    g = G_P2 + 3 * q + part + 2
                    if g < G_P3:
                        conv_group(g)
                    if part == 1 and q > 0:
                        load_u(q)
            def p3_loads(i):
                for j in range(2):
                    m = i * 2 + j
                    sp.wait_ge(s_wl, i * 4 + (G_P3 + 2 * j - 1))
                    load(0, tiles_of(win, m + IN_GA))
                    sp.wait_ge(s_wl, i * 4 + (G_P3 + 2 * j))
                    load(1, tiles_of(woa, m), CT)
            with sp.Fori(0, 4) as i:
                p3_loads(i)
                for r in range(2):
                    sp.wait_ge(s_ys[r], 16 * 8)
                sp.wait_ge(s_yl2, i + 1)
                for g in range(8):
                    sp.dma_start(TA[g * HG:(g + 1) * HG, 0:SEQ].rearrange("h (i c) -> h i c", c=NC),
                                 yscr[i * 8 + g].rearrange("(i h) c -> h i c", h=HG)[:, :, NB:UC]).then_inc(s_yl, 16)
                    sp.dma_start(TA[g * HG:(g + 1) * HG, SEQ:T], yscr[i * 8 + g, 0:HG, 0:NB]).then_inc(s_yl, 16)
                sp.dma_start(TBf[:, :], uscr[bass.ts(i, P), :]).then_inc(s_yl, 16)
            with sp.Fori(0, DT) as m:
                sp.wait_ge(s_wl, m * 2 + (G_P4 - 1))
                load(0, tiles_of(win, m + IN_GS))
                sp.wait_ge(s_wl, m * 2 + G_P4)
                load(1, tiles_of(wgb, m), CT)
                load(1, tiles_of(wga, m), CT, CT)
            with sp.Fori(0, 4) as i:
                for j in range(2):
                    sp.wait_ge(s_wl, i * 2 + (G_P5 + j - 1))
                    load(j, tiles_of(wo, i * 2 + j))
                for j in range(2):
                    if j == 0:
                        sp.wait_ge(s_tl, DT + 1)
                    sp.wait_ge(s_ev, i * 2 + (N_P5 + j - 1))
                    sp.dma_start((TA, TBf)[j][:, :], xscr[i * 2 + j]).then_inc(s_xr[j], 16)
            sp.wait_ge(s_wl, G_A0 - 1)
            load(0, tiles_of(wup, 0))
            sp.wait_ge(s_po, N_P5 + DT)
            sp.dma_start(PST[:, :, :], a["p_prompt"][0, 0].rearrange("(t p) d -> p t d", p=P)).then_inc(s_p, 16)
            sp.dma_start(PSS[:, :], a["p_sample"][0, :, 0, :]).then_inc(s_p, 16)
            sp.dma_start(DST[:, :, :], wdn[:, 0:2, :]).then_inc(s_dst, 16)
            with sp.Fori(0, FP - 1) as p:
                for j, col in ((0, p * 2 + FT), (1, p * 2 + 1), (2, p * 2 + (FT + 1)), (3, p * 2 + 2)):
                    sp.wait_ge(s_wl, p * 4 + (G_P6 + j - 1))
                    load((G_P6 + j) % 2, tiles_of(wup, col))
                    if j == 3:
                        sp.wait_ge(s_dl, p + 1)
                        sp.dma_start(DST[:, :, :], wdn[:, bass.ds(p * 2 + 2, 2), :]).then_inc(s_dst, 16)
            for j, col in enumerate((2 * FT - 2, FT - 1, 2 * FT - 1)):
                sp.wait_ge(s_wl, G_END + j - 1)
                load((G_END + j) % 2, tiles_of(wup, col))
            for m in range(2):
                sp.wait_ge(s_wl, G_P7 + m - 1)
                load((G_P7 + m) % 2, tiles_of(wgt, m))
                if m == 0:
                    sp.wait_ge(s_dl, FP)
                    sp.dma_start(DST[:, :, :], wpl).then_inc(s_dst, 16)
            with sp.Fori(0, 3) as i:
                for j in range(2):
                    sp.wait_ge(s_wl, i * 2 + (G_P7L + j - 1))
                    load(j, tiles_of(wgt, i * 2 + (2 + j)))
            sp.wait_ge(s_mf, M_OUT + 15)
            sp.dma_start(out["conv_a_p"][0, 0], OST[0:2, 0:CA]).then_inc(s_so, 16)
            sp.dma_start(out["conv_a_s"][0, :, 1, :], OST[2:2 + NB, 0:CA]).then_inc(s_so, 16)
            sp.dma_start(out["conv_a_s"][0, :, 0, :], a["state_conv_a"][0, :, 1, :]).then_inc(s_so, 16)
            sp.dma_start(out["ffn_p"][0, 0], OST[0:2, CA:]).then_inc(s_so, 16)
            sp.dma_start(out["ffn_s"][0, :, 1, :], OST[2:2 + NB, CA:]).then_inc(s_so, 16)
            sp.dma_start(out["ffn_s"][0, :, 0, :], a["state_ffn_conv"][0, :, 1, :]).then_inc(s_so, 16)
            for c, part in enumerate(("re", "im")):
                half = SST[:, c * NJ * P:(c + 1) * NJ * P]
                sp.dma_start(out[f"ssm_{part}_p"][0].rearrange("b g p -> b (g p)"), half[0:1, :]).then_inc(s_so, 16)
                sp.dma_start(out[f"ssm_{part}_s"][0].rearrange("b g p -> b (g p)"), half[1:1 + NB, :]).then_inc(s_so, 16)
            sp.wait_ge(s_po, N_P8)
            sp.dma_start(GF[:, :], a["norm_final"].rearrange("(o n) -> o n", o=1).to_broadcast([P, D])).then_inc(s_gf, 16)
            for t in range(DT + 1):
                sp.wait_ge(s_ev, N_P8 + t + 1)
                if t < DT:
                    sp.dma_start(out["y_prompt"][0, t * P:(t + 1) * P, :], OUTT[t % 3][:, :]).then_inc(s_or[t % 3], 16)
                else:
                    sp.dma_start(out["y_sample"][:, 0, :], OUTT[t % 3][0:NB, :]).then_inc(s_or[t % 3], 16)
            for r in range(3):
                sp.wait_ge(s_or[r], 48)
            sp.wait_ge(s_so, 160)

        @block.gpsimd
        def _(pool):
            own = _Steps(pool, s_pl)
            nc.gpsimd.memset(IDN[:, :], 0.0).then_inc(s_idn, 1)
            nc.gpsimd.memset(ONES[:, :], 1.0).then_inc(s_idn, 1)
            nc.gpsimd.memset(EP[:, :], EPS).then_inc(s_idn, 1)
            pool.wait_ge(s_idn, 3)
            nc.gpsimd.affine_select(out=IDN[:, :], in_=IDN[:, :], compare_op=ALU.not_equal, fill=1.0, base=0,
                                    pattern=[[-1, P]], channel_multiplier=1).then_inc(s_idn, 1)

            def lo(g, slot, tiles=DT):
                pool.wait_ge(s_wh, g + 1)
                w = slice(slot * D, slot * D + tiles * P)
                nc.gpsimd.tensor_tensor(WL[:, w], WST[:, slot, 0:tiles * P], WH[:, w].bitcast(F32),
                                        ALU.subtract).then_inc(s_wl, 1)

            def clear_sum():
                own.link(nc.gpsimd.memset(RS[:, :], 0.0))

            def add_squares(m, sq):
                pool.wait_ge(s_sq, m + 1)
                if not isinstance(m, int) or m:
                    pool.wait_ge(s_acc, m)
                nc.gpsimd.tensor_tensor(RS[:, :], RS[:, :], sq[:, :], ALU.add).then_inc(s_acc, 1)

            clear_sum()
            lo(0, 0)
            lo(1, 1)
            for m in range(DT):
                add_squares(m, TBf)
            pool.wait_ge(s_mf, M_W1)
            nc.gpsimd.memset(TO[:, :, :], 0.0).then_inc(s_z, 1)
            lo(2, 0)
            lo(3, 1)
            lo(4, 0)
            pool.wait_ge(s_to[1], 16 * CH)
            nc.gpsimd.memset(U[:, :, 0:NB], 0.0)
            nc.gpsimd.memset(U[:, :, NB + NC:UW], 0.0)
            nc.gpsimd.memset(S[:, :, :, NB:NB + 1], 0.0).then_inc(s_uz, 1)
            for g in range(G_P2 + 1, G_P3 + 1):
                lo(g, g % 2)
            with pool.Fori(0, DT) as m:
                lo(m * 2 + (G_P3 + 1), 1, CT)
                lo(m * 2 + (G_P3 + 2), 0)
            with pool.Fori(0, DT) as m:
                lo(m * 2 + (G_P4 + 1), 1)
                lo(m * 2 + (G_P4 + 2), 0)
            pool.wait_ge(s_ev, N_P4 + 3 * (DT - 1) + 1)
            clear_sum()
            with pool.Fori(0, 4) as i:
                for j in range(2):
                    lo(i * 2 + (G_P5 + j + 1), (j + 1) % 2)
                    add_squares(i * 2 + (DT + j), TC)

            def lo_down(p):
                pool.wait_ge(s_dh, p + 1)
                nc.gpsimd.tensor_tensor(DLW[:, :], DST[:, :, :].rearrange("p f n -> p (f n)"),
                                        DHW[:, :].bitcast(F32), ALU.subtract).then_inc(s_dl, 1)

            lo(G_P6, G_P6 % 2)
            lo(G_P6 + 1, 0)
            with pool.Fori(0, FP - 1) as p:
                lo(p * 4 + (G_P6 + 2), 1)
                lo_down(p)
                for j in (2, 3, 4):
                    lo(p * 4 + (G_P6 + 1 + j), (G_P6 + 1 + j) % 2)
            lo(G_END + 2, 1)
            lo_down(FP - 1)
            lo(G_P7, 0)
            pool.wait_ge(s_dh, FP + 1)
            nc.gpsimd.tensor_tensor(PLW[:, :], DST[:, :, :].rearrange("p f n -> p (f n)"),
                                    PHW[:, :].bitcast(F32), ALU.subtract).then_inc(s_dl, 1)
            pool.wait_ge(s_ev, N_DOWN_END)
            clear_sum()
            lo(G_P7 + 1, 1)
            for m in range(DT):
                add_squares(2 * DT + m, TC)
            lo(G_P7L, 0)
            for g in range(G_P7L + 1, G_P7 + DT):
                lo(g, g % 2)

        @block.scalar
        def _(act):
            own = _Steps(act, s_ac)
            copy = lambda o, i, f=ACT.Copy, **k: nc.scalar.activation(o, i, f, **k)

            def hi(g, slot, n_first, tiles=DT, i=None, per_trip=0):
                act.wait_ge(s_stage[slot], _stage_count(g, i, per_trip))
                if n_first is not None:
                    act.wait_ge(s_po, n_first)
                copy(WH[:, slot * D:slot * D + tiles * P], WST[:, slot, 0:tiles * P]).then_inc(s_wh, 1)

            def evict_misc(k, o, i, **kw):
                act.wait_ge(s_md, k + 1)
                copy(o, i, **kw).then_inc(s_mf, 1)

            def split_hi(count, xt, m, gain, sq, sums):
                if sums is not None and not isinstance(sums, int):
                    act.wait_ge(s_acc, sums)
                copy(tile(XH, m), xt, scale=gain).then_inc(s_xh, 1)
                if isinstance(sums, int):
                    act.wait_ge(s_acc, sums)
                copy(sq[:, :], xt, ACT.Square).then_inc(s_sq, 1)

            def rms(count, n):
                act.wait_ge(s_nm, count)
                copy(v3(RS[:, :]), set3(n + 1), ACT.Sqrt, bias=EP[:, :], scale=1.0 / D).then_inc(s_rt, 1)

            for t in range(4):
                src = a["x_prompt"][0, 2 * t * P:2 * (t + 1) * P, :].rearrange("(t p) d -> p t d", p=P)
                act.dma_start(XN[:, 2 * t:2 * t + 2, :], src).then_inc(s_x[t], 16)
            act.dma_start(XS[:, :], a["x_sample"][:, 0, :]).then_inc(s_x[4], 16)
            evict_misc(M_VEC, KV[:, :], bank(M_VEC)[:, 0:NK1 + NK2])
            evict_misc(M_CB, CB[:, :, :], bank(M_CB)[:, 0:(CT + FT) * 16].rearrange("p (t n) -> p t n", n=16))
            evict_misc(M_S0, S0[:, :, :, :], bank(M_S0)[:, 0:256].rearrange("p (c j b) -> p c j b", c=2, b=NB))
            evict_misc(M_CT, CTT[:, :, :, :], bank(M_CT)[:, :].rearrange("p (c j h) -> p c j h", c=2, h=HG))
            act.wait_ge(s_ang, 1)
            copy(CS[:, :, :], KF[:, :, :], ACT.Sin).then_inc(s_sin, 1)
            X3 = XT[:, :].rearrange("p (m t) -> p m t", t=T)
            for t in range(DT + 1):
                w = P if t < DT else NB
                for half in range(2):
                    evict_misc(M_X + 2 * t + half, X3[:, 4 * half:4 * half + 4, t * P:t * P + w],
                               bank(M_X + half)[:, :].rearrange("p (m t) -> p m t", t=P)[:, :, 0:w])
            hi(0, 0, None)
            hi(1, 1, None)
            act.wait_ge(s_mf, M_AP)
            for m in range(DT):
                split_hi(m, tile(XT, m), m, KV[:, K_MIX + m:K_MIX + m + 1], TBf, m if m else None)
            rms(1, N_U)
            act.wait_ge(s_xl, DT)
            act.wait_ge(s_xsp, 16)
            evict_misc(M_AP, APT[:, 0:32, :], bank(M_AP)[:, :].rearrange("p (r j) -> p r j", j=NJ))
            evict_misc(M_AP + 1, APT[:, 32:NPOW, :],
                       bank(M_AP + 1)[:, 0:(NPOW - 32) * NJ].rearrange("p (r j) -> p r j", j=NJ))

            def store_u(q):
                act.wait_ge(s_ev, N_U + q + 1)
                ut = (TA, TBf)[q % 2][:, :].rearrange("p (i c) -> p i c", i=CH)
                act.dma_start(uscr[q * P:(q + 1) * P, 0:SEQ].rearrange("p (i c) -> p i c", i=CH),
                              ut[:, :, 0:NC]).then_inc(s_us[q], 16)
                act.dma_start(uscr[q * P:(q + 1) * P, SEQ:T], US[:, q, :]).then_inc(s_us[q], 16)

            hi(2, 0, N_U + 1)
            store_u(0)
            hi(3, 1, N_U + 2)
            store_u(1)
            W1f = W1[:, :, :, :].rearrange("p c j n -> p (c j) n")
            for s in range(8):
                evict_misc(M_W1 + s, W1f[:, 4 * s:4 * s + 4, :], bank(M_W1 + s)[:, :].rearrange("p (j n) -> p j n", n=P))
            hi(4, 0, N_U + 3)
            store_u(2)
            G4 = GB[:, :, :].rearrange("h (j two) n -> h j two n", two=2)
            for s in range(8):
                if s == 4:
                    act.wait_ge(s_to[0], 16 * CH)
                jj = 4 * ((s // 2) % 2)
                evict_misc(M_G + s, G4[:, jj:jj + 4, s % 2, :], bank(M_G + s)[0:HG, :].rearrange("p (j n) -> p j n", n=P))
            store_u(3)

            def evict_y(q):
                for s, g0 in enumerate((0, 1, 4, 5)):
                    k = M_V + 8 * q + 4 + s
                    if 4 * q + s >= 2:
                        act.wait_ge(s_ys[s % 2], 16 * ((4 * q + s) // 2))
                    evict_misc(k, YST[:, s % 2, :, :], bank(k)[:, 0:2 * UC].rearrange("p (g c) -> p g c", c=UC))
                    act.wait_ge(s_mf, k + 1)
                    act.dma_start(yscr[8 * q + g0:8 * q + g0 + 3:2].rearrange("g p c -> p g c"),
                                  YST[:, s % 2, :, :]).then_inc(s_ys[s % 2], 16)

            def va_hi(q):
                act.wait_ge(s_va, q + 1)
                copy(tile(VAH, q), TA[:, :]).then_inc(s_vh, 1)

            for q in range(CT):
                n = N_P2 + 3 * q
                g = G_P2 + 3 * q
                hi(g + 1, (g + 1) % 2, n)
                hi(g + 2, (g + 2) % 2, n + 1)
                if q:
                    evict_y(q - 1)
                    va_hi(q - 1)
                    act.wait_ge(s_scan, q)
                for j in range(4):
                    k = M_V + 8 * q + j
                    evict_misc(k, S[:, :, j, NB + 1:SW], bank(k)[:, 0:2 * UC].rearrange("p (c n) -> p c n", n=UC))
                act.wait_ge(s_ci, q + 1)
                copy(TA[:, :], TBf[:, :], ACT.Identity, scale=KV[:, K_CAW + 2 * CT + q:K_CAW + 2 * CT + q + 1],
                     bias=KV[:, K_CAB + q:K_CAB + q + 1]).then_inc(s_cb, 1)
                hi(g + 3, (g + 3) % 2, n + 2)
            va_hi(CT - 1)
            evict_y(CT - 1)
            with act.Fori(0, 4) as i:
                for j in range(2):
                    n, g = N_P3 + 2 * j, G_P3 + 2 * j
                    m = i * 2 + j
                    hi(g + 1, 1, i * 4 + n, CT, i, 4)
                    hi(g + 2, 0, i * 4 + (n + 1), DT, i, 4)
                    act.wait_ge(s_ev, i * 4 + (n + 1))
                    copy(tile(TF, m), tile(TF, m), ACT.Sigmoid).then_inc(s_sa, 1)
                act.wait_ge(s_y, i + 1)
                copy(TC[:, 0:SEQ].rearrange("p (c i) -> p i c", i=CH), TA[:, 0:SEQ].rearrange("p (i c) -> p i c", i=CH),
                     ACT.Gelu_apprx_tanh).then_inc(s_yg, 1)
                copy(TC[:, SEQ:T], TA[:, SEQ:T], ACT.Gelu_apprx_tanh).then_inc(s_yg, 1)
                act.wait_ge(s_yg, i * 3 + 2)
                copy(tile(YGH, i), TC[:, :]).then_inc(s_yg, 1)
            with act.Fori(0, 4) as i:
                for j in range(2):
                    n, g = N_P4 + 3 * j, G_P4 + 2 * j
                    hi(g + 1, 1, i * 6 + n, DT, i, 4)
                    hi(g + 2, 0, i * 6 + (n + 1), DT, i, 4)
                    act.wait_ge(s_ev, i * 6 + (n + 1))
                    copy(TA[:, :], TA[:, :], ACT.Sigmoid).then_inc(s_sg, 1)
                    act.wait_ge(s_po, i * 6 + (n + 2))
                    act.wait_ge(s_tf, i * 2 + (j + 1))
                    copy(v3(TBf[:, :]), set3(n + 1), ACT.Sigmoid).then_inc(s_ev, 1)
                    act.wait_ge(s_tf, i * 2 + (j + 2))
                    copy(tile(TH, i * 2 + j), TA[:, :]).then_inc(s_th, 1)
            with act.Fori(0, 4) as i:
                for j in range(2):
                    m = i * 2 + j
                    hi(G_P5 + j + 1, (j + 1) % 2, i * 2 + (N_P5 + j), DT, i, 2)
                    act.wait_ge(s_ev, i * 2 + (N_P5 + j + 1))
                    split_hi(None, tile(XT, m), m, KV[:, bass.ds(m + K_FFN, 1)], TC, i * 2 + (DT + j))
            hi(G_P6, G_P6 % 2, N_A0)
            rms(2, N_A0)

            def hi_down(p, n_before):
                act.wait_ge(s_dst, p * 16 + 16)
                act.wait_ge(s_po, n_before)
                copy(DHW[:, :], DST[:, :, :].rearrange("p f n -> p (f n)")).then_inc(s_dh, 1)

            def conv_tap(f):
                act.wait_ge(s_fi, f + 1)
                copy(TBf[:, :], TA[:, :], ACT.Identity, scale=KV[:, bass.ds(f + (K_FW + 2 * FT), 1)],
                     bias=KV[:, bass.ds(f + K_FB, 1)]).then_inc(s_fb, 1)
                act.wait_ge(s_fc, f + 1)
                copy(TBf[:, :], TBf[:, :], ACT.Gelu_apprx_tanh).then_inc(s_ge, 1)

            def split_g(f, j):
                act.wait_ge(s_g, f + 1)
                copy(tile(GH, j), TC[:, :]).then_inc(s_gh, 1)

            hi(G_P6 + 1, 0, N_P6)
            conv_tap(0)
            with act.Fori(0, FP - 1) as p:
                nb = p * 12 + N_P6
                split_g(p * 2, 0)
                hi(G_P6 + 2, 1, nb + 1, DT, p, 4)
                hi_down(p, nb)
                conv_tap(p * 2 + 1)
                hi(G_P6 + 3, 0, nb + 2, DT, p, 4)
                split_g(p * 2 + 1, 1)
                hi(G_P6 + 4, 1, nb + 3, DT, p, 4)
                hi(G_P6 + 5, 0, nb + 4, DT, p, 4)
                conv_tap(p * 2 + 2)

            def p_hi(k):
                act.wait_ge(s_md, M_PT + k + 1)
                if k < 4:
                    kk, h = divmod(k, 2)
                    copy(PH[:, kk * T + 512 * h:kk * T + 512 * (h + 1)], bank(M_PT + k)[:, :]).then_inc(s_ph, 1)
                else:
                    copy(PH[:, :].rearrange("p (k t) -> p k t", t=T)[:, :, SEQ:T],
                         bank(M_PT + k)[:, 0:2 * NB].rearrange("p (k t) -> p k t", t=NB)).then_inc(s_ph, 1)

            split_g(FT - 2, 0)
            hi(G_END + 2, 1, N_END + 1)
            hi_down(FP - 1, N_END)
            p_hi(0)
            p_hi(1)
            p_hi(2)
            p_hi(3)
            p_hi(4)
            hi(G_P7, 0, N_END + 2)
            conv_tap(FT - 1)
            act.wait_ge(s_dst, FP * 16 + 16)
            act.wait_ge(s_md, M_PT + 5)
            copy(PHW[:, :], DST[:, :, :].rearrange("p f n -> p (f n)")).then_inc(s_dh, 1)
            split_g(FT - 1, 1)
            hi(G_P7 + 1, 1, N_DOWN_END)
            for m in range(DT):
                act.wait_ge(s_ev, N_DOWN_END + m + 1)
                split_hi(None, tile(XT, m), m, KV[:, K_PLE + m:K_PLE + m + 1], TC, 2 * DT + m)
            def states_out(k):
                if k < 7:
                    w = 512 if k < 6 else 256
                    evict_misc(M_OUT + k, OST[:, 512 * k:512 * k + w], bank(M_OUT + k)[0:NB + 2, 0:w])
                else:
                    evict_misc(M_OUT + k, SST[:, 512 * (k - 7):512 * (k - 6)], bank(M_OUT + k)[0:NB + 1, :])

            def ple_gate(m, n):
                act.wait_ge(s_ev, n + 1)
                copy(TA[:, :], TA[:, :], ACT.Sigmoid).then_inc(s_sp, 1)

            hi(G_P7L, 0, N_PW0)
            for k in range(4):
                states_out(k)
            rms(3, N_P7)
            for k in range(4, 15):
                states_out(k)
            ple_gate(0, N_P7)
            ple_gate(1, N_G1)
            for m in range(2, DT):
                n = N_P7L + 2 * (m - 2)
                if m + 1 < DT:
                    hi(G_P7 + m + 1, (m + 1) % 2, n)
                ple_gate(m, n)
            for t in range(DT + 1):
                n = N_P8 + t
                w = P if t < DT else NB
                o = PS[0:w, 3 * (n % 2):3 * (n % 2) + 2, :].rearrange("p a b -> p (a b)")
                act.wait_ge(s_po, n + 1)
                if t >= 2:
                    act.wait_ge(s_ev, n - 1)
                own.link(copy(TC[0:w, 0:D], o, ACT.Square, accum_out=SSC[0:w, t % 2:t % 2 + 1]))
                copy(SSC[0:w, 2 + t % 2:3 + t % 2], SSC[0:w, t % 2:t % 2 + 1], ACT.Sqrt, bias=EP[0:w, :],
                     scale=1.0 / D).then_inc(s_ss, 1)

        @block.vector
        def _(dve):
            own = _Steps(dve, s_dv)
            link = own.link
            tt, ts_, stt = nc.vector.tensor_tensor, nc.vector.tensor_scalar, nc.vector.scalar_tensor_tensor
            MAGIC = 12582912.0

            def exp_small(o, x, e1, e2, ei):
                link(ts_(x, x, -87.0, 88.0, ALU.max, ALU.min))
                link(ts_(e1, x, 1.0 / math.log(2.0), MAGIC, ALU.mult, ALU.add))
                link(ts_(e1, e1, MAGIC, None, ALU.subtract))
                link(stt(x, e1, -0.693359375, x, ALU.mult, ALU.add))
                link(stt(x, e1, 2.12194440e-4, x, ALU.mult, ALU.add))
                link(ts_(e2, x, 1.0 / 5040, None, ALU.mult))
                for d in (720, 120, 24, 6, 2, 1):
                    link(stt(e2, e2, 1.0 / d, x, ALU.add, ALU.mult))
                link(ts_(e1, e1, 127.0, 8388608.0, ALU.add, ALU.mult))
                link(nc.vector.tensor_copy(ei, e1))
                link(stt(o, e2, 1.0, ei.bitcast(F32), ALU.add, ALU.mult))

            dve.wait_ge(s_lam, 48)
            exp_small(DTM[:, :], LDT[:, :], E1[:, 0:2], E2[:, 0:2], EI[:, 0:2])
            dtb = DTM[:, :].unsqueeze(2).to_broadcast([NJ, 2, NS])
            lre, lim = LAM[:, 0, :], LAM[:, 1, :]
            half = "j (two p) -> j two p"
            two = lambda v: v.rearrange(half, two=2)
            link(tt(two(E3[:, :]), two(lim), dtb, ALU.mult))
            link(ts_(KF[:, 0, :], E3[:, :], 1.0 / (2 * math.pi), 0.25, ALU.mult, ALU.add))
            link(ts_(KF[:, 1, :], E3[:, :], 1.0 / (2 * math.pi), None, ALU.mult))
            link(ts_(KF[:, :, :], KF[:, :, :], MAGIC, MAGIC, ALU.add, ALU.subtract))
            for c in range(2):
                dst = CS[:, c, :]
                src = E3[:, :]
                for part in (6.28125, 1.93500518798828125e-3, 3.0199159819e-7):
                    link(stt(dst, KF[:, c, :], -part, src, ALU.mult, ALU.add))
                    src = dst
            link(ts_(KF[:, 0, :], CS[:, 0, :], math.pi / 2, None, ALU.add))
            link(nc.vector.tensor_copy(KF[:, 1, :], CS[:, 1, :]))
            ts_(KF[:, :, :], KF[:, :, :], -3.1415925, 3.1415925, ALU.max, ALU.min).then_inc(s_ang, 1)
            link(tt(two(E3[:, :]), two(lre), dtb, ALU.mult))
            exp_small(Q1[:, 0, :], E3[:, :], E1[:, :], E2[:, :], EI[:, :])
            dve.wait_ge(s_sin, 1)
            mag = Q1[:, 0:1, :].to_broadcast([NJ, 2, P])
            link(nc.vector.memset(AP[:, A_POW(0, 0), :], 1.0))
            link(nc.vector.memset(AP[:, A_POW(0, 1), :], 0.0))
            link(tt(AP[:, A_POW(1, 0):A_POW(1, 1) + 1, :], CS[:, :, :], mag, ALU.mult))
            are, aim = AP[:, A_POW(1, 0), :], AP[:, A_POW(1, 1), :]
            link(tt(E1[:, :], lre, lre, ALU.mult))
            link(tt(E2[:, :], lim, lim, ALU.mult))
            link(tt(E1[:, :], E1[:, :], E2[:, :], ALU.add))
            link(nc.vector.reciprocal(E3[:, :], E1[:, :]))
            link(ts_(E1[:, :], are, -1.0, None, ALU.add))
            link(tt(E2[:, :], E1[:, :], lre, ALU.mult))
            link(tt(Q1[:, 0, :], aim, lim, ALU.mult))
            link(tt(E2[:, :], E2[:, :], Q1[:, 0, :], ALU.add))
            link(tt(AP[:, COEF, :], E2[:, :], E3[:, :], ALU.mult))
            link(tt(E2[:, :], E1[:, :], lim, ALU.mult))
            link(tt(Q1[:, 0, :], aim, lre, ALU.mult))
            link(tt(E2[:, :], Q1[:, 0, :], E2[:, :], ALU.subtract))
            link(tt(AP[:, COEF + 1, :], E2[:, :], E3[:, :], ALU.mult))

            def cmul(dst, src, by, n):
                rows = lambda r, c: AP[:, r:r + 2 * n, :].rearrange("j (n c) p -> j n c p", c=2)[:, :, c, :]
                b = [AP[:, by + c:by + c + 1, :].to_broadcast([NJ, n, P]) for c in range(2)]
                q1, q2 = Q1[:, 0:n, :], Q2[:, 0:n, :]
                tt(q1, rows(src, 0), b[0], ALU.mult).then_inc(s_dv, 1)
                link2(tt(q2, rows(src, 1), b[1], ALU.mult))
                link(tt(rows(dst, 0), q1, q2, ALU.subtract))
                tt(q1, rows(src, 0), b[1], ALU.mult).then_inc(s_dv, 1)
                link2(tt(q2, rows(src, 1), b[0], ALU.mult))
                link(tt(rows(dst, 1), q1, q2, ALU.add))

            def link2(ins):
                own.n += 1
                link(ins)

            r = A_POW
            cmul(r(2, 0), r(1, 0), r(1, 0), 1)
            cmul(r(3, 0), r(1, 0), r(2, 0), 2)
            cmul(r(5, 0), r(1, 0), r(4, 0), 4)
            link(nc.vector.tensor_copy(AP[:, A_CHUNK(1, 0):A_CHUNK(1, 0) + 2, :], AP[:, r(8, 0):r(8, 0) + 2, :]))
            r = A_CHUNK
            cmul(r(2, 0), r(1, 0), r(1, 0), 1)
            cmul(r(3, 0), r(1, 0), r(2, 0), 2)
            cmul(r(5, 0), r(1, 0), r(4, 0), 4)
            for k in range(3):
                cmul(A_BLOCK(k + 1, 0), A_BLOCK(k, 0), A_BLOCK(k, 0), 1)
            nc.vector.tensor_copy(Q1[:, 0, 0:1], AP[:, NPOW - 1, 0:1]).then_inc(s_pow, 1)

            def split_lo(count, xt, m, gain):
                dve.wait_ge(s_xh, count + 1)
                stt(tile(XL, m), xt, gain, tile(XH, m).bitcast(F32), ALU.mult, ALU.subtract).then_inc(s_xl, 1)

            dve.wait_ge(s_md, M_X)
            for m in range(DT):
                split_lo(m, tile(XT, m), m, KV[:, K_MIX + m:K_MIX + m + 1])

            def recip(count):
                dve.wait_ge(s_rt, count)
                link(nc.vector.reciprocal(RS[:, :], RS[:, :]))

            def scaled(n, o, wait_n=None):
                dve.wait_ge(s_po, (n if wait_n is None else wait_n) + 1)
                tt(v3(o), set3(n), v3(RS[:, :]), ALU.mult).then_inc(s_ev, 1)

            def evict_u(q):
                n = N_U + q
                dve.wait_ge(s_po, n + 1)
                if q >= 2:
                    dve.wait_ge(s_us[q - 2], 32)
                if q == 1:
                    dve.wait_ge(s_acc, DT)
                tt(US[:, q, :], PS[:, 3 * (n % 2) + 2, TN - NB:TN], RS[:, SEQ:T], ALU.mult)
                o = (TA, TBf)[q % 2][:, :].rearrange("p (i c d) -> p c d i", i=CH, c=NCH)
                i0 = set3(n).rearrange("p c (d i) -> p c d i", i=CH)
                i1 = v3(RS[:, :]).rearrange("p c (d i) -> p c d i", i=CH)
                last = None
                for c in range(NCH):
                    last = tt(o[:, c], i0[:, c], i1[:, c], ALU.mult)
                last.then_inc(s_ev, 1)

            recip(1)
            evict_u(0)
            dve.wait_ge(s_mf, M_W1)
            dve.wait_ge(s_bn, 32)
            cf = [APT[:, COEF + c, :].unsqueeze(2).to_broadcast([P, NJ, HG]) for c in range(2)]
            mt = MT[:, 0:NJ * HG].rearrange("p (j h) -> p j h", h=HG)
            link(tt(BB[:, 0], BN[:, 0], cf[0], ALU.mult))
            link(tt(mt, BN[:, 1], cf[1], ALU.mult))
            link(tt(BB[:, 0], BB[:, 0], mt, ALU.subtract))
            link(tt(BB[:, 1], BN[:, 1], cf[0], ALU.mult))
            link(tt(mt, BN[:, 0], cf[1], ALU.mult))
            link(tt(BB[:, 1], BB[:, 1], mt, ALU.add))

            def power_rows(o, v, n, sign):
                w = [APT[:, 0:2 * n, :].rearrange("p (k c) j -> p c j k", c=2)[:, c].unsqueeze(3).to_broadcast([P, NJ, n, HG])
                     for c in range(2)]
                x = [v[:, c].unsqueeze(2).to_broadcast([P, NJ, n, HG]) for c in range(2)]
                m4 = MT[:, 0:NJ * n * HG].rearrange("p (j k h) -> p j k h", j=NJ, k=n)
                o4 = [o[:, c].rearrange("p j (k h) -> p j k h", k=n) for c in range(2)]
                link(tt(o4[0], x[0], w[0], ALU.mult))
                link(tt(m4, x[1], w[1], ALU.mult))
                link(tt(o4[0], o4[0], m4, ALU.subtract))
                link(tt(o4[1], x[1], w[0], ALU.mult))
                link(tt(m4, x[0], w[1], ALU.mult))
                if sign > 0:
                    return tt(o4[1], o4[1], m4, ALU.add)
                return stt(o[:, 1].rearrange("p j n -> p (j n)"), o[:, 1].rearrange("p j n -> p (j n)"), -1.0,
                           MT[:, 0:NJ * n * HG], ALU.mult, ALU.subtract)

            power_rows(W1T, BB, CH, 1).then_inc(s_w1t, 1)
            evict_u(1)
            power_rows(W2, CTT, CH + 1, -1).then_inc(s_w2, 1)
            evict_u(2)
            evict_u(3)

            def scan(q):
                dve.wait_ge(s_mf, M_V + 8 * q + 4)
                js = slice(4 * q, 4 * q + 4)
                blk = S[:, :, :, NB + 1:NB + 1 + NC].rearrange("p c j (b i) -> p c j b i", i=CH)

                def cmac(dst, src, pw, n, shp):
                    view = (lambda x: x.rearrange("p (a b) -> p a b", a=shp[0])) if len(shp) == 2 else \
                        (lambda x: x.rearrange("p (a b c) -> p a b c", a=shp[0], b=shp[1]))
                    if 2 * n <= 480:
                        t1, t2, t3, t4 = (view(x) for x in (ST1[:, 0:n], ST1[:, n:2 * n], ST2[:, 0:n], ST2[:, n:2 * n]))
                        tt(t1, src[0], pw[0], ALU.mult)
                        tt(t2, src[1], pw[1], ALU.mult)
                        tt(t3, src[1], pw[0], ALU.mult)
                        link(tt(t4, src[0], pw[1], ALU.mult))
                        tt(dst[0], dst[0], t1, ALU.add)
                        link(tt(dst[1], dst[1], t3, ALU.add))
                        tt(dst[0], dst[0], t2, ALU.subtract)
                        link(tt(dst[1], dst[1], t4, ALU.add))
                    else:
                        t1, t2 = view(ST1[:, 0:n]), view(ST2[:, 0:n])
                        tt(t1, src[0], pw[0], ALU.mult)
                        link(tt(t2, src[1], pw[1], ALU.mult))
                        link(tt(dst[0], dst[0], t1, ALU.add))
                        link(tt(dst[0], dst[0], t2, ALU.subtract))
                        tt(t1, src[1], pw[0], ALU.mult)
                        link(tt(t2, src[0], pw[1], ALU.mult))
                        link(tt(dst[1], dst[1], t1, ALU.add))
                        link(tt(dst[1], dst[1], t2, ALU.add))

                def cmac2(dst, src, row, shp):
                    n = 2 * shp[0] * shp[1]
                    t1, t2 = (x[:, 0:n].rearrange("p (c a b) -> p c a b", c=2, a=shp[0]) for x in (ST1, ST2))
                    w = [APT[:, row + c:row + c + 1, js].unsqueeze(3).to_broadcast([P, 2, *shp]) for c in range(2)]
                    tt(t1, src, w[0], ALU.mult)
                    link(tt(t2, src, w[1], ALU.mult))
                    link(tt(dst, dst, t1, ALU.add))
                    tt(dst[:, 0], dst[:, 0], t2[:, 1], ALU.subtract)
                    link(tt(dst[:, 1], dst[:, 1], t2[:, 0], ALU.add))

                def pws(row, w):
                    return [APT[:, row + c, js].unsqueeze(2).to_broadcast([P, 4, w]) for c in range(2)]

                for i in range(1, CH):
                    cmac2(blk[:, :, :, :, i], blk[:, :, :, :, i - 1], A_POW(CH, 0), [4, NBLK])
                for lv in range(4):
                    d = 1 << lv
                    w = NBLK - d
                    cmac2(blk[:, :, :, d:, CH - 1], blk[:, :, :, 0:w, CH - 1], A_BLOCK(lv, 0), [4, w])
                shp = [P, 4, NBLK - 1, CH - 1]
                pw = [APT[:, A_CHUNK(1, 0):A_CHUNK(CH, 0), js].rearrange("p (i c) j -> p c j i", c=2)[:, c]
                      .unsqueeze(2).to_broadcast(shp) for c in range(2)]
                cmac([blk[:, c, :, 1:, 0:CH - 1] for c in range(2)],
                     [blk[:, c, :, 0:NBLK - 1, CH - 1].unsqueeze(3).to_broadcast(shp) for c in range(2)],
                     pw, 4 * (NBLK - 1) * (CH - 1), shp[1:])
                s0 = [S0[:, c, js, :] for c in range(2)]
                cmac([S[:, c, :, SW - NB:SW] for c in range(2)], s0, pws(A_POW(1, 0), NB), 4 * NB, [4, NB])
                for c in range(2):
                    nc.vector.tensor_copy(FS[:, c, js, :], S[:, c, :, SW - NB - 1:SW])
                nc.vector.tensor_copy(S[:, 0, :, 0:NB], s0[0])
                nc.vector.tensor_copy(S[:, 1, :, 0:NB], s0[1]).then_inc(s_scan, 1)

            def conv(o, x, t, kw, tiles, col):
                def w(k):
                    c = col + kw + k * tiles
                    return KV[:, c:c + 1] if isinstance(c, int) else KV[:, bass.ds(c, 1)]
                st = CB[:, t, :] if isinstance(t, int) else CB[:, bass.ds(t, 1), :].rearrange("p t n -> p (t n)")
                st = st.rearrange("p (b k) -> p k b", k=2)
                stt(o[:, SEQ:T], st[:, 1], w(1), o[:, SEQ:T], ALU.mult, ALU.add)
                link(stt(o[:, 1:SEQ], x[:, 0:SEQ - 1], w(1), o[:, 1:SEQ], ALU.mult, ALU.add))
                stt(o[:, SEQ:T], st[:, 0], w(0), o[:, SEQ:T], ALU.mult, ALU.add)
                return stt(o[:, 2:SEQ], x[:, 0:SEQ - 2], w(0), o[:, 2:SEQ], ALU.mult, ALU.add)

            dve.wait_ge(s_us[2], 32)
            dve.wait_ge(s_us[3], 32)
            for q in range(CT):
                n = N_P2 + 3 * q
                if q:
                    dve.wait_ge(s_vl, q)
                scaled(n, TA[:, :])
                scaled(n + 1, TBf[:, :])
                dve.wait_ge(s_ev, n + 2)
                tt(TBf[:, :], TBf[:, :], TA[:, :], ALU.mult).then_inc(s_ci, 1)
                dve.wait_ge(s_ci, q + 1)
                nc.vector.tensor_copy(LAST[:, q, :], TBf[:, SEQ - 2:T])
                scan(q)
                dve.wait_ge(s_scan, q + 1)
                scaled(n + 2, TC[:, :])
                dve.wait_ge(s_cb, q + 1)
                link(conv(TA, TBf, q, q, CT, K_CAW))
                dve.wait_ge(s_ev, n + 3)
                tt(TA[:, :], TA[:, :], TC[:, :], ALU.mult).then_inc(s_va, 1)
                dve.wait_ge(s_va, q + 1)
                dve.wait_ge(s_vh, q + 1)
                tt(tile(VAL, q), TA[:, :], tile(VAH, q).bitcast(F32), ALU.subtract).then_inc(s_vl, 1)
            dve.wait_ge(s_vl, CT)
            nc.vector.tensor_copy(SSC[:, 0:1], EP[:, :]).then_inc(s_yl2, 1)
            with dve.Fori(0, 4) as i:
                for j in range(2):
                    n = N_P3 + 2 * j
                    scaled(n, tile(TF, i * 2 + j), i * 4 + n)
                    if j == 0:
                        dve.wait_ge(s_yl, i * 272 + 272)
                        tt_y = stt(TA[:, :], TBf[:, :], KV[:, bass.ds(i + K_DSK, 1)], TA[:, :], ALU.mult, ALU.add)
                        tt_y.then_inc(s_y, 1)
                    dve.wait_ge(s_sa, i * 2 + (j + 1))
                    dve.wait_ge(s_po, i * 4 + (n + 2))
                    tt(v3(tile(TF, i * 2 + j)), set3(n + 1), v3(tile(TF, i * 2 + j)), ALU.mult).then_inc(s_ev, 1)
                dve.wait_ge(s_yg, i * 3 + 3)
                tt(tile(YGL, i), TC[:, :], tile(YGH, i).bitcast(F32), ALU.subtract).then_inc(s_yl2, 1)
            dve.wait_ge(s_yl2, CT + 1)
            nc.vector.tensor_copy(SSC[:, 0:1], EP[:, :]).then_inc(s_tf, 1)
            nc.vector.tensor_copy(SSC[:, 1:2], EP[:, :]).then_inc(s_tl, 1)
            with dve.Fori(0, 4) as i:
                own.enter(i, 2)
                for j in range(2):
                    n = N_P4 + 3 * j
                    m = i * 2 + j
                    dve.wait_ge(s_tl, i * 2 + (j + 1))
                    scaled(n, TA[:, :], i * 6 + n)
                    dve.wait_ge(s_ev, i * 6 + (n + 2))
                    dve.wait_ge(s_po, i * 6 + (n + 3))
                    tt(v3(TBf[:, :]), set3(n + 2), v3(TBf[:, :]), ALU.mult).then_inc(s_ev, 1)
                    dve.wait_ge(s_ev, i * 6 + (n + 3))
                    dve.wait_ge(s_sg, i * 2 + (j + 1))
                    link(tt(TA[:, :], TA[:, :], TBf[:, :], ALU.mult))
                    tt(TA[:, :], TA[:, :], tile(TF, m), ALU.add).then_inc(s_tf, 1)
                    dve.wait_ge(s_th, i * 2 + (j + 1))
                    tt(tile(TL, m), TA[:, :], tile(TH, m).bitcast(F32), ALU.subtract).then_inc(s_tl, 1)
                own.leave(4)
            with dve.Fori(0, 4) as i:
                for j in range(2):
                    n = N_P5 + j
                    m = i * 2 + j
                    dve.wait_ge(s_xr[j], i * 16 + 16)
                    dve.wait_ge(s_po, i * 2 + (n + 1))
                    tt(v3(tile(XT, m)), set3(n), v3((TA, TBf)[j][:, :]), ALU.add).then_inc(s_ev, 1)
                    split_lo(i * 2 + (DT + j), tile(XT, m), m, KV[:, bass.ds(m + K_FFN, 1)])
            recip(2)

            def up_a(f, n, wait_n):
                dve.wait_ge(s_po, wait_n + 1)
                if not isinstance(f, int) or f:
                    dve.wait_ge(s_fc, f)
                tt(v3(TA[:, :]), set3(n), v3(RS[:, :]), ALU.mult).then_inc(s_ev, 1)
                dve.wait_ge(s_ev, wait_n + 1)
                nc.vector.tensor_copy(LAST[:, bass.ds(f + CT, 1), :].rearrange("p t n -> p (t n)"),
                                      TA[:, SEQ - 2:T]).then_inc(s_fi, 1)

            def conv_a(f):
                dve.wait_ge(s_fb, f + 1)
                conv(TBf, TA, f + CT, f, FT, K_FW).then_inc(s_fc, 1)

            def up_b(f, j, n, wait_n):
                dve.wait_ge(s_gl, f + 1)
                scaled(n, TC[:, :], wait_n)
                dve.wait_ge(s_ev, wait_n + 1)
                dve.wait_ge(s_ge, f + 1)
                tt(TC[:, :], TC[:, :], TBf[:, :], ALU.mult).then_inc(s_g, 1)
                dve.wait_ge(s_gh, f + 1)
                tt(tile(GL, j), TC[:, :], tile(GH, j).bitcast(F32), ALU.subtract).then_inc(s_gl, 1)

            def down(n, wait_n, ms):
                for m in ms:
                    dve.wait_ge(s_po, wait_n + (m + 1))
                    xm = v3(tile(XT, m))
                    tt(xm, set3(n + m), xm, ALU.add).then_inc(s_ev, 1)

            dve.wait_ge(s_acc, 2 * DT)
            nc.vector.tensor_copy(SSC[:, 2:3], EP[:, :]).then_inc(s_gl, 1)
            up_a(0, N_A0, N_A0)
            conv_a(0)
            with dve.Fori(0, FP - 1) as p:
                own.enter(p, 2)
                nb = p * 12 + N_P6
                up_b(p * 2, 0, N_P6, nb)
                up_a(p * 2 + 1, N_P6 + 1, nb + 1)
                conv_a(p * 2 + 1)
                up_b(p * 2 + 1, 1, N_P6 + 2, nb + 2)
                up_a(p * 2 + 2, N_P6 + 3, nb + 3)
                down(N_P6 + 4, nb + 4, (0,))
                conv_a(p * 2 + 2)
                down(N_P6 + 4, nb + 4, range(1, DT))
                own.leave(FP - 1)

            def p_lo(k):
                dve.wait_ge(s_ph, k + 1)
                if k < 4:
                    kk, h = divmod(k, 2)
                    w = slice(kk * T + 512 * h, kk * T + 512 * (h + 1))
                    tt(PL[:, w], bank(M_PT + k)[:, :], PH[:, w].bitcast(F32), ALU.subtract).then_inc(s_mf, 1)
                else:
                    w3 = lambda t: t.rearrange("p (k t) -> p k t", t=T)[:, :, SEQ:T]
                    tt(w3(PL[:, :]), bank(M_PT + k)[:, 0:2 * NB].rearrange("p (k t) -> p k t", t=NB),
                       w3(PH[:, :].bitcast(F32)), ALU.subtract).then_inc(s_mf, 1)

            up_b(FT - 2, 0, N_END, N_END)
            p_lo(0)
            p_lo(1)
            up_a(FT - 1, N_END + 1, N_END + 1)
            p_lo(2)
            p_lo(3)
            p_lo(4)
            conv_a(FT - 1)
            up_b(FT - 1, 1, N_END + 2, N_END + 2)
            for m in range(DT + 1):
                if m < DT:
                    down(N_DOWN_END, N_DOWN_END, (m,))
                if m:
                    split_lo(2 * DT + m - 1, tile(XT, m - 1), m - 1, KV[:, K_PLE + m - 1:K_PLE + m])
            recip(3)

            def ple(m, n_g, n_p, wg, wp):
                dve.wait_ge(s_po, wg + 1)
                tt(v3(TA[:, :]), set3(n_g), v3(RS[:, :]), ALU.mult).then_inc(s_ev, 1)
                dve.wait_ge(s_sp, m + 1)
                dve.wait_ge(s_po, wp + 1)
                if not isinstance(m, int) or m:
                    dve.wait_ge(s_xo, m)
                tt(v3(TBf[:, :]), set3(n_p), v3(TA[:, :]), ALU.mult).then_inc(s_ev, 1)
                dve.wait_ge(s_ev, wp + 1)
                tt(tile(XT, m), tile(XT, m), TBf[:, :], ALU.add).then_inc(s_xo, 1)

            ple(0, N_P7, N_PW0, N_P7, N_PW0)
            ple(1, N_G1, N_G1 + 1, N_G1, N_G1 + 1)
            with dve.Fori(0, 3) as i:
                for j in range(2):
                    n = N_P7L + 2 * j
                    ple(i * 2 + (2 + j), n, n + 1, i * 4 + n, i * 4 + (n + 1))
            dve.wait_ge(s_gf, 16)
            for t in range(DT + 1):
                n = N_P8 + t
                w = P if t < DT else NB
                o = PS[0:w, 3 * (n % 2):3 * (n % 2) + 2, :].rearrange("p a b -> p (a b)")
                dve.wait_ge(s_ss, t + 1)
                if t >= 3:
                    dve.wait_ge(s_or[t % 3], 16 * (t // 3))
                link(nc.vector.reciprocal(SSC[0:w, 2 + t % 2:3 + t % 2], SSC[0:w, 2 + t % 2:3 + t % 2]))
                stt(OUTT[t % 3][0:w, :], o, SSC[0:w, 2 + t % 2:3 + t % 2], GF[0:w, :], ALU.mult, ALU.mult).then_inc(s_ev, 1)

        @block.tensor
        def _(pe):
            mm, tr = nc.tensor.matmul, nc.tensor.transpose

            def product(n, wait_n, slot_off, ks, xh, xl, ready=None, wh=WH, wl=WL):
                if not isinstance(wait_n, int) or wait_n >= 2:
                    pe.wait_ge(s_ev, wait_n - 1)
                last = None
                for k in range(ks):
                    if ready is not None:
                        ready(k)
                    w = slice(slot_off + k * P, slot_off + (k + 1) * P)
                    for r, (ww, xx) in enumerate(((wh, xh), (wh, xl), (wl, xh))):
                        for c in range(NCH):
                            cols = slice(k * T + c * TN, k * T + (c + 1) * TN)
                            last = mm(PS[:, 3 * (n % 2) + c, 0:TN], ww[:, w], xx[:, cols],
                                      start=(k == 0 and r == 0), stop=(k == ks - 1 and r == 2))
                last.then_inc(s_po, 1)

            def group(g):
                pe.wait_ge(s_wl, g + 1)

            def misc(k):
                if k >= 2:
                    pe.wait_ge(s_mf, k - 1)
                return bank(k)

            def sum_squares(n, tiles):
                if n:
                    pe.wait_ge(s_ev, n)
                pe.wait_ge(s_acc, tiles)
                last = None
                for c in range(NCH):
                    last = mm(PS[:, 3 * ((n + 1) % 2) + c, 0:TN], ONES[:, :], RS[:, c * TN:(c + 1) * TN], start=True, stop=True)
                last.then_inc(s_nm, 1)

            def rms_read(count):
                pe.wait_ge(s_rt, count)

            pe.wait_ge(s_idn, 4)
            pe.wait_ge(s_nat, 16 * (8 + 4 + 32))
            b = misc(M_VEC)
            tr(b[:, 0:NK1], VA1[:, :], IDN[0:NK1, 0:NK1])
            tr(b[:, NK1:NK1 + NK2], VA2[:, :], IDN[0:NK2, 0:NK2]).then_inc(s_md, 1)
            b = misc(M_CB)
            for t in range(CT + FT):
                last = tr(b[:, 16 * t:16 * (t + 1)], CBN[:, t * P:(t + 1) * P], IDN[0:16, 0:16])
            last.then_inc(s_md, 1)
            b = misc(M_S0)
            for c in range(2):
                for j in range(NJ):
                    o = (c * NJ + j) * NB
                    last = tr(b[:, o:o + NB], S0N[:, c, j * P:(j + 1) * P], IDN[0:NB, 0:NB])
            last.then_inc(s_md, 1)
            b = misc(M_CT)
            for c in range(2):
                for half in range(2):
                    last = tr(b[:, (2 * c + half) * P:(2 * c + half + 1) * P], CN[:, c, half, :], IDN[:, :])
            last.then_inc(s_md, 1)
            for t in range(DT + 1):
                w = P if t < DT else NB
                if t % 2 == 0:
                    pe.wait_ge(s_x[t // 2], 16)
                for half in range(2):
                    b = misc(M_X + 2 * t + half)
                    for m in range(4):
                        f = slice((4 * half + m) * P, (4 * half + m + 1) * P)
                        src = XN[:, t, f] if t < DT else XS[:, f]
                        last = tr(b[:, m * P:m * P + w], src, IDN[0:w, 0:w])
                    last.then_inc(s_md, 1)
            group(0)
            product(N_U, N_U, 0, DT, XH, XL, lambda k: pe.wait_ge(s_xl, k + 1))
            sum_squares(N_U, DT)
            pe.wait_ge(s_pow, 1)
            for s, (r0, r1) in enumerate(((0, 32), (32, NPOW))):
                b = misc(M_AP + s)
                for r in range(r0, r1):
                    last = tr(b[:, (r - r0) * NJ:(r - r0 + 1) * NJ], AP[:, r, :], IDN[0:NJ, 0:NJ])
                last.then_inc(s_md, 1)
            rms_read(1)
            for q in (1, 2):
                group(q)
                product(N_U + q, N_U + q, (q % 2) * D, DT, XH, XL)
            pe.wait_ge(s_w1t, 1)
            for s in range(8):
                b = misc(M_W1 + s)
                for j in range(4):
                    c, jj = divmod(4 * s + j, NJ)
                    last = tr(b[:, j * P:(j + 1) * P], W1T[:, c, jj, :], IDN[:, :])
                last.then_inc(s_md, 1)
            group(3)
            product(N_U + 3, N_U + 3, D, DT, XH, XL)
            pe.wait_ge(s_w2, 1)
            for s in range(8):
                b = misc(M_G + s)
                two = s % 2
                rows = slice(two * NS, two * NS + NS)
                for idx in range(4):
                    j = 4 * (s // 2) + idx
                    for c in range(2):
                        last = mm(b[0:HG, idx * P:(idx + 1) * P], BB[rows, c, j, :], W2[rows, c, j, 0:P],
                                  start=(c == 0), stop=(c == 1))
                last.then_inc(s_md, 1)

            def inputs_to_states(q):
                pe.wait_ge(s_ul[q], 160)
                for j in range(4):
                    b = misc(M_V + 8 * q + j)
                    for two in range(2):
                        for c in range(2):
                            last = mm(b[two * NS:(two + 1) * NS, c * UC:(c + 1) * UC],
                                      W1[:, c, 4 * q + j, two * NS:(two + 1) * NS], U[:, 2 * j + two, NB:UW],
                                      start=True, stop=True)
                    last.then_inc(s_md, 1)

            def outputs(q):
                pe.wait_ge(s_scan, q + 1)
                for s, gs in enumerate(((0, 2), (1, 3), (4, 6), (5, 7))):
                    b = misc(M_V + 8 * q + 4 + s)
                    for idx, gl in enumerate(gs):
                        rows = slice((gl % 2) * NS, (gl % 2) * NS + NS)
                        o = b[:, idx * UC:(idx + 1) * UC]
                        for c in range(2):
                            mm(o, W2[rows, c, 4 * q + gl // 2, HG:HG + P], S[rows, c, gl // 2, 0:UC],
                               start=(c == 0), stop=False)
                        last = mm(o, TO[:, 8 * q + gl, :], U[:, gl, 0:UC], start=False, stop=True)
                    last.then_inc(s_md, 1)

            for q in range(CT):
                for part in range(3):
                    g, n = G_P2 + 3 * q + part, N_P2 + 3 * q + part
                    group(g)
                    product(n, n, (g % 2) * D, DT, XH, XL)
                    if part == 0 and q:
                        if q == 1:
                            for h in range(2):
                                pe.wait_ge(s_to[h], 16 * CH)
                        outputs(q - 1)
                    if part == 1:
                        inputs_to_states(q)
            def out_a(n, wait_n, g):
                group(g)
                product(n, wait_n, D, CT, VAH, VAL, lambda k: pe.wait_ge(s_vl, k + 1))

            def gate(n, wait_n, g):
                group(g)
                product(n, wait_n, 0, DT, XH, XL)

            gate(N_P3, N_P3, G_P3)
            outputs(CT - 1)
            with pe.Fori(0, 4) as i:
                for j in range(2):
                    n, g = N_P3 + 2 * j, G_P3 + 2 * j
                    out_a(n + 1, i * 4 + (n + 1), i * 4 + (g + 1))
                    gate(n + 2, i * 4 + (n + 2), i * 4 + (g + 2))
            def glu(n, wait_n, g):
                group(g)
                product(n + 1, wait_n + 1, D, CT, YGH, YGL, lambda k: pe.wait_ge(s_yl2, k + 2))
                product(n + 2, wait_n + 2, D + CT * P, CT, YGH, YGL)

            with pe.Fori(0, 3) as i:
                for j in range(2):
                    n, g = N_P4 + 3 * j, G_P4 + 2 * j
                    glu(n, i * 6 + n, i * 4 + (g + 1))
                    gate(n + 3, i * 6 + (n + 3), i * 4 + (g + 2))
            n, g = N_P4 + 18, G_P4 + 12
            glu(n, n, g + 1)
            gate(n + 3, n + 3, g + 2)
            glu(n + 3, n + 3, g + 3)
            with pe.Fori(0, 4) as i:
                for j in range(2):
                    group(i * 2 + (G_P5 + j))
                    product(N_P5 + j, i * 2 + (N_P5 + j), j * D, DT, TH, TL, lambda k: pe.wait_ge(s_tl, k + 2))
            group(G_A0)
            product(N_A0, N_A0, 0, DT, XH, XL, lambda k: pe.wait_ge(s_xl, DT + k + 1))
            sum_squares(N_A0, 2 * DT)
            rms_read(2)

            def down(n, wait_n, p):
                pe.wait_ge(s_dl, p + 1)
                for m in range(DT):
                    down_out(n + m, wait_n + m, m, GH, GL, ready=None if m else lambda k: pe.wait_ge(s_gl, p * 2 + (2 + k)))

            def down_out(n, wait_n, m, xh, xl, wh=DHW, wl=DLW, ready=None):
                pe.wait_ge(s_ev, wait_n - 1)
                last = None
                for k in range(2):
                    if ready is not None:
                        ready(k)
                    w = slice(k * D + m * P, k * D + (m + 1) * P)
                    for r, (ww, xx) in enumerate(((wh, xh), (wh, xl), (wl, xh))):
                        for c in range(NCH):
                            last = mm(PS[:, 3 * (n % 2) + c, 0:TN], ww[:, w], xx[:, k * T + c * TN:k * T + (c + 1) * TN],
                                      start=(k == 0 and r == 0), stop=(k == 1 and r == 2))
                last.then_inc(s_po, 1)

            with pe.Fori(0, FP - 1) as p:
                for j in range(4):
                    group(p * 4 + (G_P6 + j))
                    product(N_P6 + j, p * 12 + (N_P6 + j), ((G_P6 + j) % 2) * D, DT, XH, XL)
                down(N_P6 + 4, p * 12 + (N_P6 + 4), p)
            def transpose_p(k):
                b = misc(M_PT + k)
                if k < 4:
                    kk, h = divmod(k, 2)
                    for t in range(4):
                        last = tr(b[:, t * P:(t + 1) * P], PST[:, 4 * h + t, kk * P:(kk + 1) * P], IDN[:, :])
                else:
                    for kk in range(PT):
                        last = tr(b[:, kk * NB:(kk + 1) * NB], PSS[:, kk * P:(kk + 1) * P], IDN[0:NB, 0:NB])
                last.then_inc(s_md, 1)

            for j in range(3):
                group(G_END + j)
                product(N_END + j, N_END + j, ((G_END + j) % 2) * D, DT, XH, XL)
                if j == 0:
                    pe.wait_ge(s_p, 32)
                for k in ((0, 1), (2, 3, 4), ())[j]:
                    transpose_p(k)
            down(N_DOWN_END, N_DOWN_END, FP - 1)
            group(G_P7)
            product(N_P7, N_P7, 0, DT, XH, XL, lambda k: pe.wait_ge(s_xl, 2 * DT + k + 1))

            def states_out(k):
                b = misc(M_OUT + k)
                if k < 7:
                    for t in range(4 * k, min(4 * k + 4, CT + FT)):
                        last = tr(b[0:NB + 2, (t - 4 * k) * P:(t - 4 * k + 1) * P], LAST[:, t, :], IDN[:, :])
                else:
                    for r in range(4):
                        c, j = divmod(4 * (k - 7) + r, NJ)
                        last = tr(b[0:NB + 1, r * P:(r + 1) * P], FS[:, c, j, :], IDN[:, :])
                last.then_inc(s_md, 1)

            for k in range(4):
                states_out(k)
            sum_squares(N_P7, 3 * DT)
            for k in range(4, 8):
                states_out(k)
            rms_read(3)
            pe.wait_ge(s_dl, FP + 1)
            down_out(N_PW0, N_PW0, 0, PH, PL, PHW, PLW)
            for k in range(8, 15):
                states_out(k)
            group(G_P7 + 1)
            product(N_G1, N_G1, D, DT, XH, XL)
            down_out(N_G1 + 1, N_G1 + 1, 1, PH, PL, PHW, PLW)
            for m in range(2, DT):
                n = N_P7L + 2 * (m - 2)
                group(G_P7 + m)
                product(n, n, (m % 2) * D, DT, XH, XL)
                down_out(n + 1, n + 1, m, PH, PL, PHW, PLW)
            pe.wait_ge(s_xo, DT)
            for t in range(DT + 1):
                n = N_P8 + t
                w = P if t < DT else NB
                pe.wait_ge(s_ev, n - 1)
                for m in range(DT):
                    last = tr(PS[0:w, 3 * (n % 2) + m // 4, (m % 4) * P:(m % 4 + 1) * P],
                              XT[:, m * T + t * P:m * T + t * P + w], IDN[:, :])
                last.then_inc(s_po, 1)


_INS = ["x_prompt", "x_sample", "p_prompt", "p_sample", "state_conv_a", "state_ssm_re", "state_ssm_im",
        "state_ffn_conv", "norm_mix", "w_in", "conv_a_w", "conv_a_b", "w_out_a", "log_dt", "lam_re", "lam_im",
        "b_re", "b_im", "c_re", "c_im", "d_skip", "w_glu_a", "w_glu_b", "w_o", "norm_ffn", "w_up",
        "ffn_conv_w", "ffn_conv_b", "w_down", "norm_ple", "w_ple_gate", "w_ple", "norm_final"]
_OUTS = [("y_prompt", (1, SEQ, D)), ("y_sample", (NB, 1, D)),
         ("conv_a_p", (1, 1, 2, CA)), ("ssm_re_p", (1, 1, G, NS)), ("ssm_im_p", (1, 1, G, NS)),
         ("ffn_p", (1, 1, 2, FF)),
         ("conv_a_s", (1, NB, 2, CA)), ("ssm_re_s", (1, NB, G, NS)), ("ssm_im_s", (1, NB, G, NS)),
         ("ffn_s", (1, NB, 2, FF))]


def kernel(**inputs):
    import numpy as np
    import concourse.bacc as bacc
    from concourse.bass_utils import run_bass_kernel_spmd

    nc = bacc.Bacc("TRN2", target_bir_lowering=False, num_devices=1)
    arrays, ins, outs = {}, {}, {}
    for name in _INS:
        arr = np.ascontiguousarray(inputs[name])
        arrays["in_" + name] = arr
        ins[name] = nc.dram_tensor("in_" + name, arr.shape, F32, kind="ExternalInput").ap()
    for name, shape in _OUTS:
        outs[name] = nc.dram_tensor("out_" + name, shape, F32, kind="ExternalOutput").ap()
    decoder_step(nc, ins, outs)
    r = run_bass_kernel_spmd(nc, [arrays], core_ids=[0])
    return tuple(r.results[0]["out_" + name] for name, _ in _OUTS)
```

```python
import math
from contextlib import ExitStack

import concourse.bass as bass
from concourse import mybir

F32 = mybir.dt.float32
F32R = mybir.dt.float32r
I32 = mybir.dt.int32
ALU = mybir.AluOpType
ACT = mybir.ActivationFunctionType

P = 128
D = 1024
SEQ = 1024
NB = 8
T = SEQ + NB
NCH = 3
TN = T // NCH
DT = D // P
CA = D // 2
CT = CA // P
FF = 2816
FT = FF // P
FP = FT // 2
PLE = 256
PT = PLE // P
XSTEPS = (0, 1, 2, 4, 6, 8)
NOUT = 4
G = 32
NJ = G // 2
HG = 16
NS = 64
CH = 8
NC = SEQ // CH
NBLK = NC // CH
UC = NC + NB
UW = NC + 2 * NB
SW = NB + 1 + NC + NB
EPS = 1e-6

def A_POW(k, c):
    return 2 * k + c
COEF = 2 * (CH + 1)
NPOW1 = COEF + 2
def A_CHUNK(i, c):
    return NPOW1 + 2 * (i - 1) + c
def A_BLOCK(r, c):
    return A_CHUNK(CH, c) if r == 0 else A_CHUNK(CH, 1) + 1 + 2 * (r - 1) + c
NPOW = A_BLOCK(3, 1) + 1

K_MIX, K_FFN, K_PLE, K_CAW, K_CAB, K_DSK, K_FW, K_FB = 0, 8, 16, 24, 36, 40, 44, 110
NK1, NK2 = 44, 88

IN_H, IN_B, IN_C, IN_U, IN_GA, IN_GS = 0, 4, 8, 12, 16, 24

N_U, N_P2, G_P2 = 0, 4, 4
N_P3, G_P3 = 16, 16
N_P4, G_P4 = 32, 32
N_P5, G_P5 = 56, 48
N_A0, G_A0 = 64, 56
N_P6, G_P6 = 65, 57
N_END, G_END = N_P6 + 12 * (FP - 1), G_P6 + 4 * (FP - 1)
N_DOWN_END = N_END + 3
N_P7, G_P7 = N_DOWN_END + DT, G_END + 3
N_PW0, N_G1 = N_P7 + 1, N_P7 + 2
N_P7L, G_P7L = N_P7 + 4, G_P7 + 2
N_P8 = N_P7L + 12

M_X = 0
M_VEC, M_CB, M_S0, M_CT = M_X + 18, M_X + 19, M_X + 20, M_X + 21
M_AP = M_CT + 2
M_W1 = M_AP + 2
M_V = M_W1 + 8
M_G = M_V + 4
def M_S5(q, s):
    return M_V + 8 * q + s + (4 if q or s >= 4 else 0)
M_PT = M_S5(CT, 0)
M_OUT = M_PT + 5


def _stage_count(g, i=None, per_trip=0):
    if g % 2 == 0 or g < G_P4:
        n, each = 16 * (g // 2 + 1), 16
    elif g < G_P5:
        n, each = 16 * (G_P4 // 2) + 32 * ((g - G_P4) // 2 + 1), 32
    else:
        n, each = 16 * (G_P4 // 2) + 32 * DT + 16 * ((g - G_P5) // 2 + 1), 16
    return n if i is None else n + i * (each * per_trip // 2)


class _Steps:

    def __init__(self, eng, sem):
        self.eng, self.sem, self.n, self.i, self.per = eng, sem, 0, None, 0

    def link(self, ins):
        ins.then_inc(self.sem, 1)
        self.n += 1
        self.eng.wait_ge(self.sem, self.n if self.i is None else self.i * self.per + self.n)

    def enter(self, i, per):
        self.i, self.per, self.start = i, per, self.n

    def leave(self, trips):
        assert self.n - self.start == self.per, (self.n - self.start, self.per)
        self.n = self.start + trips * self.per
        self.i = None


def decoder_step(nc, a, out):
    ctx = ExitStack()
    with ctx:
        def sem(name):
            return ctx.enter_context(nc.semaphore(name))

        base = (nc.sbuf_base + 31) // 32 * 32
        TB4 = 4 * T
        A0 = base
        B0 = A0 + 16 * TB4
        C0 = B0 + 8 * TB4
        D0 = C0 + 8 * TB4
        E0 = D0 + 8 * TB4

        def at(name, shape, off, dt=F32):
            return nc.alloc_sbuf_tensor_at(name, shape, dt, offset=off)

        XH = at("XH", [P, DT * T], A0, F32R)
        XL = at("XL", [P, DT * T], A0 + 8 * TB4, F32R)
        XLo = A0 + 8 * TB4
        VA1 = at("VEC1", [NK1, P], XLo)
        VA2 = at("VEC2", [NK2, P], XLo + 512)
        CN = at("CN", [P, 2, 4, 2, NS], E0 + TB4 + 24576 + TB4)
        CBN = at("CBN", [2 * NB, CA + FF], XLo + 1024)
        S0N = at("S0N", [NB, 2, NJ * P], XLo + 1024 + 4 * (CA + FF))
        OUTT = [at(f"OUTT{i}", [P, D], A0 + 4096 * i) for i in range(NOUT)]
        GF = at("GF", [P, D], A0 + NOUT * 4096)
        XN = at("XN", [P, DT, D], B0)
        W1T = at("W1T", [P, 2, NJ, CH * HG], B0)
        MT = at("MT", [P, NJ * (CH + 1) * HG], B0 + 16384)
        BB = at("BB", [P, 2, NJ, HG], B0 + 16384 + 9216)
        MTP = at("MTP", [P, NJ // 2 * (CH + 1) * HG], B0 + 16384 + 9216 + 2048)
        VAH = at("VAH", [P, CT * T], B0, F32R)
        VAL = at("VAL", [P, CT * T], B0 + CT * TB4, F32R)
        TL = at("TL", [P, DT * T], B0, F32R)
        GH = at("GH", [P, 2 * T], B0, F32R)
        GL = at("GL", [P, 2 * T], B0 + 2 * TB4, F32R)
        PH = at("PH", [P, PT * T], B0 + 4 * TB4, F32R)
        PL = at("PL", [P, PT * T], B0 + 6 * TB4, F32R)
        SST = at("SST", [NB + 1, 2 * NJ * P], B0)
        AP = at("AP", [NJ, NPOW, P], C0)
        tiny0 = C0 + NPOW * 512
        LAM = at("LAM", [NJ, 2, P], tiny0)
        LDT = at("LDT", [NJ, 2], tiny0 + 1024)
        DTM = at("DTM", [NJ, 2], tiny0 + 1056)
        E1 = at("E1", [NJ, P], tiny0 + 1088)
        E2 = at("E2", [NJ, P], tiny0 + 1600)
        E3 = at("E3", [NJ, P], tiny0 + 2112)
        EI = at("EI", [NJ, P], tiny0 + 2624, I32)
        KF = at("KF", [NJ, 2, P], tiny0 + 3136)
        CS = at("CS", [NJ, 2, P], tiny0 + 4160)
        Q1 = at("Q1", [NJ, 4, P], tiny0 + 5184)
        Q2 = at("Q2", [NJ, 4, P], tiny0 + 7232)
        W1 = at("W1", [P, 2, NJ, P], C0)
        TO = at("TO", [P, G, P], C0 + 16384)
        TF = at("TF", [P, DT * T], C0)
        TH = at("TH", [P, DT * T], C0, F32R)
        DHW = at("DHW", [P, 2 * D], C0, F32R)
        DLW = at("DLW", [P, 2 * D], C0 + 8192, F32R)
        DST = at("DST", [P, 2, D], C0 + 16384)
        PST = at("PST", [P, DT, PLE], C0 + 24576)
        PHW = at("PHW", [P, 2 * D], C0 + 24576, F32R)
        PLW = at("PLW", [P, 2 * D], C0 + 16384, F32R)
        OST = at("OST", [NB + 2, CA + FF], C0)
        XT = at("XT", [P, DT * T], D0)
        W2 = at("W2", [P, 2, NJ, (CH + 1) * HG], D0)
        U = at("U", [P, CH, UW], D0 + 18432)
        S = at("S", [P, 2, 4, SW], D0 + 18432 + 4608)
        GB = at("GB", [2 * HG, NJ, P], B0)
        BBP = at("BBP", [P, 2, NJ, 2 * HG], B0 + 8192)
        APT = at("APT", [P, NPOW, NJ], D0 + 18432 + 4608 + 4640)
        YST = at("YST", [P, 2, 2, UC], D0 + 18432 + 4608 + 4640 + 4 * NPOW * NJ)
        YGH = at("YGH", [P, CT * T], D0, F32R)
        YGL = at("YGL", [P, CT * T], D0 + CT * TB4, F32R)
        X = XT
        RS = at("RS", [P, T], E0)
        W0 = E0 + TB4
        WST = at("WST", [P, 2, D], W0)
        WH = at("WH", [P, 2 * D], W0 + 8192, F32R)
        WL = at("WL", [P, 2 * D], W0 + 16384, F32R)
        T0 = W0 + 24576
        TA = at("TA", [P, T], T0)
        TBf = at("TB", [P, T], T0 + TB4)
        TC = at("TC", [P, T], T0 + 2 * TB4)
        XS = at("XS", [NB, D], T0)
        BN = at("BN", [P, 2, NJ, HG], T0 + 2 * TB4)
        CTT = at("CTT", [P, 2, NJ, HG], T0 + 2 * TB4 + 2048)
        ST1 = at("ST1", [P, 480], T0 + 2 * TB4)
        ST2 = at("ST2", [P, 480], T0 + 2 * TB4 + 1920)
        k0 = T0 + 3 * TB4
        IDN = at("IDN", [P, P], k0)
        ONES = at("ONES", [P, P], k0 + 512)
        KV = at("KV", [P, NK1 + NK2], k0 + 1024)
        CB = at("CB", [P, CT + FT, 2 * NB], k0 + 1024 + 544)
        LAST = at("LAST", [P, CT + FT, NB + 2], k0 + 1568 + 1664)
        FS = at("FS", [P, 2, NJ, NB + 1], k0 + 3232 + 1056)
        S0 = at("S0", [P, 2, NJ, NB], k0 + 4288 + 1152)
        PSS = at("PSS", [NB, PLE], k0 + 5440)
        US = at("US", [P, CT, NB], k0 + 5440 + 1024)
        EP = at("EP", [P, 1], k0 + 6464 + 128)
        TSC = at("TSC", [P, 8], T0)
        SSC = at("SSC", [P, 4], k0 + 6592 + 32)

        PS = ctx.enter_context(nc.psum_tensor("PS", [P, 8, 512], F32))
        xscr = nc.dram_tensor("xscr", [DT, P, T], F32, kind="Internal").ap()
        uscr = nc.dram_tensor("uscr", [CA, T], F32, kind="Internal").ap()
        yscr = nc.dram_tensor("yscr", [G, P, UC], F32, kind="Internal").ap()

        s_idn = sem("s_idn")
        s_lam = sem("s_lam")
        s_nat = sem("s_nat")
        s_bn = sem("s_bn")
        s_x = [sem(f"s_x{k}") for k in range(len(XSTEPS))]
        s_md = sem("s_md")
        s_mf = sem("s_mf")
        s_stage = [sem("s_stage0"), sem("s_stage1")]
        s_wh = sem("s_wh")
        s_wl = sem("s_wl")
        s_po = sem("s_po")
        s_ev = sem("s_ev")
        s_sq = sem("s_sq")
        s_acc = sem("s_acc")
        s_xh = sem("s_xh")
        s_xl = sem("s_xl")
        s_nm = sem("s_nm")
        s_rt = sem("s_rt")
        s_dv = sem("s_dv")
        s_ac = sem("s_ac")
        s_pl = sem("s_pl")
        s_xsp = sem("s_xsp")
        s_xr = [sem("s_xr0"), sem("s_xr1")]
        s_ang = sem("s_ang")
        s_sin = sem("s_sin")
        s_pow = sem("s_pow")
        s_w1t = sem("s_w1t")
        s_w2 = sem("s_w2")
        s_bbp = sem("s_bbp")
        s_z = sem("s_z")
        s_to = sem("s_to")
        s_us = [sem(f"s_us{q}") for q in range(CT)]
        s_ul = [sem(f"s_ul{q}") for q in range(CT)]
        s_uz = sem("s_uz")
        s_scan = sem("s_scan")
        s_ys = [sem("s_ys0"), sem("s_ys1")]
        s_yl = sem("s_yl")
        s_ci = sem("s_ci")
        s_cb = sem("s_cb")
        s_va = sem("s_va")
        s_vh = sem("s_vh")
        s_vl = sem("s_vl")
        s_y = sem("s_y")
        s_yg = sem("s_yg")
        s_yl2 = sem("s_yl2")
        s_sa = sem("s_sa")
        s_sg = sem("s_sg")
        s_tf = sem("s_tf")
        s_th = sem("s_th")
        s_tl = sem("s_tl")
        s_fi = sem("s_fi")
        s_fb = sem("s_fb")
        s_fc = sem("s_fc")
        s_ge = sem("s_ge")
        s_g = sem("s_g")
        s_gh = sem("s_gh")
        s_gl = sem("s_gl")
        s_dst = sem("s_dst")
        s_dh = sem("s_dh")
        s_dl = sem("s_dl")
        s_p = sem("s_p")
        s_ph = sem("s_ph")
        s_sp = sem("s_sp")
        s_xo = sem("s_xo")
        s_gf = sem("s_gf")
        s_ss = sem("s_ss")
        s_ot = sem("s_ot")
        s_or = [sem(f"s_or{i}") for i in range(NOUT)]
        s_so = sem("s_so")
        s_out = sem("s_out")

        block = ctx.enter_context(nc.Block())

        def set3(n):
            s = n % 2
            return PS[:, 3 * s:3 * s + 3, 0:TN]

        def bank(k):
            return PS[:, 6 + k % 2, :]

        def out_banks(t):
            b = (6, 0, 2, 4)[t % 4]
            return PS[0:P if t < DT else NB, b:b + 2, :]

        def v3(t):
            return t.rearrange("p (c n) -> p c n", n=TN)

        def tile(t, m):
            return t[:, bass.ts(m, T)]

        def power_rows(eng, link, o, v, js, n, tmp, sign, between=()):
            nj = len(js)
            js = slice(js[0], js[-1] + 1)
            w = [APT[:, 0:2 * n, js].rearrange("p (k c) j -> p c j k", c=2)[:, c].unsqueeze(3).to_broadcast([P, nj, n, HG])
                 for c in range(2)]
            x = [v[:, c, js].unsqueeze(2).to_broadcast([P, nj, n, HG]) for c in range(2)]
            m4 = tmp[:, 0:nj * n * HG].rearrange("p (j k h) -> p j k h", j=nj, k=n)
            o4 = [o[:, c, js].rearrange("p j (k h) -> p j k h", k=n) for c in range(2)]
            add, sub = (ALU.add, ALU.subtract) if sign > 0 else (ALU.subtract, ALU.add)
            link(eng.tensor_tensor(o4[0], x[0], w[0], ALU.mult))
            link(eng.tensor_tensor(m4, x[1], w[1], ALU.mult))
            if between:
                between[0]()
            link(eng.tensor_tensor(o4[0], o4[0], m4, sub))
            link(eng.tensor_tensor(o4[1], x[1], w[0], ALU.mult))
            if between:
                between[1]()
            link(eng.tensor_tensor(m4, x[0], w[1], ALU.mult))
            return eng.tensor_tensor(o4[1], o4[1], m4, add)

        @block.sync
        def _(sp):
            win = a["w_in"][0].rearrange("(k p) n -> p k n", p=P)
            wup = a["w_up"][0].rearrange("(k p) n -> p k n", p=P)
            woa = a["w_out_a"][0].rearrange("(k p) n -> p k n", p=P)
            wga = a["w_glu_a"][0].rearrange("(k p) n -> p k n", p=P)
            wgb = a["w_glu_b"][0].rearrange("(k p) n -> p k n", p=P)
            wo = a["w_o"][0].rearrange("(k p) n -> p k n", p=P)
            wgt = a["w_ple_gate"][0].rearrange("(k p) n -> p k n", p=P)
            wdn = a["w_down"][0].rearrange("(f p) n -> p f n", p=P)
            wpl = a["w_ple"][0].rearrange("(f p) n -> p f n", p=P)

            def load(slot, src, tiles=DT, off=0):
                dst = WST[:, slot, off * P:(off + tiles) * P].rearrange("p (k n) -> p k n", n=P)
                sp.dma_start(dst, src).then_inc(s_stage[slot], 16)

            def tiles_of(w, col):
                return w[:, :, bass.ts(col, P)]

            pair = "(j two) p -> j (two p)"
            sp.dma_start(LAM[:, 0, :], a["lam_re"][0].rearrange(pair, two=2)).then_inc(s_lam, 16)
            sp.dma_start(LAM[:, 1, :], a["lam_im"][0].rearrange(pair, two=2)).then_inc(s_lam, 16)
            sp.dma_start(LDT[:, :], a["log_dt"][0].rearrange("(j two) -> j two", two=2)).then_inc(s_lam, 16)
            row = "(t p) -> t p"
            for k, name in ((K_MIX, "norm_mix"), (K_FFN, "norm_ffn"), (K_PLE, "norm_ple"),
                            (K_CAB, "conv_a_b"), (K_DSK, "d_skip")):
                n = a[name].shape[1] // P
                sp.dma_start(VA1[k:k + n, :], a[name][0].rearrange(row, p=P)).then_inc(s_nat, 16)
            sp.dma_start(VA1[K_CAW:K_CAB, :], a["conv_a_w"][0].rearrange("k (t p) -> (k t) p", p=P)).then_inc(s_nat, 16)
            sp.dma_start(VA2[0:3 * FT, :], a["ffn_conv_w"][0].rearrange("k (t p) -> (k t) p", p=P)).then_inc(s_nat, 16)
            sp.dma_start(VA2[3 * FT:4 * FT, :], a["ffn_conv_b"][0].rearrange(row, p=P)).then_inc(s_nat, 16)
            sp.dma_start(CBN[:, 0:CA], a["state_conv_a"][0].rearrange("b k d -> (b k) d")).then_inc(s_nat, 16)
            sp.dma_start(CBN[:, CA:], a["state_ffn_conv"][0].rearrange("b k d -> (b k) d")).then_inc(s_nat, 16)
            sp.dma_start(S0N[:, 0, :], a["state_ssm_re"][0].rearrange("b g p -> b (g p)")).then_inc(s_nat, 16)
            sp.dma_start(S0N[:, 1, :], a["state_ssm_im"][0].rearrange("b g p -> b (g p)")).then_inc(s_nat, 16)
            for c, name in enumerate(("c_re", "c_im")):
                for twice in range(2):
                    sp.dma_start(CN[:, c, :, twice, :],
                                 a[name][0].rearrange("(e g) h p -> (g h) e p", e=4)).then_inc(s_nat, 16)
            load(0, tiles_of(win, IN_U))
            load(1, tiles_of(win, IN_U + 1))
            for c, name in enumerate(("b_re", "b_im")):
                sp.dma_start(BN[:, c, :, :], a[name][0].rearrange("(j two) p h -> (two p) j h", two=2)).then_inc(s_bn, 16)
            for q in (2, 3):
                sp.wait_ge(s_wl, q - 1)
                load(q % 2, tiles_of(win, IN_U + q))
            sp.wait_ge(s_mf, M_AP)
            sp.dma_start(xscr.rearrange("m p t -> p m t"), XT[:, :].rearrange("p (m t) -> p m t", t=T)).then_inc(s_xsp, 16)

            def conv_group(g):
                q, part = divmod(g - G_P2, 3)
                sp.wait_ge(s_wl, g - 1)
                load(g % 2, tiles_of(win, (IN_H, IN_C, IN_B)[part] + q))

            conv_group(G_P2)
            def load_u(q):
                sp.wait_ge(s_us[q], 32)
                if q == 0:
                    sp.wait_ge(s_uz, 1)
                else:
                    sp.wait_ge(s_md, M_S5(q, 0))
                src = uscr[q * P:(q + 1) * P, :].rearrange("(g h) t -> h g t", h=HG)
                for r in range(CH):
                    i = CH - 1 - r
                    sp.dma_start(U[r * HG:(r + 1) * HG, :, NB:NB + NC], src[:, :, i * NC:(i + 1) * NC]).then_inc(s_ul[q], 16)
                sp.dma_start(U[0:HG, :, NB + NC:UW], src[:, :, SEQ:T]).then_inc(s_ul[q], 16)
                sp.dma_start(U[P - HG:P, :, 0:NB], src[:, :, SEQ:T]).then_inc(s_ul[q], 16)

            conv_group(G_P2 + 1)
            load_u(0)
            conv_group(G_P2 + 2)
            conv_group(G_P2 + 3)
            sp.wait_ge(s_z, 1)
            sp.wait_ge(s_mf, M_G + 4)
            for r in range(CH):
                i = CH - 1 - r
                for two in range(2):
                    rows = TO[r * HG:(r + 1) * HG, :, :].rearrange("h (j two) n -> h two j n", two=2)[:, two]
                    sp.dma_start(rows[:, :, i * HG:P], GB[two * HG:(two + 1) * HG, :, 0:P - i * HG]).then_inc(s_to, 16)
            for q in range(CT):
                for part in range(3):
                    g = G_P2 + 3 * q + part + 2
                    if G_P2 + 3 < g < G_P3:
                        conv_group(g)
                    if part == 1 and q > 0:
                        load_u(q)
            def p3_loads(i):
                for j in range(2):
                    m = i * 2 + j
                    sp.wait_ge(s_wl, i * 4 + (G_P3 + 2 * j - 1))
                    load(0, tiles_of(win, m + IN_GA))
                    sp.wait_ge(s_wl, i * 4 + (G_P3 + 2 * j))
                    load(1, tiles_of(woa, m), CT)
            with sp.Fori(0, 4) as i:
                p3_loads(i)
                for r in range(2):
                    sp.wait_ge(s_ys[r], 16 * 8)
                sp.wait_ge(s_yl2, i + 1)
                for g in range(8):
                    sp.dma_start(TA[g * HG:(g + 1) * HG, 0:SEQ].rearrange("h (i c) -> h i c", c=NC),
                                 yscr[i * 8 + g].rearrange("(i h) c -> h i c", h=HG)[:, :, NB:UC]).then_inc(s_yl, 16)
                    sp.dma_start(TA[g * HG:(g + 1) * HG, SEQ:T], yscr[i * 8 + g, 0:HG, 0:NB]).then_inc(s_yl, 16)
                sp.dma_start(TBf[:, :], uscr[bass.ts(i, P), :]).then_inc(s_yl, 16)
            with sp.Fori(0, DT) as m:
                sp.wait_ge(s_wl, m * 2 + (G_P4 - 1))
                load(0, tiles_of(win, m + IN_GS))
                sp.wait_ge(s_wl, m * 2 + G_P4)
                load(1, tiles_of(wgb, m), CT)
                load(1, tiles_of(wga, m), CT, CT)
            with sp.Fori(0, 4) as i:
                for j in range(2):
                    sp.wait_ge(s_wl, i * 2 + (G_P5 + j - 1))
                    load(j, tiles_of(wo, i * 2 + j))
                for j in range(2):
                    if j == 0:
                        sp.wait_ge(s_tl, DT + 1)
                    sp.wait_ge(s_ev, i * 2 + (N_P5 + j - 1))
                    sp.dma_start((TA, TBf)[j][:, :], xscr[i * 2 + j]).then_inc(s_xr[j], 16)
            sp.wait_ge(s_wl, G_A0 - 1)
            load(0, tiles_of(wup, 0))
            sp.wait_ge(s_po, N_P5 + DT)
            sp.dma_start(PST[:, :, :], a["p_prompt"][0, 0].rearrange("(t p) d -> p t d", p=P)).then_inc(s_p, 16)
            sp.dma_start(PSS[:, :], a["p_sample"][0, :, 0, :]).then_inc(s_p, 16)
            sp.dma_start(DST[:, :, :], wdn[:, 0:2, :]).then_inc(s_dst, 16)
            with sp.Fori(0, FP - 1) as p:
                for j, col in ((0, p * 2 + FT), (1, p * 2 + 1), (2, p * 2 + (FT + 1)), (3, p * 2 + 2)):
                    sp.wait_ge(s_wl, p * 4 + (G_P6 + j - 1))
                    load((G_P6 + j) % 2, tiles_of(wup, col))
                    if j == 3:
                        sp.wait_ge(s_dl, p + 1)
                        sp.dma_start(DST[:, :, :], wdn[:, bass.ds(p * 2 + 2, 2), :]).then_inc(s_dst, 16)
            for j, col in enumerate((2 * FT - 2, FT - 1, 2 * FT - 1)):
                sp.wait_ge(s_wl, G_END + j - 1)
                load((G_END + j) % 2, tiles_of(wup, col))
            for m in range(2):
                sp.wait_ge(s_wl, G_P7 + m - 1)
                load((G_P7 + m) % 2, tiles_of(wgt, m))
                if m == 0:
                    sp.wait_ge(s_dl, FP)
                    sp.dma_start(DST[:, :, :], wpl).then_inc(s_dst, 16)
            with sp.Fori(0, 3) as i:
                for j in range(2):
                    sp.wait_ge(s_wl, i * 2 + (G_P7L + j - 1))
                    load(j, tiles_of(wgt, i * 2 + (2 + j)))
            sp.wait_ge(s_mf, M_OUT + 15)
            sp.dma_start(out["conv_a_p"][0, 0], OST[0:2, 0:CA]).then_inc(s_so, 16)
            sp.dma_start(out["conv_a_s"][0, :, 1, :], OST[2:2 + NB, 0:CA]).then_inc(s_so, 16)
            sp.dma_start(out["conv_a_s"][0, :, 0, :], a["state_conv_a"][0, :, 1, :]).then_inc(s_so, 16)
            sp.dma_start(out["ffn_p"][0, 0], OST[0:2, CA:]).then_inc(s_so, 16)
            sp.dma_start(out["ffn_s"][0, :, 1, :], OST[2:2 + NB, CA:]).then_inc(s_so, 16)
            sp.dma_start(out["ffn_s"][0, :, 0, :], a["state_ffn_conv"][0, :, 1, :]).then_inc(s_so, 16)
            for c, part in enumerate(("re", "im")):
                half = SST[:, c * NJ * P:(c + 1) * NJ * P]
                sp.dma_start(out[f"ssm_{part}_p"][0].rearrange("b g p -> b (g p)"), half[0:1, :]).then_inc(s_so, 16)
                sp.dma_start(out[f"ssm_{part}_s"][0].rearrange("b g p -> b (g p)"), half[1:1 + NB, :]).then_inc(s_so, 16)
            sp.wait_ge(s_po, N_P8)
            sp.dma_start(GF[:, :], a["norm_final"].rearrange("(o n) -> o n", o=1).to_broadcast([P, D])).then_inc(s_gf, 16)
            for t in range(DT + 1):
                sp.wait_ge(s_ev, N_P8 + t + 1)
                if t < DT:
                    sp.dma_start(out["y_prompt"][0, t * P:(t + 1) * P, :], OUTT[t % NOUT][:, :]).then_inc(s_or[t % NOUT], 16)
                else:
                    sp.dma_start(out["y_sample"][:, 0, :], OUTT[t % NOUT][0:NB, :]).then_inc(s_or[t % NOUT], 16)
            for r in range(NOUT):
                sp.wait_ge(s_or[r], 16 * len(range(r, DT + 1, NOUT)))
            sp.wait_ge(s_so, 160)

        @block.gpsimd
        def _(pool):
            own = _Steps(pool, s_pl)
            nc.gpsimd.memset(IDN[:, :], 0.0).then_inc(s_idn, 1)
            nc.gpsimd.memset(ONES[:, :], 1.0).then_inc(s_idn, 1)
            nc.gpsimd.memset(EP[:, :], EPS).then_inc(s_idn, 1)
            pool.wait_ge(s_idn, 3)
            nc.gpsimd.affine_select(out=IDN[:, :], in_=IDN[:, :], compare_op=ALU.not_equal, fill=1.0, base=0,
                                    pattern=[[-1, P]], channel_multiplier=1).then_inc(s_idn, 1)

            def lo(g, slot, tiles=DT):
                pool.wait_ge(s_wh, g + 1)
                w = slice(slot * D, slot * D + tiles * P)
                nc.gpsimd.tensor_tensor(WL[:, w], WST[:, slot, 0:tiles * P], WH[:, w].bitcast(F32),
                                        ALU.subtract).then_inc(s_wl, 1)

            def clear_sum():
                own.link(nc.gpsimd.memset(RS[:, :], 0.0))

            def add_squares(m, sq):
                pool.wait_ge(s_sq, m + 1)
                if not isinstance(m, int) or m:
                    pool.wait_ge(s_acc, m)
                nc.gpsimd.tensor_tensor(RS[:, :], RS[:, :], sq[:, :], ALU.add).then_inc(s_acc, 1)

            clear_sum()
            lo(0, 0)
            add_squares(0, TA)
            lo(1, 1)
            for m in range(1, DT):
                add_squares(m, (TA, TBf)[m % 2])
            lo(2, 0)
            lo(3, 1)
            pool.wait_ge(s_mf, M_AP + 1)
            nc.gpsimd.memset(U[:, :, 0:NB], 0.0)
            nc.gpsimd.memset(U[:, :, NB + NC:UW], 0.0)
            nc.gpsimd.memset(S[:, :, :, NB:NB + 1], 0.0).then_inc(s_uz, 1)
            power_rows(nc.gpsimd, own.link, W2, CTT, range(NJ // 2), CH + 1, MTP, -1,
                       (lambda: None, lambda: lo(4, 0))).then_inc(s_w2, 1)
            pool.wait_ge(s_mf, M_W1)
            nc.gpsimd.memset(TO[:, :, :], 0.0).then_inc(s_z, 1)
            lo(5, 1)
            for g in range(G_P2 + 2, G_P3 + 1):
                lo(g, g % 2)
            with pool.Fori(0, DT) as m:
                lo(m * 2 + (G_P3 + 1), 1, CT)
                lo(m * 2 + (G_P3 + 2), 0)
            with pool.Fori(0, DT) as m:
                lo(m * 2 + (G_P4 + 1), 1)
                lo(m * 2 + (G_P4 + 2), 0)
            pool.wait_ge(s_ev, N_P4 + 3 * (DT - 1) + 1)
            clear_sum()
            with pool.Fori(0, 4) as i:
                for j in range(2):
                    lo(i * 2 + (G_P5 + j + 1), (j + 1) % 2)
                    add_squares(i * 2 + (DT + j), TC)

            def lo_down(p):
                pool.wait_ge(s_dh, p + 1)
                nc.gpsimd.tensor_tensor(DLW[:, :], DST[:, :, :].rearrange("p f n -> p (f n)"),
                                        DHW[:, :].bitcast(F32), ALU.subtract).then_inc(s_dl, 1)

            lo(G_P6, G_P6 % 2)
            lo(G_P6 + 1, 0)
            with pool.Fori(0, FP - 1) as p:
                lo(p * 4 + (G_P6 + 2), 1)
                lo_down(p)
                for j in (2, 3, 4):
                    lo(p * 4 + (G_P6 + 1 + j), (G_P6 + 1 + j) % 2)
            lo(G_END + 2, 1)
            lo_down(FP - 1)
            lo(G_P7, 0)
            pool.wait_ge(s_dh, FP + 1)
            nc.gpsimd.tensor_tensor(PLW[:, :], DST[:, :, :].rearrange("p f n -> p (f n)"),
                                    PHW[:, :].bitcast(F32), ALU.subtract).then_inc(s_dl, 1)
            pool.wait_ge(s_ev, N_DOWN_END)
            clear_sum()
            lo(G_P7 + 1, 1)
            for m in range(DT):
                add_squares(2 * DT + m, TC)
            lo(G_P7L, 0)
            for g in range(G_P7L + 1, G_P7 + DT):
                lo(g, g % 2)

        @block.scalar
        def _(act):
            own = _Steps(act, s_ac)
            copy = lambda o, i, f=ACT.Copy, **k: nc.scalar.activation(o, i, f, **k)

            def hi(g, slot, n_first, tiles=DT, i=None, per_trip=0):
                act.wait_ge(s_stage[slot], _stage_count(g, i, per_trip))
                if n_first is not None:
                    act.wait_ge(s_po, n_first)
                copy(WH[:, slot * D:slot * D + tiles * P], WST[:, slot, 0:tiles * P]).then_inc(s_wh, 1)

            def evict_misc(k, o, i, **kw):
                act.wait_ge(s_md, k + 1)
                copy(o, i, **kw).then_inc(s_mf, 1)

            def split_hi(count, xt, m, gain, sq, sums):
                if sums is not None and not isinstance(sums, int):
                    act.wait_ge(s_acc, sums)
                copy(tile(XH, m), xt, scale=gain).then_inc(s_xh, 1)
                if isinstance(sums, int):
                    act.wait_ge(s_acc, sums)
                copy(sq[:, :], xt, ACT.Square).then_inc(s_sq, 1)

            def rms(count, n):
                act.wait_ge(s_nm, count)
                copy(v3(RS[:, :]), set3(n + 1), ACT.Sqrt, bias=EP[:, :], scale=1.0 / D).then_inc(s_rt, 1)

            for k in range(len(XSTEPS) - 1):
                t0, t1 = XSTEPS[k:k + 2]
                src = a["x_prompt"][0, t0 * P:t1 * P, :].rearrange("(t p) d -> p t d", p=P)
                act.dma_start(XN[:, t0:t1, :], src).then_inc(s_x[k], 16)
            act.dma_start(XS[:, :], a["x_sample"][:, 0, :]).then_inc(s_x[-1], 16)
            X3 = XT[:, :].rearrange("p (m t) -> p m t", t=T)
            for t in range(DT + 1):
                w = P if t < DT else NB
                for half in range(2):
                    evict_misc(M_X + 2 * t + half, X3[:, 4 * half:4 * half + 4, t * P:t * P + w],
                               bank(M_X + half)[:, :].rearrange("p (m t) -> p m t", t=P)[:, :, 0:w])
            act.wait_ge(s_ang, 1)
            copy(CS[:, :, :], KF[:, :, :], ACT.Sin).then_inc(s_sin, 1)
            evict_misc(M_VEC, KV[:, :], bank(M_VEC)[:, 0:NK1 + NK2])
            hi(0, 0, None)
            act.wait_ge(s_mf, M_VEC + 1)
            split_hi(0, tile(XT, 0), 0, KV[:, K_MIX:K_MIX + 1], TA, None)
            evict_misc(M_CB, CB[:, :, :], bank(M_CB)[:, 0:(CT + FT) * 16].rearrange("p (t n) -> p t n", n=16))
            evict_misc(M_S0, S0[:, :, :, :], bank(M_S0)[:, 0:256].rearrange("p (c j b) -> p c j b", c=2, b=NB))
            for c in range(2):
                act.wait_ge(s_md, M_CT + c + 1)
                both = bank(M_CT + c)[:, :].rearrange("p (j two h) -> p two j h", two=2, h=HG)
                for two in range(2):
                    rows = slice(two * NS, two * NS + NS)
                    last = copy(CTT[rows, c, :, :], both[rows, two], scale=(1.0, -1.0)[c])
                last.then_inc(s_mf, 1)
            act.wait_ge(s_mf, M_AP)
            hi(1, 1, None)
            for m in range(1, DT):
                split_hi(m, tile(XT, m), m, KV[:, K_MIX + m:K_MIX + m + 1], (TA, TBf)[m % 2], m - 1 if m > 1 else None)
            def store_u(q):
                act.wait_ge(s_ev, N_U + q + 1)
                ut = (TA, TBf)[q % 2][:, :].rearrange("p (i c) -> p i c", i=CH)
                act.dma_start(uscr[q * P:(q + 1) * P, 0:SEQ].rearrange("p (i c) -> p i c", i=CH),
                              ut[:, :, 0:NC]).then_inc(s_us[q], 16)
                act.dma_start(uscr[q * P:(q + 1) * P, SEQ:T], US[:, q, :]).then_inc(s_us[q], 16)

            rms(1, N_U)
            hi(2, 0, N_U + 1)
            act.wait_ge(s_xl, DT)
            act.wait_ge(s_xsp, 16)
            for s, (r0, r1) in enumerate(((0, NPOW1), (NPOW1, NPOW))):
                evict_misc(M_AP + s, APT[:, r0:r1, :], bank(M_AP + s)[:, 0:(r1 - r0) * NJ].rearrange("p (r j) -> p r j", j=NJ))
                if s == 0:
                    hi(3, 1, N_U + 2)
                    store_u(0)
                    store_u(1)
                    hi(4, 0, N_U + 3)

            store_u(2)
            hi(5, 1, N_P2)
            store_u(3)
            W1f = W1[:, :, :, :].rearrange("p c j n -> p (c j) n")
            for s in range(8):
                evict_misc(M_W1 + s, W1f[:, 4 * s:4 * s + 4, :], bank(M_W1 + s)[:, :].rearrange("p (j n) -> p j n", n=P))
            def evict_y(q, steps=range(4)):
                for s in steps:
                    g0 = (0, 1, 4, 5)[s]
                    k = M_S5(q, 4 + s)
                    if 4 * q + s >= 2:
                        act.wait_ge(s_ys[s % 2], 16 * ((4 * q + s) // 2))
                    evict_misc(k, YST[:, s % 2, :, :], bank(k)[:, 0:2 * UC].rearrange("p (g c) -> p g c", c=UC))
                    act.wait_ge(s_mf, k + 1)
                    act.dma_start(yscr[8 * q + g0:8 * q + g0 + 3:2].rearrange("g p c -> p g c"),
                                  YST[:, s % 2, :, :]).then_inc(s_ys[s % 2], 16)

            def va_hi(q):
                act.wait_ge(s_va, q + 1)
                if q == 0:
                    act.wait_ge(s_to, 32 * CH)
                copy(tile(VAH, q), TA[:, :]).then_inc(s_vh, 1)

            for q in range(CT):
                n = N_P2 + 3 * q
                g = G_P2 + 3 * q
                if q:
                    hi(g + 1, (g + 1) % 2, n)
                hi(g + 2, (g + 2) % 2, n + 1)
                if q:
                    evict_y(q - 1)
                    va_hi(q - 1)
                    act.wait_ge(s_scan, q)
                for j in range(4):
                    k = M_S5(q, j)
                    evict_misc(k, S[:, :, j, NB + 1:SW], bank(k)[:, 0:2 * UC].rearrange("p (c n) -> p c n", n=UC))
                if q == 0:
                    for s in range(4):
                        evict_misc(M_G + s, GB[:, 4 * s:4 * s + 4, :],
                                   bank(M_G + s)[0:2 * HG, :].rearrange("p (j n) -> p j n", n=P))
                act.wait_ge(s_ci, q + 1)
                copy(TA[:, :], TBf[:, :], ACT.Identity, scale=KV[:, K_CAW + 2 * CT + q:K_CAW + 2 * CT + q + 1],
                     bias=KV[:, K_CAB + q:K_CAB + q + 1]).then_inc(s_cb, 1)
                hi(g + 3, (g + 3) % 2, n + 2)
            hi(G_P3 + 1, 1, N_P3, CT)
            evict_y(CT - 1, (0, 1))
            va_hi(CT - 1)
            evict_y(CT - 1, (2, 3))
            def tiles_p3(i):
                for j in range(2):
                    n, g = N_P3 + 2 * j, G_P3 + 2 * j
                    m = i * 2 + j
                    hi(g + 2, 0, i * 4 + (n + 1), DT, i, 4)
                    act.wait_ge(s_ev, i * 4 + (n + 1))
                    copy(tile(TF, m), tile(TF, m), ACT.Sigmoid).then_inc(s_sa, 1)
                    if j == 0 or not isinstance(i, int):
                        hi(g + 3, 1, i * 4 + (n + 2), CT, i, 4)
                act.wait_ge(s_y, i + 1)
                copy(TC[:, 0:SEQ].rearrange("p (c i) -> p i c", i=CH), TA[:, 0:SEQ].rearrange("p (i c) -> p i c", i=CH),
                     ACT.Gelu_apprx_tanh).then_inc(s_yg, 1)
                copy(TC[:, SEQ:T], TA[:, SEQ:T], ACT.Gelu_apprx_tanh).then_inc(s_yg, 1)
                act.wait_ge(s_yg, i * 3 + 2)
                copy(tile(YGH, i), TC[:, :]).then_inc(s_yg, 1)

            with act.Fori(0, 3) as i:
                tiles_p3(i)
            tiles_p3(3)
            with act.Fori(0, 4) as i:
                for j in range(2):
                    n, g = N_P4 + 3 * j, G_P4 + 2 * j
                    hi(g + 1, 1, i * 6 + n, DT, i, 4)
                    hi(g + 2, 0, i * 6 + (n + 1), DT, i, 4)
                    act.wait_ge(s_ev, i * 6 + (n + 1))
                    copy(TA[:, :], TA[:, :], ACT.Sigmoid).then_inc(s_sg, 1)
                    act.wait_ge(s_po, i * 6 + (n + 2))
                    act.wait_ge(s_tf, i * 2 + (j + 1))
                    copy(v3(TBf[:, :]), set3(n + 1), ACT.Sigmoid).then_inc(s_ev, 1)
                    act.wait_ge(s_tf, i * 2 + (j + 2))
                    copy(tile(TH, i * 2 + j), TA[:, :]).then_inc(s_th, 1)
            with act.Fori(0, 4) as i:
                for j in range(2):
                    m = i * 2 + j
                    hi(G_P5 + j + 1, (j + 1) % 2, i * 2 + (N_P5 + j), DT, i, 2)
                    act.wait_ge(s_ev, i * 2 + (N_P5 + j + 1))
                    split_hi(None, tile(XT, m), m, KV[:, bass.ds(m + K_FFN, 1)], TC, i * 2 + (DT + j))
            hi(G_P6, G_P6 % 2, N_A0)
            rms(2, N_A0)

            def hi_down(p, n_before):
                act.wait_ge(s_dst, p * 16 + 16)
                act.wait_ge(s_po, n_before)
                copy(DHW[:, :], DST[:, :, :].rearrange("p f n -> p (f n)")).then_inc(s_dh, 1)

            def conv_tap(f):
                act.wait_ge(s_fi, f + 1)
                copy(TBf[:, :], TA[:, :], ACT.Identity, scale=KV[:, bass.ds(f + (K_FW + 2 * FT), 1)],
                     bias=KV[:, bass.ds(f + K_FB, 1)]).then_inc(s_fb, 1)

            def gelu(f):
                act.wait_ge(s_fc, f + 1)
                copy(TBf[:, :], TBf[:, :], ACT.Gelu_apprx_tanh).then_inc(s_ge, 1)

            def split_g(f, j):
                act.wait_ge(s_g, f + 1)
                copy(tile(GH, j), TC[:, :]).then_inc(s_gh, 1)

            hi(G_P6 + 1, 0, N_P6)
            conv_tap(0)
            gelu(0)
            with act.Fori(0, FP - 1) as p:
                nb = p * 12 + N_P6
                split_g(p * 2, 0)
                hi(G_P6 + 2, 1, nb + 1, DT, p, 4)
                hi_down(p, nb)
                conv_tap(p * 2 + 1)
                hi(G_P6 + 3, 0, nb + 2, DT, p, 4)
                gelu(p * 2 + 1)
                split_g(p * 2 + 1, 1)
                hi(G_P6 + 4, 1, nb + 3, DT, p, 4)
                hi(G_P6 + 5, 0, nb + 4, DT, p, 4)
                conv_tap(p * 2 + 2)
                gelu(p * 2 + 2)

            def p_hi(k):
                act.wait_ge(s_md, M_PT + k + 1)
                if k < 4:
                    kk, h = divmod(k, 2)
                    copy(PH[:, kk * T + 512 * h:kk * T + 512 * (h + 1)], bank(M_PT + k)[:, :]).then_inc(s_ph, 1)
                else:
                    copy(PH[:, :].rearrange("p (k t) -> p k t", t=T)[:, :, SEQ:T],
                         bank(M_PT + k)[:, 0:2 * NB].rearrange("p (k t) -> p k t", t=NB)).then_inc(s_ph, 1)

            split_g(FT - 2, 0)
            hi(G_END + 2, 1, N_END + 1)
            hi_down(FP - 1, N_END)
            p_hi(0)
            p_hi(1)
            p_hi(2)
            p_hi(3)
            p_hi(4)
            hi(G_P7, 0, N_END + 2)
            conv_tap(FT - 1)
            gelu(FT - 1)
            act.wait_ge(s_dst, FP * 16 + 16)
            act.wait_ge(s_md, M_PT + 5)
            copy(PHW[:, :], DST[:, :, :].rearrange("p f n -> p (f n)")).then_inc(s_dh, 1)
            split_g(FT - 1, 1)
            hi(G_P7 + 1, 1, N_DOWN_END)
            for m in range(DT):
                act.wait_ge(s_ev, N_DOWN_END + m + 1)
                split_hi(None, tile(XT, m), m, KV[:, K_PLE + m:K_PLE + m + 1], TC, 2 * DT + m)
            def states_out(k):
                if k < 7:
                    w = 512 if k < 6 else 256
                    evict_misc(M_OUT + k, OST[:, 512 * k:512 * k + w], bank(M_OUT + k)[0:NB + 2, 0:w])
                else:
                    evict_misc(M_OUT + k, SST[:, 512 * (k - 7):512 * (k - 6)], bank(M_OUT + k)[0:NB + 1, :])

            def ple_gate(m, n):
                act.wait_ge(s_ev, n + 1)
                copy(TA[:, :], TA[:, :], ACT.Sigmoid).then_inc(s_sp, 1)

            hi(G_P7L, 0, N_PW0)
            for k in range(4):
                states_out(k)
            rms(3, N_P7)
            for k in range(4, 15):
                states_out(k)
            ple_gate(0, N_P7)
            ple_gate(1, N_G1)
            for m in range(2, DT):
                n = N_P7L + 2 * (m - 2)
                if m + 1 < DT:
                    hi(G_P7 + m + 1, (m + 1) % 2, n)
                ple_gate(m, n)
            for t in range(DT + 1):
                w = P if t < DT else NB
                act.wait_ge(s_po, N_P8 + t + 1)
                if t >= 4:
                    act.wait_ge(s_ev, N_P8 + t - 3)
                ssq, root = (TSC[0:w, k + t % 4:k + t % 4 + 1] for k in (0, 4))
                own.link(copy(TC[0:w, 0:D], out_banks(t).rearrange("p a b -> p (a b)"), ACT.Square, accum_out=ssq))
                copy(root, ssq, ACT.Sqrt, bias=EP[0:w, :], scale=1.0 / D).then_inc(s_ss, 1)

        @block.vector
        def _(dve):
            own = _Steps(dve, s_dv)
            link = own.link
            tt, ts_, stt = nc.vector.tensor_tensor, nc.vector.tensor_scalar, nc.vector.scalar_tensor_tensor
            MAGIC = 12582912.0

            def exp_small(o, x, e1, e2, ei):
                link(ts_(x, x, -87.0, 88.0, ALU.max, ALU.min))
                link(ts_(e1, x, 1.0 / math.log(2.0), MAGIC, ALU.mult, ALU.add))
                link(ts_(e1, e1, MAGIC, None, ALU.subtract))
                link(stt(x, e1, -0.693359375, x, ALU.mult, ALU.add))
                link(stt(x, e1, 2.12194440e-4, x, ALU.mult, ALU.add))
                link(ts_(e2, x, 1.0 / 5040, None, ALU.mult))
                for d in (720, 120, 24, 6, 2, 1):
                    link(stt(e2, e2, 1.0 / d, x, ALU.add, ALU.mult))
                link(ts_(e1, e1, 127.0, 8388608.0, ALU.add, ALU.mult))
                link(nc.vector.tensor_copy(ei, e1))
                link(stt(o, e2, 1.0, ei.bitcast(F32), ALU.add, ALU.mult))

            dve.wait_ge(s_lam, 48)
            exp_small(DTM[:, :], LDT[:, :], E1[:, 0:2], E2[:, 0:2], EI[:, 0:2])
            dtb = DTM[:, :].unsqueeze(2).to_broadcast([NJ, 2, NS])
            lre, lim = LAM[:, 0, :], LAM[:, 1, :]
            half = "j (two p) -> j two p"
            two = lambda v: v.rearrange(half, two=2)
            link(tt(two(E3[:, :]), two(lim), dtb, ALU.mult))
            link(ts_(KF[:, 0, :], E3[:, :], 1.0 / (2 * math.pi), 0.25, ALU.mult, ALU.add))
            link(ts_(KF[:, 1, :], E3[:, :], 1.0 / (2 * math.pi), None, ALU.mult))
            link(ts_(KF[:, :, :], KF[:, :, :], MAGIC, MAGIC, ALU.add, ALU.subtract))
            for c in range(2):
                dst = CS[:, c, :]
                src = E3[:, :]
                for part in (6.28125, 1.93500518798828125e-3, 3.0199159819e-7):
                    link(stt(dst, KF[:, c, :], -part, src, ALU.mult, ALU.add))
                    src = dst
            link(ts_(KF[:, 0, :], CS[:, 0, :], math.pi / 2, None, ALU.add))
            link(nc.vector.tensor_copy(KF[:, 1, :], CS[:, 1, :]))
            ts_(KF[:, :, :], KF[:, :, :], -3.1415925, 3.1415925, ALU.max, ALU.min).then_inc(s_ang, 1)
            link(tt(two(E3[:, :]), two(lre), dtb, ALU.mult))
            exp_small(Q1[:, 0, :], E3[:, :], E1[:, :], E2[:, :], EI[:, :])

            def split_lo(count, xt, m, gain):
                dve.wait_ge(s_xh, count + 1)
                stt(tile(XL, m), xt, gain, tile(XH, m).bitcast(F32), ALU.mult, ALU.subtract).then_inc(s_xl, 1)

            def norm1(m):
                if m == 0:
                    dve.wait_ge(s_md, M_AP)
                split_lo(m, tile(XT, m), m, KV[:, K_MIX + m:K_MIX + m + 1])

            dve.wait_ge(s_sin, 1)
            mag = Q1[:, 0:1, :].to_broadcast([NJ, 2, P])
            link(nc.vector.memset(AP[:, A_POW(0, 0), :], 1.0))
            link(nc.vector.memset(AP[:, A_POW(0, 1), :], 0.0))
            link(tt(AP[:, A_POW(1, 0):A_POW(1, 1) + 1, :], CS[:, :, :], mag, ALU.mult))
            are, aim = AP[:, A_POW(1, 0), :], AP[:, A_POW(1, 1), :]
            link(tt(E1[:, :], lre, lre, ALU.mult))
            link(tt(E2[:, :], lim, lim, ALU.mult))
            link(tt(E1[:, :], E1[:, :], E2[:, :], ALU.add))
            link(nc.vector.reciprocal(E3[:, :], E1[:, :]))
            norm1(0)
            link(ts_(E1[:, :], are, -1.0, None, ALU.add))
            link(tt(E2[:, :], E1[:, :], lre, ALU.mult))
            link(tt(Q1[:, 0, :], aim, lim, ALU.mult))
            link(tt(E2[:, :], E2[:, :], Q1[:, 0, :], ALU.add))
            link(tt(AP[:, COEF, :], E2[:, :], E3[:, :], ALU.mult))
            norm1(1)
            link(tt(E2[:, :], E1[:, :], lim, ALU.mult))
            link(tt(Q1[:, 0, :], aim, lre, ALU.mult))
            link(tt(E2[:, :], Q1[:, 0, :], E2[:, :], ALU.subtract))
            link(tt(AP[:, COEF + 1, :], E2[:, :], E3[:, :], ALU.mult))
            norm1(2)

            def cmul(dst, src, by, n):
                rows = lambda r, c: AP[:, r:r + 2 * n, :].rearrange("j (n c) p -> j n c p", c=2)[:, :, c, :]
                b = [AP[:, by + c:by + c + 1, :].to_broadcast([NJ, n, P]) for c in range(2)]
                q1, q2 = Q1[:, 0:n, :], Q2[:, 0:n, :]
                tt(q1, rows(src, 0), b[0], ALU.mult).then_inc(s_dv, 1)
                link2(tt(q2, rows(src, 1), b[1], ALU.mult))
                link(tt(rows(dst, 0), q1, q2, ALU.subtract))
                tt(q1, rows(src, 0), b[1], ALU.mult).then_inc(s_dv, 1)
                link2(tt(q2, rows(src, 1), b[0], ALU.mult))
                link(tt(rows(dst, 1), q1, q2, ALU.add))

            def link2(ins):
                own.n += 1
                link(ins)

            r = A_POW
            cmul(r(2, 0), r(1, 0), r(1, 0), 1)
            norm1(3)
            cmul(r(3, 0), r(1, 0), r(2, 0), 2)
            norm1(4)
            cmul(r(5, 0), r(1, 0), r(4, 0), 4)
            norm1(5)
            norm1(6)
            norm1(7)
            nc.vector.tensor_copy(Q1[:, 0, 0:1], AP[:, r(8, 0), 0:1]).then_inc(s_pow, 1)

            def recip(count):
                dve.wait_ge(s_rt, count)
                link(nc.vector.reciprocal(RS[:, :], RS[:, :]))

            def scaled(n, o, wait_n=None):
                dve.wait_ge(s_po, (n if wait_n is None else wait_n) + 1)
                tt(v3(o), set3(n), v3(RS[:, :]), ALU.mult).then_inc(s_ev, 1)

            def evict_u(q):
                n = N_U + q
                dve.wait_ge(s_po, n + 1)
                if q >= 2:
                    dve.wait_ge(s_us[q - 2], 32)
                if q == 0:
                    dve.wait_ge(s_acc, DT)
                tt(US[:, q, :], PS[:, 3 * (n % 2) + 2, TN - NB:TN], RS[:, SEQ:T], ALU.mult)
                o = (TA, TBf)[q % 2][:, :].rearrange("p (i c d) -> p c d i", i=CH, c=NCH)
                i0 = set3(n).rearrange("p c (d i) -> p c d i", i=CH)
                i1 = v3(RS[:, :]).rearrange("p c (d i) -> p c d i", i=CH)
                last = None
                for c in range(NCH):
                    last = tt(o[:, c], i0[:, c], i1[:, c], ALU.mult)
                last.then_inc(s_ev, 1)

            recip(1)
            evict_u(0)
            evict_u(1)
            dve.wait_ge(s_pow, 1)
            link(nc.vector.tensor_copy(AP[:, A_CHUNK(1, 0):A_CHUNK(1, 0) + 2, :], AP[:, r(8, 0):r(8, 0) + 2, :]))
            r = A_CHUNK
            cmul(r(2, 0), r(1, 0), r(1, 0), 1)
            cmul(r(3, 0), r(1, 0), r(2, 0), 2)
            cmul(r(5, 0), r(1, 0), r(4, 0), 4)
            for k in range(3):
                cmul(A_BLOCK(k + 1, 0), A_BLOCK(k, 0), A_BLOCK(k, 0), 1)
            nc.vector.tensor_copy(Q1[:, 0, 0:1], AP[:, NPOW - 1, 0:1]).then_inc(s_pow, 1)
            evict_u(2)
            dve.wait_ge(s_mf, M_AP + 1)
            dve.wait_ge(s_bn, 32)
            cf = [APT[:, COEF + c, :].unsqueeze(2).to_broadcast([P, NJ, HG]) for c in range(2)]
            mt = MT[:, 0:NJ * HG].rearrange("p (j h) -> p j h", h=HG)
            link(tt(BB[:, 0], BN[:, 0], cf[0], ALU.mult))
            link(tt(mt, BN[:, 1], cf[1], ALU.mult))
            link(tt(BB[:, 0], BB[:, 0], mt, ALU.subtract))
            link(tt(BB[:, 1], BN[:, 1], cf[0], ALU.mult))
            link(tt(mt, BN[:, 0], cf[1], ALU.mult))
            link(tt(BB[:, 1], BB[:, 1], mt, ALU.add))

            power_rows(nc.vector, link, W1T, BB, range(NJ), CH, MT, 1,
                       (lambda: None, lambda: evict_u(3))).then_inc(s_w1t, 1)
            power_rows(nc.vector, link, W2, CTT, range(NJ // 2, NJ), CH + 1, MT, -1).then_inc(s_w2, 1)
            dve.wait_ge(s_md, M_V)
            link(nc.vector.memset(BBP[:, :, :, :], 0.0))
            for two in range(2):
                rows = slice(two * NS, two * NS + NS)
                last = nc.vector.tensor_copy(BBP[rows, :, :, two * HG:(two + 1) * HG], BB[rows, :, :, :])
            last.then_inc(s_bbp, 1)

            def scan(q):
                dve.wait_ge(s_mf, M_S5(q, 3) + 1)
                js = slice(4 * q, 4 * q + 4)
                blk = S[:, :, :, NB + 1:NB + 1 + NC].rearrange("p c j (b i) -> p c j b i", i=CH)

                def cmac(dst, src, pw, n, shp):
                    view = (lambda x: x.rearrange("p (a b) -> p a b", a=shp[0])) if len(shp) == 2 else \
                        (lambda x: x.rearrange("p (a b c) -> p a b c", a=shp[0], b=shp[1]))
                    if 2 * n <= 480:
                        t1, t2, t3, t4 = (view(x) for x in (ST1[:, 0:n], ST1[:, n:2 * n], ST2[:, 0:n], ST2[:, n:2 * n]))
                        tt(t1, src[0], pw[0], ALU.mult)
                        tt(t2, src[1], pw[1], ALU.mult)
                        tt(t3, src[1], pw[0], ALU.mult)
                        link(tt(t4, src[0], pw[1], ALU.mult))
                        tt(dst[0], dst[0], t1, ALU.add)
                        link(tt(dst[1], dst[1], t3, ALU.add))
                        tt(dst[0], dst[0], t2, ALU.subtract)
                        link(tt(dst[1], dst[1], t4, ALU.add))
                    else:
                        t1, t2 = view(ST1[:, 0:n]), view(ST2[:, 0:n])
                        tt(t1, src[0], pw[0], ALU.mult)
                        link(tt(t2, src[1], pw[1], ALU.mult))
                        link(tt(dst[0], dst[0], t1, ALU.add))
                        link(tt(dst[0], dst[0], t2, ALU.subtract))
                        tt(t1, src[1], pw[0], ALU.mult)
                        link(tt(t2, src[0], pw[1], ALU.mult))
                        link(tt(dst[1], dst[1], t1, ALU.add))
                        link(tt(dst[1], dst[1], t2, ALU.add))

                def cmac2(dst, src, row, shp):
                    n = 2 * shp[0] * shp[1]
                    t1, t2 = (x[:, 0:n].rearrange("p (c a b) -> p c a b", c=2, a=shp[0]) for x in (ST1, ST2))
                    w = [APT[:, row + c:row + c + 1, js].unsqueeze(3).to_broadcast([P, 2, *shp]) for c in range(2)]
                    tt(t1, src, w[0], ALU.mult)
                    link(tt(t2, src, w[1], ALU.mult))
                    link(tt(dst, dst, t1, ALU.add))
                    tt(dst[:, 0], dst[:, 0], t2[:, 1], ALU.subtract)
                    link(tt(dst[:, 1], dst[:, 1], t2[:, 0], ALU.add))

                def pws(row, w):
                    return [APT[:, row + c, js].unsqueeze(2).to_broadcast([P, 4, w]) for c in range(2)]

                for i in range(1, CH):
                    cmac2(blk[:, :, :, :, i], blk[:, :, :, :, i - 1], A_POW(CH, 0), [4, NBLK])
                for lv in range(4):
                    d = 1 << lv
                    w = NBLK - d
                    cmac2(blk[:, :, :, d:, CH - 1], blk[:, :, :, 0:w, CH - 1], A_BLOCK(lv, 0), [4, w])
                shp = [P, 4, NBLK - 1, CH - 1]
                pw = [APT[:, A_CHUNK(1, 0):A_CHUNK(CH, 0), js].rearrange("p (i c) j -> p c j i", c=2)[:, c]
                      .unsqueeze(2).to_broadcast(shp) for c in range(2)]
                cmac([blk[:, c, :, 1:, 0:CH - 1] for c in range(2)],
                     [blk[:, c, :, 0:NBLK - 1, CH - 1].unsqueeze(3).to_broadcast(shp) for c in range(2)],
                     pw, 4 * (NBLK - 1) * (CH - 1), shp[1:])
                s0 = [S0[:, c, js, :] for c in range(2)]
                cmac([S[:, c, :, SW - NB:SW] for c in range(2)], s0, pws(A_POW(1, 0), NB), 4 * NB, [4, NB])
                for c in range(2):
                    nc.vector.tensor_copy(FS[:, c, js, :], S[:, c, :, SW - NB - 1:SW])
                nc.vector.tensor_copy(S[:, 0, :, 0:NB], s0[0])
                nc.vector.tensor_copy(S[:, 1, :, 0:NB], s0[1]).then_inc(s_scan, 1)

            def conv(o, x, t, kw, tiles, col):
                def w(k):
                    c = col + kw + k * tiles
                    return KV[:, c:c + 1] if isinstance(c, int) else KV[:, bass.ds(c, 1)]
                st = CB[:, t, :] if isinstance(t, int) else CB[:, bass.ds(t, 1), :].rearrange("p t n -> p (t n)")
                st = st.rearrange("p (b k) -> p k b", k=2)
                stt(o[:, SEQ:T], st[:, 1], w(1), o[:, SEQ:T], ALU.mult, ALU.add)
                link(stt(o[:, 1:SEQ], x[:, 0:SEQ - 1], w(1), o[:, 1:SEQ], ALU.mult, ALU.add))
                stt(o[:, SEQ:T], st[:, 0], w(0), o[:, SEQ:T], ALU.mult, ALU.add)
                return stt(o[:, 2:SEQ], x[:, 0:SEQ - 2], w(0), o[:, 2:SEQ], ALU.mult, ALU.add)

            dve.wait_ge(s_us[2], 32)
            dve.wait_ge(s_us[3], 32)
            for q in range(CT):
                n = N_P2 + 3 * q
                if q:
                    dve.wait_ge(s_vl, q)
                scaled(n, TA[:, :])
                scaled(n + 1, TBf[:, :])
                dve.wait_ge(s_ev, n + 2)
                tt(TBf[:, :], TBf[:, :], TA[:, :], ALU.mult).then_inc(s_ci, 1)
                dve.wait_ge(s_ci, q + 1)
                nc.vector.tensor_copy(LAST[:, q, :], TBf[:, SEQ - 2:T])
                scan(q)
                dve.wait_ge(s_scan, q + 1)
                scaled(n + 2, TC[:, :])
                dve.wait_ge(s_cb, q + 1)
                link(conv(TA, TBf, q, q, CT, K_CAW))
                dve.wait_ge(s_ev, n + 3)
                tt(TA[:, :], TA[:, :], TC[:, :], ALU.mult).then_inc(s_va, 1)
                dve.wait_ge(s_va, q + 1)
                dve.wait_ge(s_vh, q + 1)
                tt(tile(VAL, q), TA[:, :], tile(VAH, q).bitcast(F32), ALU.subtract).then_inc(s_vl, 1)
            dve.wait_ge(s_vl, CT)
            nc.vector.tensor_copy(SSC[:, 0:1], EP[:, :]).then_inc(s_yl2, 1)
            with dve.Fori(0, 4) as i:
                for j in range(2):
                    n = N_P3 + 2 * j
                    scaled(n, tile(TF, i * 2 + j), i * 4 + n)
                    dve.wait_ge(s_sa, i * 2 + (j + 1))
                    dve.wait_ge(s_po, i * 4 + (n + 2))
                    tt(v3(tile(TF, i * 2 + j)), set3(n + 1), v3(tile(TF, i * 2 + j)), ALU.mult).then_inc(s_ev, 1)
                    if j == 0:
                        dve.wait_ge(s_yl, i * 272 + 272)
                        tt_y = stt(TA[:, :], TBf[:, :], KV[:, bass.ds(i + K_DSK, 1)], TA[:, :], ALU.mult, ALU.add)
                        tt_y.then_inc(s_y, 1)
                dve.wait_ge(s_yg, i * 3 + 3)
                tt(tile(YGL, i), TC[:, :], tile(YGH, i).bitcast(F32), ALU.subtract).then_inc(s_yl2, 1)
            dve.wait_ge(s_yl2, CT + 1)
            nc.vector.tensor_copy(SSC[:, 0:1], EP[:, :]).then_inc(s_tf, 1)
            nc.vector.tensor_copy(SSC[:, 1:2], EP[:, :]).then_inc(s_tl, 1)
            with dve.Fori(0, 4) as i:
                own.enter(i, 2)
                for j in range(2):
                    n = N_P4 + 3 * j
                    m = i * 2 + j
                    dve.wait_ge(s_tl, i * 2 + (j + 1))
                    scaled(n, TA[:, :], i * 6 + n)
                    dve.wait_ge(s_ev, i * 6 + (n + 2))
                    dve.wait_ge(s_po, i * 6 + (n + 3))
                    tt(v3(TBf[:, :]), set3(n + 2), v3(TBf[:, :]), ALU.mult).then_inc(s_ev, 1)
                    dve.wait_ge(s_ev, i * 6 + (n + 3))
                    dve.wait_ge(s_sg, i * 2 + (j + 1))
                    link(tt(TA[:, :], TA[:, :], TBf[:, :], ALU.mult))
                    tt(TA[:, :], TA[:, :], tile(TF, m), ALU.add).then_inc(s_tf, 1)
                    dve.wait_ge(s_th, i * 2 + (j + 1))
                    tt(tile(TL, m), TA[:, :], tile(TH, m).bitcast(F32), ALU.subtract).then_inc(s_tl, 1)
                own.leave(4)
            with dve.Fori(0, 4) as i:
                for j in range(2):
                    n = N_P5 + j
                    m = i * 2 + j
                    dve.wait_ge(s_xr[j], i * 16 + 16)
                    dve.wait_ge(s_po, i * 2 + (n + 1))
                    tt(v3(tile(XT, m)), set3(n), v3((TA, TBf)[j][:, :]), ALU.add).then_inc(s_ev, 1)
                    split_lo(i * 2 + (DT + j), tile(XT, m), m, KV[:, bass.ds(m + K_FFN, 1)])
            recip(2)

            def up_a(f, n, wait_n):
                dve.wait_ge(s_po, wait_n + 1)
                if not isinstance(f, int) or f:
                    dve.wait_ge(s_fc, f)
                tt(v3(TA[:, :]), set3(n), v3(RS[:, :]), ALU.mult).then_inc(s_ev, 1)
                dve.wait_ge(s_ev, wait_n + 1)
                nc.vector.tensor_copy(LAST[:, bass.ds(f + CT, 1), :].rearrange("p t n -> p (t n)"),
                                      TA[:, SEQ - 2:T]).then_inc(s_fi, 1)

            def conv_a(f):
                dve.wait_ge(s_fb, f + 1)
                conv(TBf, TA, f + CT, f, FT, K_FW).then_inc(s_fc, 1)

            def up_b(f, j, n, wait_n):
                dve.wait_ge(s_gl, f + 1)
                scaled(n, TC[:, :], wait_n)
                dve.wait_ge(s_ev, wait_n + 1)
                dve.wait_ge(s_ge, f + 1)
                tt(TC[:, :], TC[:, :], TBf[:, :], ALU.mult).then_inc(s_g, 1)
                dve.wait_ge(s_gh, f + 1)
                tt(tile(GL, j), TC[:, :], tile(GH, j).bitcast(F32), ALU.subtract).then_inc(s_gl, 1)

            def down(n, wait_n, ms):
                for m in ms:
                    dve.wait_ge(s_po, wait_n + (m + 1))
                    xm = v3(tile(XT, m))
                    tt(xm, set3(n + m), xm, ALU.add).then_inc(s_ev, 1)

            dve.wait_ge(s_acc, 2 * DT)
            nc.vector.tensor_copy(SSC[:, 2:3], EP[:, :]).then_inc(s_gl, 1)
            up_a(0, N_A0, N_A0)
            conv_a(0)
            with dve.Fori(0, FP - 1) as p:
                own.enter(p, 2)
                nb = p * 12 + N_P6
                up_b(p * 2, 0, N_P6, nb)
                up_a(p * 2 + 1, N_P6 + 1, nb + 1)
                conv_a(p * 2 + 1)
                up_b(p * 2 + 1, 1, N_P6 + 2, nb + 2)
                up_a(p * 2 + 2, N_P6 + 3, nb + 3)
                down(N_P6 + 4, nb + 4, (0,))
                conv_a(p * 2 + 2)
                down(N_P6 + 4, nb + 4, range(1, DT))
                own.leave(FP - 1)

            def p_lo(k):
                dve.wait_ge(s_ph, k + 1)
                if k < 4:
                    kk, h = divmod(k, 2)
                    w = slice(kk * T + 512 * h, kk * T + 512 * (h + 1))
                    tt(PL[:, w], bank(M_PT + k)[:, :], PH[:, w].bitcast(F32), ALU.subtract).then_inc(s_mf, 1)
                else:
                    w3 = lambda t: t.rearrange("p (k t) -> p k t", t=T)[:, :, SEQ:T]
                    tt(w3(PL[:, :]), bank(M_PT + k)[:, 0:2 * NB].rearrange("p (k t) -> p k t", t=NB),
                       w3(PH[:, :].bitcast(F32)), ALU.subtract).then_inc(s_mf, 1)

            up_b(FT - 2, 0, N_END, N_END)
            p_lo(0)
            p_lo(1)
            up_a(FT - 1, N_END + 1, N_END + 1)
            p_lo(2)
            p_lo(3)
            p_lo(4)
            conv_a(FT - 1)
            up_b(FT - 1, 1, N_END + 2, N_END + 2)
            for m in range(DT + 1):
                if m < DT:
                    down(N_DOWN_END, N_DOWN_END, (m,))
                if m:
                    split_lo(2 * DT + m - 1, tile(XT, m - 1), m - 1, KV[:, K_PLE + m - 1:K_PLE + m])
            recip(3)

            def ple(m, n_g, n_p, wg, wp):
                dve.wait_ge(s_po, wg + 1)
                tt(v3(TA[:, :]), set3(n_g), v3(RS[:, :]), ALU.mult).then_inc(s_ev, 1)
                dve.wait_ge(s_sp, m + 1)
                dve.wait_ge(s_po, wp + 1)
                if not isinstance(m, int) or m:
                    dve.wait_ge(s_xo, m)
                tt(v3(TBf[:, :]), set3(n_p), v3(TA[:, :]), ALU.mult).then_inc(s_ev, 1)
                dve.wait_ge(s_ev, wp + 1)
                tt(tile(XT, m), tile(XT, m), TBf[:, :], ALU.add).then_inc(s_xo, 1)

            ple(0, N_P7, N_PW0, N_P7, N_PW0)
            ple(1, N_G1, N_G1 + 1, N_G1, N_G1 + 1)
            with dve.Fori(0, 3) as i:
                for j in range(2):
                    n = N_P7L + 2 * j
                    ple(i * 2 + (2 + j), n, n + 1, i * 4 + n, i * 4 + (n + 1))
            dve.wait_ge(s_gf, 16)
            for t in range(DT + 1):
                w = P if t < DT else NB
                root = TSC[0:w, 4 + t % 4:5 + t % 4]
                dve.wait_ge(s_ss, t + 1)
                if t >= NOUT:
                    dve.wait_ge(s_or[t % NOUT], 16 * (t // NOUT))
                link(nc.vector.reciprocal(root, root))
                stt(OUTT[t % NOUT][0:w, :], out_banks(t).rearrange("p a b -> p (a b)"), root, GF[0:w, :],
                    ALU.mult, ALU.mult).then_inc(s_ev, 1)

        @block.tensor
        def _(pe):
            mm, tr = nc.tensor.matmul, nc.tensor.transpose

            def product(n, wait_n, slot_off, ks, xh, xl, ready=None, wh=WH, wl=WL):
                if not isinstance(wait_n, int) or wait_n >= 2:
                    pe.wait_ge(s_ev, wait_n - 1)
                last = None
                for k in range(ks):
                    if ready is not None:
                        ready(k)
                    w = slice(slot_off + k * P, slot_off + (k + 1) * P)
                    for r, (ww, xx) in enumerate(((wh, xh), (wh, xl), (wl, xh))):
                        for c in range(NCH):
                            cols = slice(k * T + c * TN, k * T + (c + 1) * TN)
                            last = mm(PS[:, 3 * (n % 2) + c, 0:TN], ww[:, w], xx[:, cols],
                                      start=(k == 0 and r == 0), stop=(k == ks - 1 and r == 2))
                last.then_inc(s_po, 1)

            def group(g):
                pe.wait_ge(s_wl, g + 1)

            def misc(k):
                if k >= 2:
                    pe.wait_ge(s_mf, k - 1)
                return bank(k)

            def sum_squares(n, tiles):
                if n:
                    pe.wait_ge(s_ev, n)
                pe.wait_ge(s_acc, tiles)
                last = None
                for c in range(NCH):
                    last = mm(PS[:, 3 * ((n + 1) % 2) + c, 0:TN], ONES[:, :], RS[:, c * TN:(c + 1) * TN], start=True, stop=True)
                last.then_inc(s_nm, 1)

            def rms_read(count):
                pe.wait_ge(s_rt, count)

            pe.wait_ge(s_idn, 4)
            for t in range(DT + 1):
                w = P if t < DT else NB
                if t in XSTEPS:
                    pe.wait_ge(s_x[XSTEPS.index(t)], 16)
                for half in range(2):
                    b = misc(M_X + 2 * t + half)
                    for m in range(4):
                        f = slice((4 * half + m) * P, (4 * half + m + 1) * P)
                        src = XN[:, t, f] if t < DT else XS[:, f]
                        last = tr(b[:, m * P:m * P + w], src, IDN[0:w, 0:w])
                    last.then_inc(s_md, 1)
            pe.wait_ge(s_nat, 16 * (8 + 4 + 4))
            b = misc(M_VEC)
            tr(b[:, 0:NK1], VA1[:, :], IDN[0:NK1, 0:NK1])
            tr(b[:, NK1:NK1 + NK2], VA2[:, :], IDN[0:NK2, 0:NK2]).then_inc(s_md, 1)
            b = misc(M_CB)
            for t in range(CT + FT):
                last = tr(b[:, 16 * t:16 * (t + 1)], CBN[:, t * P:(t + 1) * P], IDN[0:16, 0:16])
            last.then_inc(s_md, 1)
            b = misc(M_S0)
            for c in range(2):
                for j in range(NJ):
                    o = (c * NJ + j) * NB
                    last = tr(b[:, o:o + NB], S0N[:, c, j * P:(j + 1) * P], IDN[0:NB, 0:NB])
            last.then_inc(s_md, 1)
            for c in range(2):
                b = misc(M_CT + c)
                for e in range(4):
                    last = tr(b[:, e * P:(e + 1) * P], CN[:, c, e, :, :].rearrange("p two n -> p (two n)"), IDN[:, :])
                last.then_inc(s_md, 1)
            group(0)
            product(N_U, N_U, 0, DT, XH, XL, lambda k: pe.wait_ge(s_xl, k + 1))
            sum_squares(N_U, DT)

            def powers(s):
                r0, r1 = ((0, NPOW1), (NPOW1, NPOW))[s]
                pe.wait_ge(s_pow, s + 1)
                b = misc(M_AP + s)
                for r in range(r0, r1):
                    last = tr(b[:, (r - r0) * NJ:(r - r0 + 1) * NJ], AP[:, r, :], IDN[0:NJ, 0:NJ])
                last.then_inc(s_md, 1)

            powers(0)
            rms_read(1)
            group(1)
            product(N_U + 1, N_U + 1, D, DT, XH, XL)
            group(2)
            product(N_U + 2, N_U + 2, 0, DT, XH, XL)
            group(3)
            product(N_U + 3, N_U + 3, D, DT, XH, XL)
            powers(1)
            for part in range(2):
                group(G_P2 + part)
                product(N_P2 + part, N_P2 + part, part * D, DT, XH, XL)
            pe.wait_ge(s_w1t, 1)
            for s in range(8):
                b = misc(M_W1 + s)
                for j in range(4):
                    c, jj = divmod(4 * s + j, NJ)
                    last = tr(b[:, j * P:(j + 1) * P], W1T[:, c, jj, :], IDN[:, :])
                last.then_inc(s_md, 1)

            def responses():
                pe.wait_ge(s_w2, 2)
                pe.wait_ge(s_bbp, 1)
                for s in range(4):
                    b = misc(M_G + s)
                    for idx in range(4):
                        for c in range(2):
                            last = mm(b[0:2 * HG, idx * P:(idx + 1) * P], BBP[:, c, 4 * s + idx, :],
                                      W2[:, c, 4 * s + idx, 0:P], start=(c == 0), stop=(c == 1))
                    last.then_inc(s_md, 1)

            def inputs_to_states(q):
                pe.wait_ge(s_ul[q], 160)
                for j in range(4):
                    b = misc(M_S5(q, j))
                    for two in range(2):
                        for c in range(2):
                            last = mm(b[two * NS:(two + 1) * NS, c * UC:(c + 1) * UC],
                                      W1[:, c, 4 * q + j, two * NS:(two + 1) * NS], U[:, 2 * j + two, NB:UW],
                                      start=True, stop=True)
                    last.then_inc(s_md, 1)

            def outputs(q):
                pe.wait_ge(s_scan, q + 1)
                for s, gs in enumerate(((0, 2), (1, 3), (4, 6), (5, 7))):
                    b = misc(M_S5(q, 4 + s))
                    for idx, gl in enumerate(gs):
                        rows = slice((gl % 2) * NS, (gl % 2) * NS + NS)
                        o = b[:, idx * UC:(idx + 1) * UC]
                        for c in range(2):
                            mm(o, W2[rows, c, 4 * q + gl // 2, HG:HG + P], S[rows, c, gl // 2, 0:UC],
                               start=(c == 0), stop=False)
                        last = mm(o, TO[:, 8 * q + gl, :], U[:, gl, 0:UC], start=False, stop=True)
                    last.then_inc(s_md, 1)

            for q in range(CT):
                for part in range(3):
                    g, n = G_P2 + 3 * q + part, N_P2 + 3 * q + part
                    if g > G_P2 + 1:
                        group(g)
                        product(n, n, (g % 2) * D, DT, XH, XL)
                    if part == 0 and q:
                        if q == 1:
                            pe.wait_ge(s_to, 32 * CH)
                        outputs(q - 1)
                    if part == 1:
                        inputs_to_states(q)
                        if q == 0:
                            responses()
            def out_a(n, wait_n, g):
                group(g)
                product(n, wait_n, D, CT, VAH, VAL, lambda k: pe.wait_ge(s_vl, k + 1))

            def gate(n, wait_n, g):
                group(g)
                product(n, wait_n, 0, DT, XH, XL)

            gate(N_P3, N_P3, G_P3)
            outputs(CT - 1)
            with pe.Fori(0, 4) as i:
                for j in range(2):
                    n, g = N_P3 + 2 * j, G_P3 + 2 * j
                    out_a(n + 1, i * 4 + (n + 1), i * 4 + (g + 1))
                    gate(n + 2, i * 4 + (n + 2), i * 4 + (g + 2))
            def glu(n, wait_n, g):
                group(g)
                product(n + 1, wait_n + 1, D, CT, YGH, YGL, lambda k: pe.wait_ge(s_yl2, k + 2))
                product(n + 2, wait_n + 2, D + CT * P, CT, YGH, YGL)

            with pe.Fori(0, 3) as i:
                for j in range(2):
                    n, g = N_P4 + 3 * j, G_P4 + 2 * j
                    glu(n, i * 6 + n, i * 4 + (g + 1))
                    gate(n + 3, i * 6 + (n + 3), i * 4 + (g + 2))
            n, g = N_P4 + 18, G_P4 + 12
            glu(n, n, g + 1)
            gate(n + 3, n + 3, g + 2)
            glu(n + 3, n + 3, g + 3)
            with pe.Fori(0, 4) as i:
                for j in range(2):
                    group(i * 2 + (G_P5 + j))
                    product(N_P5 + j, i * 2 + (N_P5 + j), j * D, DT, TH, TL, lambda k: pe.wait_ge(s_tl, k + 2))
            group(G_A0)
            product(N_A0, N_A0, 0, DT, XH, XL, lambda k: pe.wait_ge(s_xl, DT + k + 1))
            sum_squares(N_A0, 2 * DT)
            rms_read(2)

            def down(n, wait_n, p):
                pe.wait_ge(s_dl, p + 1)
                for m in range(DT):
                    down_out(n + m, wait_n + m, m, GH, GL, ready=None if m else lambda k: pe.wait_ge(s_gl, p * 2 + (2 + k)))

            def down_out(n, wait_n, m, xh, xl, wh=DHW, wl=DLW, ready=None):
                pe.wait_ge(s_ev, wait_n - 1)
                last = None
                for k in range(2):
                    if ready is not None:
                        ready(k)
                    w = slice(k * D + m * P, k * D + (m + 1) * P)
                    for r, (ww, xx) in enumerate(((wh, xh), (wh, xl), (wl, xh))):
                        for c in range(NCH):
                            last = mm(PS[:, 3 * (n % 2) + c, 0:TN], ww[:, w], xx[:, k * T + c * TN:k * T + (c + 1) * TN],
                                      start=(k == 0 and r == 0), stop=(k == 1 and r == 2))
                last.then_inc(s_po, 1)

            with pe.Fori(0, FP - 1) as p:
                for j in range(4):
                    group(p * 4 + (G_P6 + j))
                    product(N_P6 + j, p * 12 + (N_P6 + j), ((G_P6 + j) % 2) * D, DT, XH, XL)
                down(N_P6 + 4, p * 12 + (N_P6 + 4), p)
            def transpose_p(k):
                b = misc(M_PT + k)
                if k < 4:
                    kk, h = divmod(k, 2)
                    for t in range(4):
                        last = tr(b[:, t * P:(t + 1) * P], PST[:, 4 * h + t, kk * P:(kk + 1) * P], IDN[:, :])
                else:
                    for kk in range(PT):
                        last = tr(b[:, kk * NB:(kk + 1) * NB], PSS[:, kk * P:(kk + 1) * P], IDN[0:NB, 0:NB])
                last.then_inc(s_md, 1)

            for j in range(3):
                group(G_END + j)
                product(N_END + j, N_END + j, ((G_END + j) % 2) * D, DT, XH, XL)
                if j == 0:
                    pe.wait_ge(s_p, 32)
                for k in ((0, 1), (2, 3, 4), ())[j]:
                    transpose_p(k)
            down(N_DOWN_END, N_DOWN_END, FP - 1)
            group(G_P7)
            product(N_P7, N_P7, 0, DT, XH, XL, lambda k: pe.wait_ge(s_xl, 2 * DT + k + 1))

            def states_out(k):
                b = misc(M_OUT + k)
                if k < 7:
                    for t in range(4 * k, min(4 * k + 4, CT + FT)):
                        last = tr(b[0:NB + 2, (t - 4 * k) * P:(t - 4 * k + 1) * P], LAST[:, t, :], IDN[:, :])
                else:
                    for r in range(4):
                        c, j = divmod(4 * (k - 7) + r, NJ)
                        last = tr(b[0:NB + 1, r * P:(r + 1) * P], FS[:, c, j, :], IDN[:, :])
                last.then_inc(s_md, 1)

            for k in range(4):
                states_out(k)
            sum_squares(N_P7, 3 * DT)
            for k in range(4, 8):
                states_out(k)
            rms_read(3)
            pe.wait_ge(s_dl, FP + 1)
            down_out(N_PW0, N_PW0, 0, PH, PL, PHW, PLW)
            for k in range(8, 15):
                states_out(k)
            group(G_P7 + 1)
            product(N_G1, N_G1, D, DT, XH, XL)
            down_out(N_G1 + 1, N_G1 + 1, 1, PH, PL, PHW, PLW)
            for m in range(2, DT):
                n = N_P7L + 2 * (m - 2)
                group(G_P7 + m)
                product(n, n, (m % 2) * D, DT, XH, XL)
                down_out(n + 1, n + 1, m, PH, PL, PHW, PLW)
            pe.wait_ge(s_mf, M_OUT + 15)
            for t in range(DT + 1):
                w = P if t < DT else NB
                if t:
                    pe.wait_ge(s_ev, max(N_P8, N_P8 + t - 3))
                for m in range(DT):
                    if t == 0:
                        pe.wait_ge(s_xo, m + 1)
                    last = tr(out_banks(t)[:, m // 4, (m % 4) * P:(m % 4 + 1) * P],
                              XT[:, m * T + t * P:m * T + t * P + w], IDN[:, :])
                last.then_inc(s_po, 1)


_INS = ["x_prompt", "x_sample", "p_prompt", "p_sample", "state_conv_a", "state_ssm_re", "state_ssm_im",
        "state_ffn_conv", "norm_mix", "w_in", "conv_a_w", "conv_a_b", "w_out_a", "log_dt", "lam_re", "lam_im",
        "b_re", "b_im", "c_re", "c_im", "d_skip", "w_glu_a", "w_glu_b", "w_o", "norm_ffn", "w_up",
        "ffn_conv_w", "ffn_conv_b", "w_down", "norm_ple", "w_ple_gate", "w_ple", "norm_final"]
_OUTS = [("y_prompt", (1, SEQ, D)), ("y_sample", (NB, 1, D)),
         ("conv_a_p", (1, 1, 2, CA)), ("ssm_re_p", (1, 1, G, NS)), ("ssm_im_p", (1, 1, G, NS)),
         ("ffn_p", (1, 1, 2, FF)),
         ("conv_a_s", (1, NB, 2, CA)), ("ssm_re_s", (1, NB, G, NS)), ("ssm_im_s", (1, NB, G, NS)),
         ("ffn_s", (1, NB, 2, FF))]


def kernel(**inputs):
    import numpy as np
    import concourse.bacc as bacc
    from concourse.bass_utils import run_bass_kernel_spmd

    nc = bacc.Bacc("TRN2", target_bir_lowering=False, num_devices=1)
    arrays, ins, outs = {}, {}, {}
    for name in _INS:
        arr = np.ascontiguousarray(inputs[name])
        arrays["in_" + name] = arr
        ins[name] = nc.dram_tensor("in_" + name, arr.shape, F32, kind="ExternalInput").ap()
    for name, shape in _OUTS:
        outs[name] = nc.dram_tensor("out_" + name, shape, F32, kind="ExternalOutput").ap()
    decoder_step(nc, ins, outs)
    r = run_bass_kernel_spmd(nc, [arrays], core_ids=[0])
    return tuple(r.results[0]["out_" + name] for name, _ in _OUTS)
```
